# Optimizing a Trainium2 kernel written in Bass

```python
import jax, jax.numpy as jnp
from jax import lax
import numpy as np

D_MODEL = 1024
BATCH = 1
SEQ = 1024
DEPTH = 2
DEC_BATCH = 8
DEC_SEQ = 1
PAST_LEN = 2048
PAGE_SIZE = 128

N_MIXERS = 2
HEAD_DIM = 64
RWKV_HEADS = D_MODEL // HEAD_DIM
DECAY_LORA = 64
AAA_LORA = 64
GATE_LORA = 128
N_MIX_VEC = 6
ATT_HEADS = D_MODEL // HEAD_DIM
KV_HEADS = 4
GROUP = ATT_HEADS // KV_HEADS
WINDOW = 128
ATT_BLOCK = 128
ROPE_DIM = HEAD_DIM // 4
ROPE_THETA = 500000.0
D_FF = 4 * D_MODEL
N_RWKV = (DEPTH + N_MIXERS - 1) // N_MIXERS
N_ATTN = DEPTH // N_MIXERS
NORM_EPS = 1e-6
LNX_EPS = 64e-5
N_ADA = 6

kernel_name = 'rwkv7_swa_sink_hybrid_decode_step'

def rms_norm(x, g):
    xf = x.astype(jnp.float32)
    y = xf * lax.rsqrt(jnp.mean(xf * xf, axis=-1, keepdims=True) + NORM_EPS)
    return (y * g.astype(jnp.float32)).astype(x.dtype)

def ada_params(c, w, b):
    m = jax.nn.silu(c) @ w + b
    m = m.reshape(c.shape[0], N_ADA, 1, D_MODEL)
    return [m[:, i] for i in range(N_ADA)]

def pre_norm(x, g, shift, scale):
    return rms_norm(x, g) * (1 + scale) + shift

def rope_partial(x, pos):
    half = ROPE_DIM // 2
    inv_freq = ROPE_THETA ** (-jnp.arange(half, dtype=jnp.float32) / half)
    ang = pos.astype(jnp.float32)[:, None] * inv_freq[None, :]
    cos = jnp.cos(ang)[:, None, :]
    sin = jnp.sin(ang)[:, None, :]
    xf = x[..., :ROPE_DIM].astype(jnp.float32)
    x1, x2 = xf[..., :half], xf[..., half:]
    rot = jnp.concatenate([x1 * cos - x2 * sin, x2 * cos + x1 * sin], axis=-1).astype(x.dtype)
    return jnp.concatenate([rot, x[..., ROPE_DIM:]], axis=-1)

def sink_softmax(scores, sink):
    s = sink[:, :, None, None]
    m = jnp.maximum(jnp.max(scores, axis=-1, keepdims=True), s)
    p = jnp.exp(scores - m)
    return p / (jnp.sum(p, axis=-1, keepdims=True) + jnp.exp(s - m))

def sq_relu_mlp(h, w_up, w_down):
    return jnp.square(jax.nn.relu(h @ w_up)) @ w_down

def wkv7_step(state, inp):
    r_t, w_t, k_t, v_t, a_t, b_t = inp
    sa = jnp.einsum('bhij,bhj->bhi', state, a_t)
    state = (state * w_t[:, :, None, :] + sa[..., None] * b_t[:, :, None, :]
             + v_t[..., None] * k_t[:, :, None, :])
    y = jnp.einsum('bhij,bhj->bhi', state, r_t)
    return state, y

def rwkv7_time_mix(h, shift_prev, wkv_prev, mix, w_r, w_k, w_v, w_o, w0, w1, w2,
                   a0, a1, a2, g1, g2, k_k, k_a, r_k, lnx_g, lnx_b):
    B, S, D = h.shape
    H, N = RWKV_HEADS, HEAD_DIM
    f32 = jnp.float32
    prev = jnp.concatenate([shift_prev[:, None, :].astype(h.dtype), h[:, :-1]], axis=1)
    xx = prev - h
    xr, xw, xk, xv, xa, xg = [h + xx * mix[i] for i in range(N_MIX_VEC)]
    r = xr @ w_r
    k = xk @ w_k
    v = xv @ w_v
    w = -jax.nn.softplus(-(w0 + jnp.tanh(xw @ w1) @ w2)) - 0.5
    a = jax.nn.sigmoid(a0 + (xa @ a1) @ a2)
    g = jax.nn.sigmoid(xg @ g1) @ g2
    heads = lambda t: t.reshape(B, S, H, N).astype(f32)
    kk = heads(k * k_k)
    kk = kk / jnp.maximum(jnp.sqrt(jnp.sum(kk * kk, axis=-1, keepdims=True)), 1e-12)
    k = k * (1 + (a - 1) * k_a)
    r_h, k_h, v_h, a_h = heads(r), heads(k), heads(v), heads(a)
    decay = jnp.exp(-jnp.exp(heads(w)))
    seq_first = lambda t: jnp.moveaxis(t, 1, 0)
    xs = tuple(seq_first(t) for t in (r_h, decay, k_h, v_h, -kk, kk * a_h))
    state, y = lax.scan(wkv7_step, wkv_prev.astype(f32), xs)
    y = jnp.moveaxis(y, 0, 1)
    mu = jnp.mean(y, axis=-1, keepdims=True)
    var = jnp.mean(jnp.square(y - mu), axis=-1, keepdims=True)
    y = ((y - mu) * lax.rsqrt(var + LNX_EPS) * lnx_g.astype(f32).reshape(H, N)
         + lnx_b.astype(f32).reshape(H, N))
    bonus = jnp.sum(r_h * k_h * r_k.astype(f32), axis=-1, keepdims=True) * v_h
    out = ((y + bonus).reshape(B, S, D).astype(h.dtype) * g) @ w_o
    return out, h[:, -1], state.astype(wkv_prev.dtype)

def qkv_proj(h, w_qkv, b_qkv, pos):
    B, S, _ = h.shape
    qkv = h @ w_qkv + b_qkv
    nq, nk = ATT_HEADS * HEAD_DIM, KV_HEADS * HEAD_DIM
    q = qkv[..., :nq].reshape(B, S, ATT_HEADS, HEAD_DIM)
    k = qkv[..., nq:nq + nk].reshape(B, S, KV_HEADS, HEAD_DIM)
    v = qkv[..., nq + nk:].reshape(B, S, KV_HEADS, HEAD_DIM)
    return rope_partial(q, pos), rope_partial(k, pos), v

def swa_prompt(h, w_qkv, b_qkv, w_o, sink):
    B, S, _ = h.shape
    pos = jnp.arange(S, dtype=jnp.int32)
    q, k, v = qkv_proj(h, w_qkv, b_qkv, pos)
    nb = S // ATT_BLOCK
    qb = q.reshape(B, nb, ATT_BLOCK, KV_HEADS, GROUP, HEAD_DIM)
    kb = k.reshape(B, nb, ATT_BLOCK, KV_HEADS, HEAD_DIM)
    vb = v.reshape(B, nb, ATT_BLOCK, KV_HEADS, HEAD_DIM)

    def with_prev(t):
        prev = jnp.concatenate([jnp.zeros_like(t[:, :1]), t[:, :-1]], axis=1)
        return jnp.concatenate([prev, t], axis=2)

    kw, vw = with_prev(kb), with_prev(vb)
    scores = jnp.einsum('bnqkgd,bnskd->bnkgqs', qb, kw,
                        preferred_element_type=jnp.float32) * (HEAD_DIM ** -0.5)
    blk = jnp.arange(nb, dtype=jnp.int32)[:, None, None]
    qpos = blk * ATT_BLOCK + jnp.arange(ATT_BLOCK, dtype=jnp.int32)[None, :, None]
    kpos = (blk - 1) * ATT_BLOCK + jnp.arange(2 * ATT_BLOCK, dtype=jnp.int32)[None, None, :]
    mask = (kpos <= qpos) & (kpos >= qpos - WINDOW) & (kpos >= 0)
    scores = jnp.where(mask[None, :, None, None], scores, -jnp.inf)
    probs = sink_softmax(scores, sink.astype(jnp.float32).reshape(KV_HEADS, GROUP)).astype(h.dtype)
    o = jnp.einsum('bnkgqs,bnskd->bnqkgd', probs, vw).reshape(B, S, ATT_HEADS * HEAD_DIM)
    w_keep = min(WINDOW, S)
    return o @ w_o, k[:, S - w_keep:], v[:, S - w_keep:]

def swa_sample(h, k_buf, v_buf, w_qkv, b_qkv, w_o, sink):
    B, S, _ = h.shape
    W = k_buf.shape[1]
    qpos = PAST_LEN + jnp.arange(S, dtype=jnp.int32)
    q, k, v = qkv_proj(h, w_qkv, b_qkv, qpos)
    k_all = jnp.concatenate([k_buf.astype(k.dtype), k], axis=1)
    v_all = jnp.concatenate([v_buf.astype(v.dtype), v], axis=1)
    kpos = jnp.concatenate([PAST_LEN - W + jnp.arange(W, dtype=jnp.int32), qpos])
    mask = (kpos[None, :] <= qpos[:, None]) & (kpos[None, :] >= qpos[:, None] - WINDOW)
    qg = q.reshape(B, S, KV_HEADS, GROUP, HEAD_DIM)
    scores = jnp.einsum('bqkgd,bskd->bkgqs', qg, k_all,
                        preferred_element_type=jnp.float32) * (HEAD_DIM ** -0.5)
    scores = jnp.where(mask, scores, -jnp.inf)
    probs = sink_softmax(scores, sink.astype(jnp.float32).reshape(KV_HEADS, GROUP)).astype(h.dtype)
    o = jnp.einsum('bkgqs,bskd->bqkgd', probs, v_all).reshape(B, S, ATT_HEADS * HEAD_DIM)
    return o @ w_o, k_all[:, S:], v_all[:, S:]

def setup_inputs(seed: int = 0) -> dict:
    key = jax.random.key(seed)
    ks = iter(jax.random.split(key, 64))
    f32 = jnp.float32

    def nrm(shape, scale):
        return jax.random.normal(next(ks), shape, f32) * scale

    def uni(shape, lo, hi):
        return jax.random.uniform(next(ks), shape, f32, lo, hi)

    D, H, N = D_MODEL, RWKV_HEADS, HEAD_DIM
    w_buf = min(WINDOW, PAST_LEN)
    qkv_out = (ATT_HEADS + 2 * KV_HEADS) * HEAD_DIM
    return {
        'x_prompt': nrm((BATCH, SEQ, D), 1.0),
        'x_sample': nrm((DEC_BATCH, DEC_SEQ, D), 1.0),
        'c_prompt': nrm((BATCH, D), 1.0),
        'c_sample': nrm((DEC_BATCH, D), 1.0),
        'state_wkv': nrm((N_RWKV, DEC_BATCH, H, N, N), 0.3),
        'state_shift': nrm((N_RWKV, DEC_BATCH, D), 1.0),
        'cache_k': nrm((N_ATTN, DEC_BATCH, w_buf, KV_HEADS, HEAD_DIM), 1.0),
        'cache_v': nrm((N_ATTN, DEC_BATCH, w_buf, KV_HEADS, HEAD_DIM), 1.0),
        'norm1_g': 1.0 + nrm((DEPTH, D), 0.05),
        'norm2_g': 1.0 + nrm((DEPTH, D), 0.05),
        'ada_w': nrm((DEPTH, D, N_ADA * D), 0.5 * D ** -0.5),
        'ada_b': nrm((DEPTH, N_ADA * D), 0.02),
        'mlp_up': nrm((DEPTH, D, D_FF), D ** -0.5),
        'mlp_down': nrm((DEPTH, D_FF, D), D_FF ** -0.5),
        'final_g': 1.0 + nrm((D,), 0.05),
        'rw_mix': uni((N_RWKV, N_MIX_VEC, D), 0.0, 1.0),
        'rw_wr': nrm((N_RWKV, D, D), D ** -0.5),
        'rw_wk': nrm((N_RWKV, D, D), D ** -0.5),
        'rw_wv': nrm((N_RWKV, D, D), D ** -0.5),
        'rw_wo': nrm((N_RWKV, D, D), D ** -0.5),
        'rw_w0': uni((N_RWKV, D), -6.0, 1.0),
        'rw_w1': nrm((N_RWKV, D, DECAY_LORA), D ** -0.5),
        'rw_w2': nrm((N_RWKV, DECAY_LORA, D), 0.5 * DECAY_LORA ** -0.5),
        'rw_a0': nrm((N_RWKV, D), 0.5),
        'rw_a1': nrm((N_RWKV, D, AAA_LORA), D ** -0.5),
        'rw_a2': nrm((N_RWKV, AAA_LORA, D), 0.5 * AAA_LORA ** -0.5),
        'rw_g1': nrm((N_RWKV, D, GATE_LORA), D ** -0.5),
        'rw_g2': nrm((N_RWKV, GATE_LORA, D), GATE_LORA ** -0.5),
        'rw_kk': 0.85 + nrm((N_RWKV, D), 0.05),
        'rw_ka': 1.0 + nrm((N_RWKV, D), 0.05),
        'rw_rk': nrm((N_RWKV, H, N), 0.1),
        'rw_lnx_g': 1.0 + nrm((N_RWKV, D), 0.05),
        'rw_lnx_b': nrm((N_RWKV, D), 0.02),
        'at_wqkv': nrm((N_ATTN, D, qkv_out), D ** -0.5),
        'at_bqkv': nrm((N_ATTN, qkv_out), 0.02),
        'at_wo': nrm((N_ATTN, ATT_HEADS * HEAD_DIM, D), (ATT_HEADS * HEAD_DIM) ** -0.5),
        'at_sink': nrm((N_ATTN, ATT_HEADS), 1.0),
    }

def reference(x_prompt, x_sample, c_prompt, c_sample, state_wkv, state_shift, cache_k, cache_v,
              norm1_g, norm2_g, ada_w, ada_b, mlp_up, mlp_down, final_g,
              rw_mix, rw_wr, rw_wk, rw_wv, rw_wo, rw_w0, rw_w1, rw_w2, rw_a0, rw_a1, rw_a2,
              rw_g1, rw_g2, rw_kk, rw_ka, rw_rk, rw_lnx_g, rw_lnx_b,
              at_wqkv, at_bqkv, at_wo, at_sink):
    xp, xs = x_prompt, x_sample
    bp = xp.shape[0]
    wkv_p, wkv_s, sh_p, sh_s = [], [], [], []
    k_p, k_s, v_p, v_s = [], [], [], []
    for i in range(DEPTH):
        mp = ada_params(c_prompt, ada_w[i], ada_b[i])
        ms = ada_params(c_sample, ada_w[i], ada_b[i])
        hp = pre_norm(xp, norm1_g[i], mp[0], mp[1])
        hs = pre_norm(xs, norm1_g[i], ms[0], ms[1])
        j = i // N_MIXERS
        if i % N_MIXERS == 0:
            prm = (rw_mix[j], rw_wr[j], rw_wk[j], rw_wv[j], rw_wo[j], rw_w0[j], rw_w1[j], rw_w2[j],
                   rw_a0[j], rw_a1[j], rw_a2[j], rw_g1[j], rw_g2[j], rw_kk[j], rw_ka[j], rw_rk[j],
                   rw_lnx_g[j], rw_lnx_b[j])
            zero_shift = jnp.zeros((bp, D_MODEL), hp.dtype)
            zero_wkv = jnp.zeros((bp, RWKV_HEADS, HEAD_DIM, HEAD_DIM), hp.dtype)
            op, shift_new_p, wkv_new_p = rwkv7_time_mix(hp, zero_shift, zero_wkv, *prm)
            os_, shift_new_s, wkv_new_s = rwkv7_time_mix(hs, state_shift[j], state_wkv[j], *prm)
            sh_p.append(shift_new_p)
            wkv_p.append(wkv_new_p)
            sh_s.append(shift_new_s)
            wkv_s.append(wkv_new_s)
        else:
            op, kn_p, vn_p = swa_prompt(hp, at_wqkv[j], at_bqkv[j], at_wo[j], at_sink[j])
            os_, kn_s, vn_s = swa_sample(hs, cache_k[j], cache_v[j], at_wqkv[j], at_bqkv[j],
                                        at_wo[j], at_sink[j])
            k_p.append(kn_p)
            v_p.append(vn_p)
            k_s.append(kn_s)
            v_s.append(vn_s)
        xp = xp + mp[2] * op
        xs = xs + ms[2] * os_
        hp = pre_norm(xp, norm2_g[i], mp[3], mp[4])
        hs = pre_norm(xs, norm2_g[i], ms[3], ms[4])
        xp = xp + mp[5] * sq_relu_mlp(hp, mlp_up[i], mlp_down[i])
        xs = xs + ms[5] * sq_relu_mlp(hs, mlp_up[i], mlp_down[i])
    y_prompt = rms_norm(xp, final_g)
    y_sample = rms_norm(xs, final_g)
    return (y_prompt, y_sample, jnp.stack(wkv_p), jnp.stack(wkv_s), jnp.stack(sh_p), jnp.stack(sh_s),
            jnp.stack(k_p), jnp.stack(k_s), jnp.stack(v_p), jnp.stack(v_s))


_drawn_inputs = setup_inputs


def setup_inputs(seed=0):
    import zlib

    import numpy as np

    out = dict(_drawn_inputs(seed))
    spreads = {}
    factors = {'rw_lnx_g': 7.078, 'rw_lnx_b': 24.479, 'at_bqkv': 3.17, 'at_sink': 8.0}
    for name, (base, spread) in spreads.items():
        noise = np.random.default_rng([zlib.crc32(name.encode()), seed]).standard_normal(out[name].shape)
        drawn = base * np.exp(spread * noise) if base else spread * noise
        out[name] = __import__('jax').numpy.asarray(drawn.astype(out[name].dtype))
    for name, factor in factors.items():
        out[name] = (out[name] * factor).astype(out[name].dtype)
    return out
```

```python
from contextlib import ExitStack, contextmanager

import numpy as np

import concourse.bass as bass
from concourse import mybir

F32 = mybir.dt.float32
F32R = mybir.dt.float32r
ALU = mybir.AluOpType
ACT = mybir.ActivationFunctionType
AX = mybir.AxisListType.X

D = 1024
DB = D // 128
SEQ = 1024
DEC = 8
NV = 1 + DEC
TOK = SEQ + DEC
NT = 3
TT = TOK // NT
HD = 64
HEADS = D // HD
C = 64
NCH = SEQ // C
N_ADA = 6
FF_GROUPS = 4
KV = 4
WIN = 128
EPS = 1e-6
LNX_EPS = 64e-5
DECAY_SCALE = float(np.exp(-0.5))
SCALE = HD ** -0.5

PARAM_TABLES = [
    [("norm1_g", 16), ("norm2_g", 16), ("final_g", 8), ("rw_mix", 48), ("at_bqkv", 12)],
    [("rw_w0", 8), ("rw_a0", 8), ("rw_kk", 8), ("rw_ka", 8), ("rw_rk", 8), ("rw_lnx_g", 8), ("rw_lnx_b", 8)],
    [("ada_b", 96)],
]
PARAM_AT = {}
for _t, _rows in enumerate(PARAM_TABLES):
    _at = 128 * _t
    for _name, _n in _rows:
        PARAM_AT[_name] = _at
        _at += _n

CONST_COLS = [("ident", 128), ("ones", 128), ("headsum", 128), ("lt", 64), ("le", 64), ("swap", 128)]
CONST_AT, _at = {}, 0
for _name, _n in CONST_COLS:
    CONST_AT[_name] = _at
    _at += _n
CONST_N = _at
WIDE = ["chunkstart", "cos", "sin"]


def shape_constants():
    p = np.arange(128)
    small = {
        "ident": np.eye(128),
        "ones": np.ones((128, 128)),
        "headsum": (p[:, None] // 64 == p[None, :] // 64),
        "lt": (p[:, None] % 64 < np.arange(64)[None, :]),
        "le": (p[:, None] % 64 <= np.arange(64)[None, :]),
    }
    d = p % 64
    partner = np.where(d < 8, p + 8, np.where(d < 16, p - 8, p))
    swap = np.zeros((128, 128))
    swap[p, partner] = 1
    small["swap"] = swap
    const = np.concatenate([np.asarray(small[n], np.float32) for n, _ in CONST_COLS], 1)
    start = np.ones((128, TOK))
    start[:, 0:SEQ:C] = 0
    start[:, SEQ:] = 0
    pos = np.concatenate([np.arange(SEQ), np.full(DEC, 2048)]).astype(np.float32)
    inv = (np.float32(500000.0) ** (-np.arange(8, dtype=np.float32) / np.float32(8))).astype(np.float32)
    ang = (pos[None, :] * inv[np.minimum(d, 15) % 8][:, None]).astype(np.float64)
    rot = (d < 16)[:, None]
    cos = np.where(rot, np.cos(ang), 1.0)
    sin = np.where(rot, np.sin(ang) * np.where(d < 8, -1.0, 1.0)[:, None], 0.0)
    wide = np.concatenate([start, cos, sin], 1).astype(np.float32)
    q, k = np.arange(128)[:, None], np.arange(256)[None, :]
    mask = np.where((k - 128 <= q) & (k - 128 >= q - WIN), 0, -1e30).astype(np.float32)
    return {"const_small": const, "const_wide": wide, "const_mask": mask}


class Chain:

    def __init__(self, eng, sem, per=0, i=0, base=0):
        self.eng, self.sem, self.n = eng, sem, 0
        self.start = i * per + base
        self.per = per

    def link(self, ins):
        ins.then_inc(self.sem, 1)
        self.n += 1
        self.eng.wait_ge(self.sem, self.start + self.n)


class Net:

    def semaphore(self, name):
        self.sems.append(self.nc.alloc_semaphore(name=name))
        return self.sems[-1]


@contextmanager
def stage(net):
    net.sems = []
    yield
    net.nc.clear_and_free_semaphores(net.sems)
    net.nc.all_engine_barrier()


def tiles(ap, n=TT):
    return ap.rearrange("p (n t) -> p n t", t=n)


def blk(ap, i):
    return ap[:, bass.ds(i, 1), :].rearrange("p a n -> p (a n)")


def build(nc, io):
    with ExitStack() as root:
        net = Net()
        net.nc, net.io = nc, io

        def sb(name, shape, dt=F32):
            return root.enter_context(nc.sbuf_tensor(name, shape, dt))

        net.const = sb("const", [128, CONST_N])
        net.param = sb("param", [128, 3 * 128])
        net.mod = sb("mod", [128, 2 * N_ADA * DB, NV])
        net.gain = sb("gain", [128, 5, DB, NV])

        def scratch(name, shape):
            return nc.dram_tensor(name, shape, F32).ap()

        net.scratch = scratch
        net.x_saved = scratch("x_saved", [128, DB, TOK])
        net.sL, net.sLm, net.sA, net.sG, net.sRt, net.sAt, net.sBt, net.sKt, net.sBS, net.sBV = (
            scratch("scr_" + n, [DB, 128, TOK]) for n in ("L", "Lm", "A", "G", "Rt", "At", "Bt", "Kt", "BS", "BV"))
        net.sBK = scratch("scr_BK", [NCH, 128, DB, 2, C])
        net.sM = scratch("scr_M", [NCH, DB, 128, C])
        net.sT = scratch("scr_T", [NCH, DB, 128, C])
        net.sG3 = scratch("scr_G3", [NCH, 128, DB, 3, C])
        net.sV = scratch("scr_V", [TOK, D])
        net.sY = scratch("scr_Y", [TOK, D])
        net.sSmp = scratch("scr_Smp", [6, DEC, D])
        with ExitStack() as rwkv:
            net.hx = rwkv.enter_context(nc.sbuf_tensor("hx", [128, DB, 1 + TOK], F32))
            net.sprev = rwkv.enter_context(nc.sbuf_tensor("sprev", [128, DB, DEC], F32))
            net.pend = rwkv.enter_context(nc.sbuf_tensor("pend", [128, DB, NCH], F32))
            net.Ps = rwkv.enter_context(nc.sbuf_tensor("Ps", [128, DB, DEC], F32))
            with ExitStack() as first:
                net.X = first.enter_context(nc.sbuf_tensor("X0", [128, DB, TOK], F32))
                with stage(net):
                    stage_start(net)
                with stage(net):
                    stage_norm1_rwkv(net)
            with ExitStack() as ops:
                operands(net, ops, "rk")
                with stage(net):
                    stage_lora(net, "w")
                with stage(net):
                    stage_lora(net, "a")
                with stage(net):
                    stage_lora(net, "g")
                with stage(net):
                    stage_r(net)
                with stage(net):
                    stage_k(net)
            with stage(net):
                stage_products(net)
            with ExitStack() as ops:
                operands(net, ops, "v")
                with stage(net):
                    stage_v(net)
            with stage(net):
                stage_samples(net)
            with stage(net):
                stage_scan(net)
        net.X = sb("X", [128, DB, TOK])
        with ExitStack() as ops:
            operands(net, ops, "ro")
            with stage(net):
                stage_rwkv_out(net)
            with stage(net):
                stage_mlp(net, 0)
        with ExitStack() as ops:
            operands(net, ops, "at", False)
            with ExitStack() as heads:
                def hb(name, shape):
                    return heads.enter_context(nc.sbuf_tensor(name, shape, F32))
                net.Q = hb("Q", [128, DB, TOK])
                net.Kd = hb("Kd", [128, KV, TOK])
                net.Vt = hb("Vt", [128, SEQ // 128 + 1, KV * HD])
                net.Vd = hb("Vd", [128, KV, DEC])
                with stage(net):
                    stage_qkv(net)
                with stage(net):
                    stage_attend_samples(net)
                with stage(net):
                    stage_attend(net)
            with stage(net):
                stage_attend_out(net)
        with ExitStack() as ops:
            operands(net, ops, "m1")
            with stage(net):
                stage_mlp(net, 1)
        with stage(net):
            stage_final(net)


def operands(net, ctx, tag, with_weights=True):
    nc = net.nc
    net.HH = ctx.enter_context(nc.sbuf_tensor(f"{tag}_HH", [128, DB, TOK], F32R))
    net.HL = ctx.enter_context(nc.sbuf_tensor(f"{tag}_HL", [128, DB, TOK], F32R))
    if with_weights:
        weights(net, ctx, tag)


def weights(net, ctx, tag):
    nc = net.nc
    net.wraw = ctx.enter_context(nc.sbuf_tensor(f"{tag}_wraw", [128, 2, DB, 128], F32))
    net.wH = ctx.enter_context(nc.sbuf_tensor(f"{tag}_wH", [128, 2, DB, 128], F32R))
    net.wL = ctx.enter_context(nc.sbuf_tensor(f"{tag}_wL", [128, 2, DB, 128], F32R))


def c_(net, name):
    at = CONST_AT[name]
    return net.const[:, at:at + dict(CONST_COLS)[name]]




def stage_start(net):
    nc, io = net.nc, net.io
    GROUP = 2048
    groups = 2 * N_ADA * D // GROUP
    per_layer = groups // 2
    SLOTS = 6
    with ExitStack() as ctx:
        def sb(name, shape, dt=F32):
            return ctx.enter_context(nc.sbuf_tensor(name, shape, dt))

        def sem(name):
            return net.semaphore(name)

        rows = sb("param_rows", [128, 3, 128])
        crow = sb("c_row", [NV, D])
        csig = sb("c_sig", [NV, D])
        csil = sb("c_silu", [128, DB, 32])
        xrow = sb("x_rows", [128, DB, D])
        xsrow = sb("xs_rows", [DEC, D])
        ada_w = sb("ada_ring", [128, 8, GROUP])
        strip = sb("ada_strip", [128, 512])
        tp = [ctx.enter_context(nc.psum_tensor(f"tp{i}", [128, 4, 128], F32)) for i in range(2)]
        acc = ctx.enter_context(nc.psum_tensor("ada_acc", [128, 512], F32))
        accT = ctx.enter_context(nc.psum_tensor("ada_accT", [128, 4, 128], F32))

        s_const, s_param, s_c, s_x = sem("s_const"), sem("s_param"), sem("s_c"), sem("s_x")
        s_w = [sem(f"s_adaw{k}") for k in range(8)]
        s_rows0 = sem("s_rows_zero")
        s_sig, s_sil, s_sil0, s_silT = sem("s_sig"), sem("s_sil"), sem("s_sil_zero"), sem("s_silT")
        s_tp, s_tp_free = sem("s_tp"), sem("s_tp_free")
        s_acc, s_strip, s_accT, s_mod = sem("s_acc"), sem("s_strip"), sem("s_accT"), sem("s_mod")
        s_dv = sem("s_dv")
        ident = c_(net, "ident")
        n_param = 0
        block = ctx.enter_context(nc.Block())

        turns = [("param", None)] + [("c", i) for i in range(2)] + [("x", (t, h)) for t in range(DB) for h in range(2)] + [("xs", h) for h in range(2)]

        @block.sync
        def _(sp):
            sp.dma_start(net.const[:], io["const_small"]).then_inc(s_const, 16)
            sp.dma_start(crow[0:1, :], io["c_prompt"]).then_inc(s_c, 16)
            sp.dma_start(crow[1:NV, :], io["c_sample"]).then_inc(s_c, 16)
            sp.wait_ge(s_rows0, 1)
            for t, table in enumerate(PARAM_TABLES):
                for name, n in table:
                    at = PARAM_AT[name] - 128 * t
                    ap = io[name]
                    ap = ap.rearrange({1: "(r p) -> r p", 2: "a (r p) -> (a r) p", 3: "a b (r p) -> (a b r) p"}[len(ap.shape)], p=128) if name != "rw_rk" else ap.rearrange("a (b h) d -> (a b) (h d)", h=2)
                    sp.dma_start(rows[at:at + n, t, :], ap).then_inc(s_param, 16)
            for l in range(2):
                with sp.Fori(0, per_layer) as g:
                    for k in range(8):
                        sp.wait_ge(s_acc, g + l * per_layer + 1)
                        sp.dma_start(ada_w[:, k, :], io["ada_w"][l, k * 128:(k + 1) * 128, bass.ds(g * GROUP, GROUP)]).then_inc(s_w[k], 16)

        @block.gpsimd
        def _(pool):
            for t in range(DB):
                pool.dma_start(xrow[:, t, :], io["x_prompt"][0, t * 128:(t + 1) * 128, :]).then_inc(s_x, 16)
            pool.dma_start(xsrow[:], io["x_sample"].rearrange("b o d -> (b o) d")).then_inc(s_x, 16)

        @block.scalar
        def _(act):
            act.wait_ge(s_c, 32)
            nc.scalar.activation(csig[:], crow[:], ACT.Sigmoid).then_inc(s_sig, 1)

        @block.tensor
        def _(pe):
            pe.sem_inc(s_acc, 1)
            pe.wait_ge(s_const, 16)
            for n, (what, arg) in enumerate(turns):
                bank = tp[n % 2]
                if n >= 2:
                    pe.wait_ge(s_tp_free, n - 1)
                if what == "param":
                    pe.wait_ge(s_param, 16 * sum(len(t) for t in PARAM_TABLES))
                    for t in range(3):
                        ins = pe.transpose(bank[:, t, :], rows[:, t, :], ident)
                elif what == "c":
                    pe.wait_ge(s_sil, 1)
                    for q in range(4):
                        ins = pe.transpose(bank[:, q, 0:NV], crow[:, (4 * arg + q) * 128:(4 * arg + q + 1) * 128], ident[0:NV, 0:NV])
                elif what == "x":
                    t, h = arg
                    pe.wait_ge(s_x, 16 * (DB + 1))
                    for q in range(4):
                        ins = pe.transpose(bank[:, q, :], xrow[:, t, (4 * h + q) * 128:(4 * h + q + 1) * 128], ident)
                else:
                    for q in range(4):
                        ins = pe.transpose(bank[:, q, 0:DEC], xsrow[:, (4 * arg + q) * 128:(4 * arg + q + 1) * 128], ident[0:DEC, 0:DEC])
                ins.then_inc(s_tp, 1)
            pe.wait_ge(s_silT, 2)
            with pe.Fori(0, groups) as g:
                pe.wait_ge(s_strip, g + 1)
                for k in range(8):
                    pe.wait_ge(s_w[k], g * 16 + 16)
                    for q in range(4):
                        ins = pe.matmul(acc[32 * q:32 * q + 32, :], csil[:, k, :], ada_w[:, k, 512 * q:512 * q + 512], start=(k == 0), stop=(k == 7), tile_position=(0, 32 * q))
                ins.then_inc(s_acc, 1)
                pe.wait_ge(s_strip, g + 2)
                pe.wait_ge(s_mod, g + 1)
                for r in range(4):
                    ins = pe.transpose(accT[:, r, :], strip[:, r * 128:(r + 1) * 128], ident)
                ins.then_inc(s_accT, 1)

        @block.vector
        def _(dve):
            dve.sem_inc(s_strip, 1)
            dve.sem_inc(s_mod, 1)
            dve.memset(rows[:], 0.0).then_inc(s_rows0, 1)
            dve.memset(csil[:], 0.0).then_inc(s_sil0, 1)
            dve.wait_ge(s_sig, 1)
            dve.tensor_tensor(crow[:], crow[:], csig[:], ALU.mult).then_inc(s_sil, 1)
            dve.wait_ge(s_sil0, 1)
            for n, (what, arg) in enumerate(turns):
                bank = tp[n % 2]
                dve.wait_ge(s_tp, n + 1)
                if what == "param":
                    dve.tensor_copy(net.param[:].rearrange("p (t n) -> p t n", t=3), bank[:, 0:3, :]).then_inc(s_tp_free, 1)
                elif what == "c":
                    ins = dve.tensor_copy(csil[:, 4 * arg:4 * arg + 4, 0:NV], bank[:, :, 0:NV])
                    ins.then_inc(s_silT, 1)
                    dve.wait_ge(s_silT, arg + 1)
                    dve.sem_inc(s_tp_free, 1)
                elif what == "x":
                    t, h = arg
                    dve.tensor_copy(net.X[:, 4 * h:4 * h + 4, t * 128:(t + 1) * 128], bank[:]).then_inc(s_tp_free, 1)
                else:
                    dve.tensor_copy(net.X[:, 4 * arg:4 * arg + 4, SEQ:TOK], bank[:, :, 0:DEC]).then_inc(s_tp_free, 1)
            dve.wait_ge(s_tp_free, len(turns))
            adab = net.param[:, PARAM_AT["ada_b"]:PARAM_AT["ada_b"] + 96]
            with dve.Fori(0, groups) as g:
                dve.wait_ge(s_acc, g + 2)
                dve.tensor_copy(strip[:], acc[:]).then_inc(s_strip, 1)
                dve.wait_ge(s_accT, g + 1)
                dve.tensor_tensor(
                    net.mod[:, bass.ds(g * 16, 16), :].rearrange("p (q r) v -> p q r v", r=4),
                    accT[:].rearrange("p r (q v) -> p q r v", v=32)[:, :, :, 0:NV],
                    adab[:, bass.ds(g * 16, 16)].rearrange("p (q r) -> p q r", r=4).unsqueeze(3).to_broadcast([128, 4, 4, NV]),
                    ALU.add).then_inc(s_mod, 1)
            dve.wait_ge(s_mod, groups + 1)
            for n, (name, l, part) in enumerate([("norm1_g", 0, 1), ("norm2_g", 0, 4), ("norm1_g", 1, 1), ("norm2_g", 1, 4)]):
                at = PARAM_AT[name] + 8 * l
                scale = net.mod[:, (l * N_ADA + part) * DB:(l * N_ADA + part + 1) * DB, :]
                g = net.param[:, at:at + DB].unsqueeze(2).to_broadcast([128, DB, NV])
                dve.scalar_tensor_tensor(out=net.gain[:, n], in0=scale, scalar=1.0, in1=g, op0=ALU.add, op1=ALU.mult).then_inc(s_dv, 1)
            at = PARAM_AT["final_g"]
            dve.tensor_copy(net.gain[:, 4], net.param[:, at:at + DB].unsqueeze(2).to_broadcast([128, DB, NV])).then_inc(s_dv, 1)
            dve.wait_ge(s_dv, 5)


def mod_part(net, layer, part):
    at = (layer * N_ADA + part) * DB
    return net.mod[:, at:at + DB, :]




class Norm:

    def __init__(self, net, ctx, tag, gain, shift, keep=None, split=True):
        nc = net.nc
        self.net, self.gain, self.shift, self.keep, self.split = net, gain, shift, keep, split
        sem = lambda name: net.semaphore(f"{tag}_{name}")
        self.sq = ctx.enter_context(nc.sbuf_tensor(f"{tag}_sq", [128, 2, TOK], F32))
        self.rs = ctx.enter_context(nc.sbuf_tensor(f"{tag}_rs", [128, TOK], F32))
        self.ps = ctx.enter_context(nc.psum_tensor(f"{tag}_ps", [128, NT, 512], F32))
        self.s_sq, self.s_used, self.s_sum = sem("sq"), sem("sq_used"), sem("sum")
        self.s_mean, self.s_root, self.s_rs = sem("mean"), sem("root"), sem("rs")
        self.s_xn, self.s_h, self.s_hi, self.s_lo = sem("xn"), sem("h"), sem("hi"), sem("lo")
        self.s_smp, self.s_dv = sem("smp"), sem("dv")

    def pe(self, pe):
        ones = c_(self.net, "ones")
        for b in range(DB):
            pe.wait_ge(self.s_sq, b + 1)
            for n in range(NT):
                ins = pe.matmul(self.ps[:, n, 0:TT], ones, self.sq[:, b % 2, n * TT:(n + 1) * TT], start=(b == 0), stop=(b == DB - 1))
            ins.then_inc(self.s_used, 1)

    def act(self, act):
        net = self.net
        for b in range(DB):
            if b >= 2:
                act.wait_ge(self.s_used, b - 1)
            act.activation(self.sq[:, b % 2, :], net.X[:, b, :], ACT.Square).then_inc(self.s_sq, 1)
        act.wait_ge(self.s_mean, 1)
        act.activation(self.rs[:], self.rs[:], ACT.Sqrt).then_inc(self.s_root, 1)
        for b in range(DB):
            act.wait_ge(self.s_xn, b + 1)
            h = self.h(b)
            act.activation(h[:, 0:SEQ], self.sq[:, b % 2, 0:SEQ], ACT.Identity, bias=self.shift[:, b, 0:1], scale=self.gain[:, b, 0:1]).then_inc(self.s_h, 1)
            if not self.split:
                continue
            act.wait_ge(self.s_h, b + 1)
            act.wait_ge(self.s_smp, b + 1)
            act.activation(net.HH[:, b, :], h[:, 0:TOK], ACT.Copy).then_inc(self.s_hi, 1)

    def h(self, b):
        return self.sq[:, b % 2, :] if self.keep is None else self.keep[:, b, :]

    def dve(self, dve):
        net = self.net
        dve.wait_ge(self.s_used, DB)
        dve.tensor_scalar(tiles(self.rs[:]), self.ps[:, :, 0:TT], 1.0 / D, EPS, ALU.mult, ALU.add).then_inc(self.s_mean, 1)
        dve.wait_ge(self.s_root, 1)
        dve.reciprocal(self.rs[:], self.rs[:]).then_inc(self.s_rs, 1)
        dve.wait_ge(self.s_rs, 1)
        for b in range(DB):
            if b >= 2 and self.split:
                dve.wait_ge(self.s_hi, b - 1)
                dve.wait_ge(self.s_lo, b - 1)
            elif b >= 2:
                dve.wait_ge(self.s_h, b - 1)
                dve.wait_ge(self.s_smp, b - 1)
            xn = self.sq[:, b % 2, :]
            dve.tensor_tensor(xn, net.X[:, b, :], self.rs[:], ALU.mult).then_inc(self.s_xn, 1)
            dve.wait_ge(self.s_xn, b + 1)
            h = self.h(b)
            dve.tensor_tensor(h[:, SEQ:TOK], xn[:, SEQ:TOK], self.gain[:, b, 1:NV], ALU.mult).then_inc(self.s_dv, 1)
            dve.wait_ge(self.s_dv, b + 1)
            dve.tensor_tensor(h[:, SEQ:TOK], h[:, SEQ:TOK], self.shift[:, b, 1:NV], ALU.add).then_inc(self.s_smp, 1)
            if b >= 1 and self.split:
                self.low(dve, b - 1)
        if self.split:
            self.low(dve, DB - 1)

    def low(self, dve, b):
        net = self.net
        dve.wait_ge(self.s_hi, b + 1)
        dve.wait_ge(self.s_h, b + 1)
        dve.tensor_tensor(net.HL[:, b, :], self.h(b)[:, 0:TOK], net.HH[:, b, :].bitcast(F32), ALU.subtract).then_inc(self.s_lo, 1)




class Panels:

    LOW0, DONE0 = 2, 2 * NT

    def __init__(self, net, ctx, tag, cols=128):
        nc = net.nc
        self.net, self.cols = net, cols
        sem = lambda name: net.semaphore(f"{tag}_{name}")
        self.acc = ctx.enter_context(nc.psum_tensor(f"{tag}_acc", [128, NT, 512], F32))
        self.landed = [sem("landed0"), sem("landed1")]
        self.high, self.low = sem("high"), sem("low")
        self.done, self.free = sem("acc_done"), sem("acc_free")

    def load(self, sp, p, s, src):
        sp.wait_ge(self.low, p + 1)
        sp.dma_start(self.net.wraw[:, s, :, 0:self.cols], src).then_inc(self.landed[s], 16)

    def split(self, pool, p, s, i):
        net = self.net
        raw, high = net.wraw[:, s, :, 0:self.cols], net.wH[:, s, :, 0:self.cols]
        pool.wait_ge(self.landed[s], i * 16 + 16)
        pool.wait_ge(self.done, p * NT + NT)
        one = c_(net, "ones")[:, 0:self.cols].unsqueeze(1).to_broadcast([128, DB, self.cols])
        pool.tensor_tensor(high, raw, one, ALU.mult).then_inc(self.high, 1)
        pool.wait_ge(self.high, p + 1)
        pool.tensor_tensor(net.wL[:, s, :, 0:self.cols], raw, high.bitcast(F32), ALU.subtract).then_inc(self.low, 1)

    def multiply(self, pe, p, s, hi, lo, ready=None, free=None):
        net = self.net
        pe.wait_ge(self.low, p + 1 + self.LOW0)
        for n in range(NT):
            for sem, value in free or [(self.free, p * NT + 1)]:
                pe.wait_ge(sem, value + n)
            t = slice(n * TT, (n + 1) * TT)
            for k in range(DB):
                if n == 0 and ready is not None:
                    pe.wait_ge(ready[0], ready[1] + k)
                out = self.acc[0:self.cols, n, 0:TT]
                wh, wl = net.wH[:, s, k, 0:self.cols], net.wL[:, s, k, 0:self.cols]
                pe.matmul(out, wh, hi[:, k, t], start=(k == 0), stop=False)
                pe.matmul(out, wh, lo[:, k, t], start=False, stop=False)
                ins = pe.matmul(out, wl, hi[:, k, t], start=False, stop=(k == DB - 1))
            ins.then_inc(self.done, 1)

    def summed(self, eng, p, n):
        eng.wait_ge(self.done, p * NT + n + 1 + self.DONE0)


def panel_of(w, m):
    return w[:, bass.ds(m, 128)].rearrange("(k p) m -> p k m", p=128)


def add_gated(dve, net, pan, p, m, gate, tmp, s_free, s_tmp, n_before):
    X = blk(net.X, m)
    for n in range(NT):
        pan.summed(dve, p, n)
        a, z = n * TT, min((n + 1) * TT, SEQ)
        ins = dve.scalar_tensor_tensor(out=X[:, a:z], in0=pan.acc[:, n, 0:z - a], scalar=blk(gate, m)[:, 0:1], in1=X[:, a:z], op0=ALU.mult, op1=ALU.add)
        if n < NT - 1:
            ins.then_inc(s_free, 1)
    dve.tensor_tensor(tmp, pan.acc[:, NT - 1, TT - DEC:TT], blk(gate, m)[:, 1:NV], ALU.mult).then_inc(s_tmp, 1)
    dve.wait_ge(s_tmp, n_before + 1)
    dve.tensor_tensor(X[:, SEQ:TOK], X[:, SEQ:TOK], tmp, ALU.add).then_inc(s_free, 1)


def stage_mlp(net, layer):
    nc, io = net.nc, net.io
    up = io["mlp_up"][layer]
    down = io["mlp_down"][layer]
    gate = mod_part(net, layer, 5)
    with ExitStack() as ctx:
        def sb(name, shape, dt=F32):
            return ctx.enter_context(nc.sbuf_tensor(f"mlp{layer}_{name}", shape, dt))

        def sem(name):
            return net.semaphore(f"mlp{layer}_{name}")

        with ExitStack() as nctx:
            norm = Norm(net, nctx, f"mlpn{layer}", net.gain[:, 2 * layer + 1], mod_part(net, layer, 3))
            block = nctx.enter_context(nc.Block())
            block.tensor(norm.pe)
            block.scalar(norm.act)
            block.vector(norm.dve)
        GH, GL = sb("GH", [128, DB, TOK], F32R), sb("GL", [128, DB, TOK], F32R)
        act_buf = sb("relu", [128, 2, TOK])
        smp = sb("smp", [128, DEC])
        pan = Panels(net, ctx, f"mlp{layer}p")
        s_relu, s_sqr, s_gh, s_gl, s_smp = sem("relu"), sem("sqr"), sem("gh"), sem("gl"), sem("smp")
        s_added = sem("added")
        block = ctx.enter_context(nc.Block())
        GP = 2 * DB

        @block.sync
        def _(sp):
            with sp.Fori(0, FF_GROUPS) as g:
                with sp.Fori(0, DB // 2) as j:
                    for s in range(2):
                        pan.load(sp, g * GP + j * 2 + s, s, panel_of(up, g * 1024 + j * 256 + s * 128))
                with sp.Fori(0, DB // 2) as j:
                    for s in range(2):
                        pan.load(sp, g * GP + DB + j * 2 + s, s, panel_of(down[bass.ds(g * 1024, 1024), :], j * 256 + s * 128))

        @block.gpsimd
        def _(pool):
            with pool.Fori(0, FF_GROUPS * DB) as j:
                for s in range(2):
                    pan.split(pool, j * 2 + s, s, j)

        @block.tensor
        def _(pe):
            with pe.Fori(0, FF_GROUPS) as g:
                with pe.Fori(0, DB // 2) as j:
                    for s in range(2):
                        pan.multiply(pe, g * GP + j * 2 + s, s, net.HH, net.HL, free=[(pan.free, (g * DB + j * 2 + s) * NT + 1), (s_added, g * DB * NT + 1)])
                with pe.Fori(0, DB // 2) as j:
                    for s in range(2):
                        pan.multiply(pe, g * GP + DB + j * 2 + s, s, GH, GL, ready=(s_gl, g * DB + 3),
                                     free=[(pan.free, (g + 1) * DB * NT + 1), (s_added, (g * DB + j * 2 + s) * NT + 1)])

        @block.scalar
        def _(act):
            act.sem_inc(pan.free, NT)
            with act.Fori(0, FF_GROUPS) as g:
                with act.Fori(0, DB // 2) as j:
                    for s in range(2):
                        h, p = g * DB + j * 2 + s, g * GP + j * 2 + s
                        act.wait_ge(s_gl, h + 1)
                        for n in range(NT):
                            pan.summed(act, p, n)
                            act.activation(act_buf[:, s, n * TT:(n + 1) * TT], pan.acc[:, n, 0:TT], ACT.Relu).then_inc(pan.free, 1)
                        act.wait_ge(s_sqr, h + 1)
                        act.activation(blk(GH, j * 2 + s), act_buf[:, s, :], ACT.Copy).then_inc(s_gh, 1)

        @block.vector
        def _(dve):
            dve.sem_inc(s_gl, 2)
            dve.sem_inc(pan.low, pan.LOW0)
            dve.sem_inc(pan.done, pan.DONE0)
            dve.sem_inc(s_added, NT)
            with dve.Fori(0, FF_GROUPS) as g:
                with dve.Fori(0, DB // 2) as j:
                    for s in range(2):
                        h, p = g * DB + j * 2 + s, g * GP + j * 2 + s
                        dve.wait_ge(pan.free, h * NT + 2 * NT)
                        dve.tensor_tensor(act_buf[:, s, :], act_buf[:, s, :], act_buf[:, s, :], ALU.mult).then_inc(s_sqr, 1)
                        dve.wait_ge(s_gh, h + 1)
                        dve.wait_ge(s_sqr, h + 1)
                        dve.tensor_tensor(blk(GL, j * 2 + s), act_buf[:, s, :], blk(GH, j * 2 + s).bitcast(F32), ALU.subtract).then_inc(s_gl, 1)
                with dve.Fori(0, DB // 2) as j:
                    for s in range(2):
                        add_gated(dve, net, pan, g * GP + DB + j * 2 + s, j * 2 + s, gate, smp[:], s_added, s_smp, g * DB + j * 2 + s)





def row(scratch, b):
    return scratch[bass.ds(b, 1)].rearrange("a p t -> p (a t)")


def stage_norm1_rwkv(net):
    nc, io = net.nc, net.io
    with ExitStack() as ctx:
        norm = Norm(net, ctx, "rn", net.gain[:, 0], mod_part(net, 0, 0), keep=net.hx[:, :, 1:1 + TOK], split=False)
        sem = lambda name: net.semaphore(f"rn_{name}")
        srow = ctx.enter_context(nc.sbuf_tensor("shift_rows", [DEC, D], F32))
        last = ctx.enter_context(nc.sbuf_tensor("last_rows", [NV, D], F32))
        tp = [ctx.enter_context(nc.psum_tensor(f"rn_tp{i}", [128, 4, 128], F32)) for i in range(2)]
        s_in, s_tp, s_prev, s_last, s_out, s_zero = sem("in"), sem("tp"), sem("prev"), sem("last"), sem("out"), sem("zero")
        ident = c_(net, "ident")
        block = ctx.enter_context(nc.Block())

        @block.sync
        def _(sp):
            sp.dma_start(srow[:], io["state_shift"][0]).then_inc(s_in, 16)
            sp.dma_start(net.x_saved, net.X[:]).then_inc(s_out, 16)
            sp.wait_ge(s_last, 4)
            sp.dma_start(io["out_shift_prompt"].rearrange("a b d -> (a b) d"), last[0:1, :]).then_inc(s_out, 16)
            sp.dma_start(io["out_shift_sample"].rearrange("a b d -> (a b) d"), last[1:NV, :]).then_inc(s_out, 16)
            sp.wait_ge(s_out, 48)

        @block.tensor
        def _(pe):
            norm.pe(pe)
            pe.wait_ge(s_in, 16)
            for n in range(2):
                for q in range(4):
                    ins = pe.transpose(tp[n][:, q, 0:DEC], srow[:, (4 * n + q) * 128:(4 * n + q + 1) * 128], ident[0:DEC, 0:DEC])
                ins.then_inc(s_tp, 1)
            pe.wait_ge(norm.s_h, DB)
            pe.wait_ge(norm.s_smp, DB)
            for n in range(2):
                pe.wait_ge(s_prev, n + 1)
                for q in range(4):
                    ins = pe.transpose(tp[n][0:NV, q, :], net.hx[:, 4 * n + q, SEQ:SEQ + NV], ident)
                ins.then_inc(s_tp, 1)

        @block.scalar
        def _(act):
            norm.act(act)

        @block.vector
        def _(dve):
            dve.memset(net.hx[:, :, 0:1], 0.0).then_inc(s_zero, 1)
            norm.dve(dve)
            for n in range(2):
                dve.wait_ge(s_tp, n + 1)
                dve.tensor_copy(net.sprev[:, 4 * n:4 * n + 4, :], tp[n][:, :, 0:DEC]).then_inc(s_prev, 1)
            for n in range(2):
                dve.wait_ge(s_tp, n + 3)
                dve.tensor_copy(last[:, n * 512:(n + 1) * 512].rearrange("v (q c) -> v q c", q=4), tp[n][0:NV, :, :]).then_inc(s_last, 2)


class Mix:

    def __init__(self, net, ctx, tag, which):
        self.net, self.at = net, PARAM_AT["rw_mix"] + 8 * which
        sem = lambda name: net.semaphore(f"{tag}_{name}")
        self.buf = ctx.enter_context(net.nc.sbuf_tensor(f"{tag}_xm", [128, 2, TOK], F32))
        self.s_d, self.s_xm, self.s_hi, self.s_lo = sem("d"), sem("xm"), sem("hi"), sem("lo")

    def act(self, act):
        for b in range(DB):
            act.wait_ge(self.s_xm, b + 1)
            act.activation(self.net.HH[:, b, :], self.buf[:, b % 2, :], ACT.Copy).then_inc(self.s_hi, 1)

    def dve(self, dve):
        net = self.net

        def low(b):
            dve.wait_ge(self.s_hi, b + 1)
            dve.tensor_tensor(net.HL[:, b, :], self.buf[:, b % 2, :], net.HH[:, b, :].bitcast(F32), ALU.subtract).then_inc(self.s_lo, 1)

        for b in range(DB):
            d, h = self.buf[:, b % 2, :], net.hx[:, b, 1:1 + TOK]
            if b >= 2:
                dve.wait_ge(self.s_lo, b - 1)
            dve.tensor_tensor(d[:, 0:SEQ], net.hx[:, b, 0:SEQ], net.hx[:, b, 1:1 + SEQ], ALU.subtract).then_inc(self.s_d, 1)
            dve.tensor_tensor(d[:, SEQ:TOK], net.sprev[:, b, :], net.hx[:, b, 1 + SEQ:1 + TOK], ALU.subtract).then_inc(self.s_d, 1)
            dve.wait_ge(self.s_d, 2 * b + 2)
            dve.scalar_tensor_tensor(out=d, in0=d, scalar=net.param[:, self.at + b:self.at + b + 1], in1=h, op0=ALU.mult, op1=ALU.add).then_inc(self.s_xm, 1)
            if b >= 1:
                low(b - 1)
        low(DB - 1)


def stage_lora(net, which):
    nc, io = net.nc, net.io
    tag = f"lora_{which}"
    R = {"w": 64, "a": 64, "g": 128}[which]
    first, second = io[f"rw_{which}1"][0], io[f"rw_{which}2"][0]
    inner = {"w": ACT.Tanh, "a": ACT.Copy, "g": ACT.Sigmoid}[which]
    stores = 2 if which == "w" else 1
    with ExitStack() as ctx:
        def sb(name, shape, dt=F32):
            return ctx.enter_context(nc.sbuf_tensor(f"{tag}_{name}", shape, dt))

        def sem(name):
            return net.semaphore(f"{tag}_{name}")

        mix = Mix(net, ctx, tag, {"w": 1, "a": 4, "g": 5}[which])
        pan = Panels(net, ctx, tag, R)
        w2 = sb("w2", [R, D])
        low_rank = sb("inner", [R, TOK])
        out = sb("out", [128, 2, TOK])
        cum = sb("cum", [128, 2, TOK]) if which == "w" else None
        start = sb("start", [128, TOK]) if which == "w" else None
        ps = ctx.enter_context(nc.psum_tensor(f"{tag}_ps", [128, NT, 512], F32))
        s_w2, s_in, s_ps, s_ps_free = sem("w2"), sem("inner"), sem("ps"), sem("ps_free")
        s_out, s_dv, s_ready = sem("sig"), sem("dv"), sem("ready")
        s_stored = [sem("stored0"), sem("stored1")]
        block = ctx.enter_context(nc.Block())

        @block.sync
        def _(sp):
            pan.load(sp, 0, 0, first.rearrange("(k p) m -> p k m", p=128))
            sp.dma_start(w2[:], second).then_inc(s_w2, 16)
            if which == "w":
                sp.dma_start(start[:], io["const_wide"][:, 0:TOK]).then_inc(s_w2, 16)
            for b in range(DB):
                s = b % 2
                if which == "w":
                    sp.wait_ge(s_ready, b + 1)
                    sp.dma_start(net.sL[b], cum[:, s, :]).then_inc(s_stored[s], 16)
                    sp.dma_start(net.sLm[b], out[:, s, :]).then_inc(s_stored[s], 16)
                else:
                    sp.wait_ge(s_out, b * NT + NT)
                    sp.dma_start({"a": net.sA, "g": net.sG}[which][b], out[:, s, :]).then_inc(s_stored[s], 16)
            for s in range(2):
                sp.wait_ge(s_stored[s], 16 * stores * (DB // 2))

        @block.gpsimd
        def _(pool):
            pan.split(pool, 0, 0, 0)

        @block.tensor
        def _(pe):
            pan.multiply(pe, 0, 0, net.HH, net.HL, ready=(mix.s_lo, 1))
            pe.wait_ge(s_in, NT)
            pe.wait_ge(s_w2, 32 if which == "w" else 16)
            for b in range(DB):
                for n in range(NT):
                    if b:
                        pe.wait_ge(s_out, (b - 1) * NT + n + 1)
                    pe.matmul(ps[:, n, 0:TT], w2[:, b * 128:(b + 1) * 128], low_rank[:, n * TT:(n + 1) * TT], start=True, stop=True).then_inc(s_ps, 1)

        @block.scalar
        def _(act):
            mix.act(act)
            for n in range(NT):
                pan.summed(act, 0, n)
                act.activation(low_rank[:, n * TT:(n + 1) * TT], pan.acc[0:R, n, 0:TT], inner).then_inc(s_in, 1)
            for b in range(DB):
                if b >= 2:
                    act.wait_ge(s_stored[b % 2], 16 * stores * (b // 2))
                for n in range(NT):
                    act.wait_ge(s_ps, b * NT + n + 1)
                    o = out[:, b % 2, n * TT:(n + 1) * TT]
                    if which == "g":
                        act.activation(o, ps[:, n, 0:TT], ACT.Copy).then_inc(s_out, 1)
                    else:
                        at = PARAM_AT[f"rw_{which}0"] + b
                        act.activation(o, ps[:, n, 0:TT], ACT.Sigmoid, bias=net.param[:, at:at + 1]).then_inc(s_out, 1)

        @block.vector
        def _(dve):
            dve.sem_inc(pan.low, pan.LOW0)
            dve.sem_inc(pan.done, pan.DONE0)
            dve.sem_inc(pan.free, NT)
            mix.dve(dve)
            if which == "w":
                chain = Chain(dve, s_dv)
                dve.wait_ge(s_w2, 32)
                for b in range(DB):
                    o, L = out[:, b % 2, :], cum[:, b % 2, :]
                    dve.wait_ge(s_out, (b + 1) * NT)
                    if b >= 2:
                        dve.wait_ge(s_stored[b % 2], 16 * stores * (b // 2))
                    chain.link(dve.tensor_scalar(o, o, -DECAY_SCALE, None, ALU.mult))
                    chain.link(dve.tensor_tensor_scan(L, start[:], o, 0.0, ALU.mult, ALU.add))
                    dve.tensor_tensor(o, L, o, ALU.subtract).then_inc(s_ready, 1)


def stage_r(net):
    nc, io = net.nc, net.io
    with ExitStack() as ctx:
        def sb(name, shape, dt=F32):
            return ctx.enter_context(nc.sbuf_tensor(f"r_{name}", shape, dt))

        def sem(name):
            return net.semaphore(f"r_{name}")

        mix = Mix(net, ctx, "r", 0)
        pan = Panels(net, ctx, "rp")
        L, Rt = sb("L", [128, 2, TOK]), sb("Rt", [128, 2, TOK])
        s_L, s_P, s_Rt, s_st = [sem("L0"), sem("L1")], sem("P"), sem("Rt"), [sem("st0"), sem("st1")]
        block = ctx.enter_context(nc.Block())
        w = io["rw_wr"][0]

        @block.sync
        def _(sp):
            with sp.Fori(0, DB // 2) as j:
                for s in range(2):
                    pan.load(sp, j * 2 + s, s, panel_of(w, j * 256 + s * 128))
                    sp.wait_ge(s_Rt, j * 2 + s + 1)
                    sp.dma_start(L[:, s, :], row(net.sL, j * 2 + s)).then_inc(s_L[s], 16)

        @block.gpsimd
        def _(pool):
            with pool.Fori(0, DB // 2) as j:
                for s in range(2):
                    pan.split(pool, j * 2 + s, s, j)

        @block.tensor
        def _(pe):
            with pe.Fori(0, DB // 2) as j:
                for s in range(2):
                    pan.multiply(pe, j * 2 + s, s, net.HH, net.HL, ready=(mix.s_lo, 1))

        @block.scalar
        def _(act):
            mix.act(act)
            with act.Fori(0, DB // 2) as j:
                for s in range(2):
                    act.wait_ge(s_L[s], j * 16 + 16)
                    act.activation(L[:, s, :], L[:, s, :], ACT.Exp).then_inc(s_P, 1)
                    act.wait_ge(s_Rt, j * 2 + s + 3)
                    act.dma_start(row(net.sRt, j * 2 + s), Rt[:, s, :]).then_inc(s_st[s], 16)
            for s in range(2):
                act.wait_ge(s_st[s], 16 * (DB // 2) + 16)

        @block.vector
        def _(dve):
            dve.sem_inc(pan.low, pan.LOW0)
            dve.sem_inc(pan.done, pan.DONE0)
            dve.sem_inc(pan.free, NT)
            dve.sem_inc(s_Rt, 2)
            for s in range(2):
                dve.sem_inc(s_st[s], 16)
            mix.dve(dve)
            with dve.Fori(0, DB // 2) as j:
                for s in range(2):
                    dve.wait_ge(s_P, j * 2 + s + 1)
                    dve.wait_ge(s_st[s], j * 16 + 16)
                    for n in range(NT):
                        pan.summed(dve, j * 2 + s, n)
                        t = slice(n * TT, (n + 1) * TT)
                        ins = dve.tensor_tensor(Rt[:, s, t], pan.acc[:, n, 0:TT], L[:, s, t], ALU.mult)
                        ins.then_inc(pan.free, 1)
                    dve.wait_ge(pan.free, (j * 2 + s) * NT + 2 * NT)
                    dve.sem_inc(s_Rt, 1)


def stage_k(net):
    nc, io = net.nc, net.io
    with ExitStack() as ctx:
        def sb(name, shape, dt=F32):
            return ctx.enter_context(nc.sbuf_tensor(f"k_{name}", shape, dt))

        def sem(name):
            return net.semaphore(f"k_{name}")

        with ExitStack() as mctx:
            mix = Mix(net, mctx, "k", 2)
            block = mctx.enter_context(nc.Block())
            block.scalar(mix.act)
            block.vector(mix.dve)
        pan = Panels(net, ctx, "kp")
        A, L, Lm, Rt = (sb(n, [128, 2, TOK]) for n in ("a", "L", "Lm", "Rt"))
        k, inv, am, bs = (sb(n, [128, TOK]) for n in ("k", "inv", "am", "bs"))
        omka = sb("omka", [128, DB])
        ps = ctx.enter_context(nc.psum_tensor("k_ps", [128, NT, 512], F32))
        s_ld, s_st, s_bst = [sem("ld0"), sem("ld1")], [sem("st0"), sem("st1")], sem("bst")
        s_sq, s_exp, s_ln, s_inv, s_bsev = sem("sq"), sem("exp"), sem("ln"), sem("inv"), sem("bsev")
        s_m, s_out, s_bq, s_dv, s_ssr = sem("max"), sem("out"), sem("bonus"), sem("dv"), sem("ss_read")
        s_ss, s_bsum = sem("ss"), sem("bsum")
        w = io["rw_wk"][0]
        headsum = c_(net, "headsum")
        DV = 8
        block = ctx.enter_context(nc.Block())

        def col(name, b):
            at = PARAM_AT[name]
            return net.param[:, bass.ds(b + at, 1)]

        def around(eng, body):
            body(0, 0, 0)
            with eng.Fori(0, 3) as i:
                body(i * 2 + 1, 1, i)
                body(i * 2 + 2, 0, i + 1)
            body(7, 1, 3)

        @block.sync
        def _(sp):
            def body(b, s, i):
                pan.load(sp, b, s, panel_of(w, b * 128))
                sp.wait_ge(s_out, b + 1)
                sp.wait_ge(s_st[s], i * 48 + 48)
                for buf, src in ((A, net.sA), (L, net.sL), (Lm, net.sLm), (Rt, net.sRt)):
                    sp.dma_start(buf[:, s, :], row(src, b)).then_inc(s_ld[s], 16)
            around(sp, body)

        @block.gpsimd
        def _(pool):
            with pool.Fori(0, DB // 2) as j:
                for s in range(2):
                    pan.split(pool, j * 2 + s, s, j)

        @block.tensor
        def _(pe):
            def bonus(b):
                pe.wait_ge(s_bq, b + 1)
                pe.wait_ge(s_ssr, b + 1)
                for n in range(NT):
                    ins = pe.matmul(ps[:, n, 0:TT], headsum, inv[:, n * TT:(n + 1) * TT], start=True, stop=True)
                ins.then_inc(s_bsum, 1)

            def squares(b):
                pe.wait_ge(s_bsev, b + 1)
                for n in range(NT):
                    pe.wait_ge(s_sq, b * NT + n + 1)
                    ins = pe.matmul(ps[:, n, 0:TT], headsum, inv[:, n * TT:(n + 1) * TT], start=True, stop=True)
                ins.then_inc(s_ss, 1)

            def body(b, s, i):
                pan.multiply(pe, b, s, net.HH, net.HL)
                if not (isinstance(b, int) and b == 0):
                    bonus(b - 1)
                squares(b)
            around(pe, body)
            bonus(7)

        @block.scalar
        def _(act):
            def bonus_out(b):
                act.wait_ge(s_bsum, b + 1)
                act.wait_ge(s_bst, b * 16 + 16)
                act.activation(tiles(bs[:]), ps[:, :, 0:TT], ACT.Copy).then_inc(s_bsev, 1)
                act.wait_ge(s_bsev, b + 2)
                act.dma_start(row(net.sBS, b), bs[:]).then_inc(s_bst, 16)

            def body(b, s, i):
                first = isinstance(b, int) and b == 0
                for n in range(NT):
                    t = slice(n * TT, (n + 1) * TT)
                    pan.summed(act, b, n)
                    if n == 0:
                        act.wait_ge(s_out, b + 2)
                    act.activation(k[:, t], pan.acc[:, n, 0:TT], ACT.Copy).then_inc(pan.free, 1)
                if not first:
                    bonus_out(b - 1)
                act.wait_ge(pan.free, b * NT + 2 * NT)
                for n in range(NT):
                    t = slice(n * TT, (n + 1) * TT)
                    act.activation(inv[:, t], k[:, t], ACT.Square, scale=col("rw_kk", b)).then_inc(s_sq, 1)
                act.wait_ge(s_ld[s], i * 64 + 64)
                act.activation(blk(net.pend, b), L[:, s, C - 1:SEQ:C], ACT.Exp).then_inc(s_exp, 1)
                act.activation(blk(net.Ps, b), L[:, s, SEQ:TOK], ACT.Exp).then_inc(s_exp, 1)
                act.wait_ge(s_exp, b * 4 + 2)
                act.activation(L[:, s, :], L[:, s, :], ACT.Exp, scale=-1.0).then_inc(s_exp, 1)
                act.activation(Lm[:, s, :], Lm[:, s, :], ACT.Exp).then_inc(s_exp, 1)
                act.wait_ge(s_m, b + 1)
                act.activation(inv[:], inv[:], ACT.Ln).then_inc(s_ln, 1)
                act.wait_ge(s_ln, b + 1)
                act.activation(inv[:], inv[:], ACT.Exp, scale=-0.5).then_inc(s_inv, 1)
                act.wait_ge(s_out, b + 3)
                for dst, src in ((net.sAt, Lm[:, s, :]), (net.sBt, A[:, s, :]), (net.sKt, am[:])):
                    act.dma_start(row(dst, b), src).then_inc(s_st[s], 16)
            around(act, body)
            bonus_out(7)
            for s in range(2):
                act.wait_ge(s_st[s], 5 * 48)
            act.wait_ge(s_bst, 16 * DB + 16)

        @block.vector
        def _(dve):
            dve.sem_inc(pan.low, pan.LOW0)
            dve.sem_inc(pan.done, pan.DONE0)
            dve.sem_inc(pan.free, NT)
            dve.sem_inc(s_out, 2)
            dve.sem_inc(s_bsev, 1)
            dve.sem_inc(s_bst, 16)
            for s in range(2):
                dve.sem_inc(s_st[s], 48)
            ka = net.param[:, PARAM_AT["rw_ka"]:PARAM_AT["rw_ka"] + DB]
            dve.tensor_scalar(omka[:], ka, -1.0, 1.0, ALU.mult, ALU.add).then_inc(s_dv, 1)

            def body(b, s, i):
                ch = Chain(dve, s_dv, DV, b, 1)
                a, e2, e1 = A[:, s, :], L[:, s, :], Lm[:, s, :]
                dve.wait_ge(s_ss, b + 1)
                dve.tensor_scalar(tiles(inv[:]), ps[:, :, 0:TT], 1e-24, float(2 ** 20), ALU.max, ALU.mult).then_inc(s_m, 1)
                dve.wait_ge(s_m, b + 1)
                dve.wait_ge(s_ld[s], i * 64 + 64)
                dve.wait_ge(s_st[1 - s], (i + s) * 48 + 48)
                ch.link(dve.tensor_scalar(am[:], a, col("rw_ka", b), omka[:, bass.ds(b, 1)], ALU.mult, ALU.add))
                ch.link(dve.tensor_tensor(am[:], am[:], k[:], ALU.mult))
                ch.link(dve.tensor_scalar(k[:], k[:], col("rw_kk", b), 1024.0, ALU.mult, ALU.mult))
                dve.wait_ge(s_inv, b + 1)
                ch.link(dve.tensor_tensor(k[:], k[:], inv[:], ALU.mult))
                dve.sem_inc(s_ssr, 1)
                dve.wait_ge(s_exp, b * 4 + 4)
                ch.link(dve.tensor_tensor(a, a, k[:], ALU.mult))
                ch.link(dve.tensor_tensor(am[:], am[:], e2, ALU.mult))
                ch.link(dve.tensor_tensor(a, a, e2, ALU.mult))
                dve.scalar_tensor_tensor(out=inv[:], in0=Rt[:, s, :], scalar=col("rw_rk", b), in1=am[:], op0=ALU.mult, op1=ALU.mult).then_inc(s_bq, 1)
                ch.link(dve.scalar_tensor_tensor(out=e1, in0=k[:], scalar=-1.0, in1=e1, op0=ALU.mult, op1=ALU.mult))
                dve.wait_ge(s_bq, b + 1)
                dve.sem_inc(s_out, 1)
                assert ch.n == DV
            around(dve, body)


def stage_products(net):
    nc, io = net.nc, net.io
    with ExitStack() as ctx:
        def sb(name, shape, dt=F32):
            return ctx.enter_context(nc.sbuf_tensor(f"g_{name}", shape, dt))

        def sem(name):
            return net.semaphore(f"g_{name}")

        AR = sb("AR", [128, 2, NCH, 2, C])
        BK = sb("BK", [128, 2, 2, NCH, 128])
        G = sb("G", [128, NCH, 4, C])
        T = sb("T", [128, NCH, 2, C])
        banks_g = [ctx.enter_context(nc.psum_tensor(f"g_bank{i}", [128, 4, 128], F32)) for i in range(4)]
        banks_t = [ctx.enter_context(nc.psum_tensor(f"g_tbank{i}", [128, 4, 128], F32)) for i in range(4)]
        s_zero, s_ld = sem("zero"), [sem("ld0"), sem("ld1")]
        s_g, s_gev, s_t, s_tev, s_gst, s_tst = sem("g"), sem("gev"), sem("t"), sem("tev"), sem("gst"), sem("tst")
        ident = c_(net, "ident")
        at = CONST_AT["lt"]
        lt_le = net.const[:, at:at + 128].unsqueeze(1).to_broadcast([128, 4, 128])
        NG = NCH // 2
        block = ctx.enter_context(nc.Block())

        @block.sync
        def _(sp):
            sp.wait_ge(s_zero, 2)
            with sp.Fori(0, DB // 2) as j:
                for s in range(2):
                    b = j * 2 + s
                    sp.wait_ge(s_g, (b + 1) * NG)
                    sp.wait_ge(s_t, (b + 1) * NG)
                    for i, src in enumerate((net.sAt, net.sRt)):
                        sp.dma_start(AR[:, s, :, i, :], row(src, b)[:, 0:SEQ].rearrange("p (c t) -> p c t", t=C)).then_inc(s_ld[s], 16)
                    for i, src in enumerate((net.sBt, net.sKt)):
                        for h in range(2):
                            r = slice(64 * h, 64 * h + 64)
                            sp.dma_start(BK[r, s, i, :, r], row(src, b)[r, 0:SEQ].rearrange("p (c t) -> p c t", t=C)).then_inc(s_ld[s], 16)

        @block.tensor
        def _(pe):
            with pe.Fori(0, DB // 2) as j:
                for s in range(2):
                    b = j * 2 + s
                    pe.wait_ge(s_ld[s], j * 96 + 96)
                    for q in range(NG):
                        bank = banks_g[q % 4]
                        pe.wait_ge(s_gev, b * NG + q + 1)
                        for c in range(2):
                            for i in range(2):
                                ins = pe.matmul(bank[:, 2 * c + i, :], BK[:, s, i, 2 * q + c, :], AR[:, s, 2 * q + c].rearrange("p a t -> p (a t)"), start=True, stop=True)
                        ins.then_inc(s_g, 1)
                        bank = banks_t[q % 4]
                        pe.wait_ge(s_tev, b * NG * 2 + q * 2 + 2)
                        for c in range(2):
                            for i in range(2):
                                ins = pe.transpose(bank[:, 2 * c + i, :], BK[:, s, i, 2 * q + c, :], ident)
                        ins.then_inc(s_t, 1)

        @block.scalar
        def _(act):
            with act.Fori(0, DB) as b:
                act.wait_ge(s_tst, b * 16 + 16)
                for q in range(NG):
                    act.wait_ge(s_t, b * NG + q + 1 + 2 * NG)
                    for h in range(2):
                        r = slice(64 * h, 64 * h + 64)
                        act.activation(T[r, 2 * q:2 * q + 2].rearrange("p c i t -> p (c i) t"), banks_t[q % 4][r, :, r], ACT.Copy).then_inc(s_tev, 1)
                act.wait_ge(s_tev, (b + 1) * 2 * NG + 8)
                act.dma_start(net.sBK[:, :, bass.ds(b, 1)].rearrange("c p a i t -> p c (a i t)"), T[:].rearrange("p c i t -> p c (i t)")).then_inc(s_tst, 16)
                act.wait_ge(s_gev, (b + 1) * NG + 4)
                act.dma_start(net.sM[:, bass.ds(b, 1)].rearrange("c a p t -> p c (a t)"), G[:, :, 0, :]).then_inc(s_gst, 16)
                act.dma_start(net.sG3[:, :, bass.ds(b, 1)].rearrange("c p a i t -> p c (a i t)"), G[:, :, 1:4, :].rearrange("p c i t -> p c (i t)")).then_inc(s_gst, 16)
            act.wait_ge(s_tst, DB * 16 + 16)
            act.wait_ge(s_gst, DB * 32 + 32)

        @block.vector
        def _(dve):
            dve.memset(BK[:, 0], 0.0).then_inc(s_zero, 1)
            dve.memset(BK[:, 1], 0.0).then_inc(s_zero, 1)
            dve.sem_inc(s_g, 2 * NG)
            dve.sem_inc(s_t, 2 * NG)
            dve.sem_inc(s_gev, 4)
            dve.sem_inc(s_tev, 8)
            dve.sem_inc(s_gst, 32)
            dve.sem_inc(s_tst, 16)
            with dve.Fori(0, DB) as b:
                dve.wait_ge(s_gst, b * 32 + 32)
                for q in range(NG):
                    dve.wait_ge(s_g, b * NG + q + 1 + 2 * NG)
                    dve.tensor_tensor(G[:, 2 * q:2 * q + 2].rearrange("p c (i a) t -> p (c i) (a t)", a=2), banks_g[q % 4][:], lt_le, ALU.mult).then_inc(s_gev, 1)


def around(eng, body):
    body(0, 0, 0)
    with eng.Fori(0, DB // 2 - 1) as i:
        body(i * 2 + 1, 1, i)
        body(i * 2 + 2, 0, i + 1)
    body(DB - 1, 1, DB // 2 - 1)


def stage_v(net):
    nc, io = net.nc, net.io
    with ExitStack() as ctx:
        def sb(name, shape, dt=F32):
            return ctx.enter_context(nc.sbuf_tensor(f"v_{name}", shape, dt))

        def sem(name):
            return net.semaphore(f"v_{name}")

        with ExitStack() as mctx:
            mix = Mix(net, mctx, "v", 3)
            block = mctx.enter_context(nc.Block())
            block.scalar(mix.act)
            block.vector(mix.dve)
        pan = Panels(net, ctx, "vp")
        v, bs = sb("v", [128, 2, TOK]), sb("bs", [128, 2, TOK])
        tok, stok = sb("tok", [128, 2, 4, 128]), sb("stok", [DEC, 128])
        Z, tmp = sb("Z", [128, 2, C * C]), sb("tmp", [128, 2, 1024])
        tb = [ctx.enter_context(nc.psum_tensor(f"v_tb{i}", [128, 4, 128], F32)) for i in range(3)]
        s_bs, s_v, s_bv, s_bvst = [sem("bs0"), sem("bs1")], sem("v"), sem("bv"), [sem("bvst0"), sem("bvst1")]
        s_t, s_tev, s_vst, s_M, s_z, s_diag, s_zst = sem("t"), sem("tev"), sem("vst"), sem("M"), sem("z"), sem("diag"), sem("zst")
        ident = c_(net, "ident")
        w = io["rw_wv"][0]
        half = NCH // 2
        systems = lambda t: t.rearrange("(g c) b (r s) t -> g (c b r) (s t)", g=2, r=2)
        block = ctx.enter_context(nc.Block())

        @block.sync
        def _(sp):
            for g in range(2):
                sp.dma_start(Z[:, g, :], systems(net.sM)[g]).then_inc(s_M, 16)
            with sp.Fori(0, DB // 2) as j:
                for s in range(2):
                    b = j * 2 + s
                    pan.load(sp, b, s, panel_of(w, b * 128))
                    sp.wait_ge(s_bvst[s], j * 16 + 16)
                    sp.dma_start(bs[:, s, :], row(net.sBS, b)).then_inc(s_bs[s], 16)
            for g in range(2):
                sp.wait_ge(s_z, 4 * (C - 2) - 1 + g)
                sp.wait_ge(s_diag, 1)
                sp.dma_start(systems(net.sT)[g], Z[:, g, :]).then_inc(s_zst, 16)
            sp.wait_ge(s_zst, 32)

        @block.gpsimd
        def _(pool):
            def product(b, s, i):
                pool.wait_ge(s_v, b * NT + NT)
                pool.wait_ge(s_bs[s], i * 16 + 16)
                pool.tensor_tensor(bs[:, s, :], bs[:, s, :], v[:, s, :], ALU.mult).then_inc(s_bv, 1)

            def body(b, s, i):
                pan.split(pool, b, s, i)
                if not (isinstance(b, int) and b == 0):
                    product(b - 1, 1 - s, i + s - 1)
            around(pool, body)
            product(DB - 1, 1, DB // 2 - 1)

        @block.tensor
        def _(pe):
            def turn(b, s):
                pe.wait_ge(s_v, b * NT + NT)
                for h in range(2):
                    pe.wait_ge(s_tev, b * 3 + h + 1)
                    for q in range(4):
                        t = (4 * h + q) * 128
                        ins = pe.transpose(tb[h][:, q, :], v[:, s, t:t + 128], ident)
                    ins.then_inc(s_t, 1)
                pe.wait_ge(s_tev, b * 3 + 3)
                pe.transpose(tb[2][0:DEC, 0, :], v[:, s, SEQ:TOK], ident).then_inc(s_t, 1)

            def body(b, s, i):
                pan.multiply(pe, b, s, net.HH, net.HL)
                if not (isinstance(b, int) and b == 0):
                    turn(b - 1, 1 - s)
            around(pe, body)
            turn(DB - 1, 1)

        @block.scalar
        def _(act):
            def out(b):
                act.wait_ge(s_vst, b * 48 + 48)
                for h in range(2):
                    act.wait_ge(s_t, b * 3 + h + 1)
                    act.activation(tok[:, h], tb[h][:], ACT.Copy).then_inc(s_tev, 1)
                act.wait_ge(s_t, b * 3 + 3)
                act.activation(stok[:], tb[2][0:DEC, 0, :], ACT.Copy).then_inc(s_tev, 1)
                act.wait_ge(s_tev, b * 3 + 6)
                cols = net.sV[:, bass.ds(b * 128, 128)]
                for h in range(2):
                    act.dma_start(cols[512 * h:512 * h + 512].rearrange("(q p) c -> p q c", p=128), tok[:, h]).then_inc(s_vst, 16)
                act.dma_start(cols[SEQ:TOK], stok[:]).then_inc(s_vst, 16)

            def product_out(b, s):
                act.wait_ge(s_bv, b + 1)
                act.dma_start(row(net.sBV, b), bs[:, s, :]).then_inc(s_bvst[s], 16)

            def body(b, s, i):
                if not (isinstance(b, int) and b < 2):
                    act.wait_ge(s_bv, b - 1)
                    act.wait_ge(s_t, b * 3 - 3)
                for n in range(NT):
                    t = slice(n * TT, (n + 1) * TT)
                    pan.summed(act, b, n)
                    act.activation(v[:, s, t], pan.acc[:, n, 0:TT], ACT.Copy).then_inc(s_v, 1)
                act.wait_ge(s_v, b * NT + NT)
                act.sem_inc(pan.free, NT)
                if not (isinstance(b, int) and b == 0):
                    out(b - 1)
                    product_out(b - 1, 1 - s)
            body(0, 0, 0)
            body(1, 1, 0)
            with act.Fori(1, DB // 2) as i:
                body(i * 2, 0, i)
                body(i * 2 + 1, 1, i)
            out(DB - 1)
            product_out(DB - 1, 1)
            act.wait_ge(s_vst, DB * 48 + 48)
            for s in range(2):
                act.wait_ge(s_bvst[s], 16 * (DB // 2) + 16)

        @block.vector
        def _(dve):
            dve.sem_inc(pan.low, pan.LOW0)
            dve.sem_inc(pan.done, pan.DONE0)
            dve.sem_inc(pan.free, NT)
            dve.sem_inc(s_tev, 3)
            dve.sem_inc(s_vst, 48)
            for s in range(2):
                dve.sem_inc(s_bvst[s], 16)
            dve.wait_ge(s_M, 32)
            n = 0
            for s in range(1, C - 1):
                for g in range(2):
                    z = Z[:, g, :].rearrange("p (u t) -> p u t", t=C)
                    if n >= 2:
                        dve.wait_ge(s_z, n - 1)
                    shape = [128, s, C - 1 - s]
                    p = tmp[:, g, 0:s * (C - 1 - s)].rearrange("p (u t) -> p u t", u=s)
                    dve.tensor_tensor(p, z[:, 0:s, s:s + 1].to_broadcast(shape), z[:, s:s + 1, s + 1:C].to_broadcast(shape), ALU.mult).then_inc(s_z, 1)
                    n += 1
                for g in range(2):
                    z = Z[:, g, :].rearrange("p (u t) -> p u t", t=C)
                    shape = [128, s, C - 1 - s]
                    p = tmp[:, g, 0:s * (C - 1 - s)].rearrange("p (u t) -> p u t", u=s)
                    dve.wait_ge(s_z, n - 1)
                    dve.tensor_tensor(z[:, 0:s, s + 1:C], z[:, 0:s, s + 1:C], p, ALU.add).then_inc(s_z, 1)
                    n += 1
            dve.memset(Z[:, :, 0:C * C:C + 1], 1.0).then_inc(s_diag, 1)


def stage_samples(net):
    nc, io = net.nc, net.io
    with ExitStack() as ctx:
        def sb(name, shape, dt=F32):
            return ctx.enter_context(nc.sbuf_tensor(f"step_{name}", shape, dt))

        def sem(name):
            return net.semaphore(f"step_{name}")

        cols = sb("cols", [128, 4, DB, DEC])
        rows = sb("rows", [DEC, 5, D])
        vec = sb("vec", [128, 6, HD])
        S, tmp = sb("S", [128, HD, HD]), sb("tmp", [128, HD, HD])
        sa, y = sb("sa", [128, HD]), sb("y", [128, HD])
        tb = [ctx.enter_context(nc.psum_tensor(f"step_tb{i}", [128, 4, 128], F32)) for i in range(2)]
        s_in, s_S, s_t, s_tev, s_rows, s_vec, s_dv, s_out = sem("in"), sem("S"), sem("t"), sem("tev"), sem("rows"), sem("vec"), sem("dv"), sem("out")
        ident = c_(net, "ident")
        block = ctx.enter_context(nc.Block())

        @block.sync
        def _(sp):
            for i, src in enumerate((net.sAt, net.sRt, net.sBt, net.sKt)):
                sp.dma_start(cols[:, i], src[:, :, SEQ:TOK].rearrange("b p t -> p b t")).then_inc(s_in, 16)
            sp.dma_start(S[:], io["state_wkv"][0].rearrange("s h i j -> (s h) i j")).then_inc(s_S, 16)
            sp.dma_start(vec[:, 5, :], net.sV[SEQ:TOK].rearrange("s (h d) -> (s h) d", d=HD)).then_inc(s_vec, 16)
            sp.wait_ge(s_tev, 10)
            sp.dma_start(net.sSmp[0:5].rearrange("i s c -> s i c"), rows[:]).then_inc(s_rows, 16)
            sp.wait_ge(s_rows, 16)
            for i in range(5):
                sp.dma_start(vec[:, i, :], net.sSmp[i].rearrange("s (h d) -> (s h) d", d=HD)).then_inc(s_vec, 16)
            sp.wait_ge(s_dv, 12)
            sp.dma_start(io["out_wkv_sample"][0].rearrange("s h i j -> (s h) i j"), S[:]).then_inc(s_out, 16)
            sp.dma_start(net.sY[SEQ:TOK].rearrange("s (h d) -> (s h) d", d=HD), y[:]).then_inc(s_out, 16)
            sp.wait_ge(s_out, 32)

        @block.tensor
        def _(pe):
            pe.wait_ge(s_in, 64)
            for n in range(10):
                i, h = n // 2, n % 2
                if n >= 2:
                    pe.wait_ge(s_tev, n - 1)
                for q in range(4):
                    src = cols[:, i, 4 * h + q, :] if i < 4 else net.Ps[:, 4 * h + q, :]
                    ins = pe.transpose(tb[n % 2][0:DEC, q, :], src, ident)
                ins.then_inc(s_t, 1)

        @block.scalar
        def _(act):
            for n in range(10):
                act.wait_ge(s_t, n + 1)
                act.activation(rows[:, n // 2, (n % 2) * 512:(n % 2) * 512 + 512].rearrange("s (q c) -> s q c", q=4), tb[n % 2][0:DEC], ACT.Copy).then_inc(s_tev, 1)

        @block.vector
        def _(dve):
            ch = Chain(dve, s_dv)
            At, Rt, Bt, Kt, P, V = (vec[:, i, :] for i in range(6))
            shape = [128, HD, HD]
            along_j = lambda x: x.unsqueeze(1).to_broadcast(shape)
            along_i = lambda x: x.unsqueeze(2).to_broadcast(shape)
            dve.wait_ge(s_S, 16)
            dve.wait_ge(s_vec, 96)
            ch.link(dve.tensor_tensor(tmp[:], S[:], along_j(At), ALU.mult))
            ch.link(dve.tensor_reduce(sa[:], tmp[:], AX, ALU.add))
            ch.link(dve.tensor_tensor(tmp[:], along_i(sa[:]), along_j(Bt), ALU.mult))
            ch.link(dve.tensor_tensor(S[:], S[:], tmp[:], ALU.add))
            ch.link(dve.tensor_tensor(tmp[:], along_i(V), along_j(Kt), ALU.mult))
            ch.link(dve.tensor_tensor(S[:], S[:], tmp[:], ALU.add))
            ch.link(dve.tensor_tensor(tmp[:], S[:], along_j(Rt), ALU.mult))
            ch.link(dve.tensor_reduce(y[:], tmp[:], AX, ALU.add))
            ch.link(dve.tensor_tensor(S[:], S[:], along_j(P), ALU.mult))
            dve.sem_inc(s_dv, 3)


def stage_scan(net):
    nc, io = net.nc, net.io
    Q = DB // 2
    with ExitStack() as ctx:
        def sb(name, shape, dt=F32):
            return ctx.enter_context(nc.sbuf_tensor(f"c_{name}", shape, dt))

        def sem(name):
            return net.semaphore(f"c_{name}")

        At, Rt = sb("At", [128, 2, DB, C]), sb("Rt", [128, 2, DB, C])
        G3 = sb("G3", [128, 2, DB, 3, C])
        Z = sb("Z", [128, 2, DB, C])
        BK = sb("BK", [128, 2, DB, 2, C])
        V = sb("V", [128, 2, DB, 128])
        S, U, SA = sb("S", [128, DB, 128]), sb("U", [128, DB, 128]), sb("SA", [128, DB, 128])
        Y = sb("Y", [128, 2, Q, 128])
        St = sb("St", [128, DB, 128])
        pU, pSA, pD, pY = ([ctx.enter_context(nc.psum_tensor(f"c_p{n}{i}", [128, Q, 128], F32)) for i in range(2)] for n in "UADY")
        s_zero, s_ld = sem("zero"), [sem("ld0"), sem("ld1")]
        s_U, s_SA, s_D, s_Y = sem("U"), sem("SA"), sem("D"), sem("Y")
        s_Ua, s_Ud, s_Sa, s_Sd, s_S, s_dv = sem("Ua"), sem("Ud"), sem("Sa"), sem("Sd"), sem("S"), sem("dv")
        s_Yev, s_yst = sem("Yev"), [sem("yst0"), sem("yst1")]
        s_T, s_Tev, s_out = sem("T"), sem("Tev"), sem("out")
        ident = c_(net, "ident")
        block = ctx.enter_context(nc.Block())

        @block.sync
        def _(sp):
            sp.wait_ge(s_zero, 5)
            with sp.Fori(0, NCH // 2) as i:
                for s in range(2):
                    c = i * 2 + s
                    sp.wait_ge(s_Y, c + 1)
                    t = bass.ds(c * C, C)
                    sp.dma_start(At[:, s], net.sAt[:, :, t].rearrange("b p t -> p b t")).then_inc(s_ld[s], 16)
                    sp.dma_start(Rt[:, s], net.sRt[:, :, t].rearrange("b p t -> p b t")).then_inc(s_ld[s], 16)
                    sp.dma_start(G3[:, s], net.sG3[bass.ds(c, 1)].rearrange("c p b i t -> p (c b) i t")).then_inc(s_ld[s], 16)
                    sp.dma_start(Z[:, s], net.sT[bass.ds(c, 1)].rearrange("c b p t -> p (c b) t")).then_inc(s_ld[s], 16)
                    sp.dma_start(BK[:, s], net.sBK[bass.ds(c, 1)].rearrange("c p b i t -> p (c b) i t")).then_inc(s_ld[s], 16)
                    rows = net.sV[t].rearrange("t (b h d) -> h t b d", h=2, d=HD)
                    for h in range(2):
                        r = slice(64 * h, 64 * h + 64)
                        sp.dma_start(V[r, s, :, r], rows[h]).then_inc(s_ld[s], 16)

        @block.tensor
        def _(pe):
            def mm(out, b, lhsT, rhs, start, stop):
                h = b % 2
                return pe.matmul(out[64 * h:64 * h + 64, b // 2, :], lhsT, rhs, start=start, stop=stop, skip_group_check=True, tile_position=(0, 64 * h))

            def chunk(c, s, i):
                pe.wait_ge(s_ld[s], i * 112 + 112)
                pe.wait_ge(s_S, c + 1)
                pe.wait_ge(s_Ua, c + 1)
                pe.wait_ge(s_Ud, c + 1)
                for b in range(DB):
                    mm(pU[s], b, At[:, s, b, :], S[:, b, :], b < 2, False)
                    ins = mm(pU[s], b, G3[:, s, b, 1, :], V[:, s, b, :], False, True)
                ins.then_inc(s_U, 1)
                pe.wait_ge(s_Yev, c + 1)
                for b in range(DB):
                    mm(pY[s], b, Rt[:, s, b, :], S[:, b, :], b < 2, False)
                    mm(pY[s], b, G3[:, s, b, 2, :], V[:, s, b, :], False, False)
                pe.wait_ge(s_Ua, c + 3)
                pe.wait_ge(s_Ud, c + 3)
                for b in range(DB):
                    ins = mm(pSA[s], b, Z[:, s, b, :], U[:, b, :], b < 2, True)
                ins.then_inc(s_SA, 1)
                for b in range(DB):
                    mm(pD[s], b, BK[:, s, b, 1, :], V[:, s, b, :], b < 2, False)
                pe.wait_ge(s_Sa, c + 3)
                pe.wait_ge(s_Sd, c + 3)
                for b in range(DB):
                    ins = mm(pD[s], b, BK[:, s, b, 0, :], SA[:, b, :], False, True)
                ins.then_inc(s_D, 1)
                for b in range(DB):
                    ins = mm(pY[s], b, G3[:, s, b, 0, :], SA[:, b, :], False, True)
                ins.then_inc(s_Y, 1)

            with pe.Fori(0, NCH // 2) as i:
                for s in range(2):
                    chunk(i * 2 + s, s, i)
            pe.wait_ge(s_S, NCH + 1)
            for n in range(2):
                for q in range(4):
                    ins = pe.transpose(pU[n][:, q, :], S[:, 4 * n + q, :], ident)
                ins.then_inc(s_T, 1)

        def halves(h, out, src):
            for a in range(2):
                r = slice(64 * a, 64 * a + 64)
                yield out[r, h::2, r], src[64 * h:64 * h + 64, :, r]

        @block.scalar
        def _(act):
            with act.Fori(0, NCH // 2) as i:
                for s in range(2):
                    c = i * 2 + s
                    act.wait_ge(s_U, c + 1)
                    act.wait_ge(s_SA, c + 2)
                    for n, (o, p) in enumerate(halves(0, U, pU[s])):
                        ins = act.activation(o, p, ACT.Copy)
                    ins.then_inc(s_Ua, 1)
                    act.wait_ge(s_SA, c + 3)
                    act.wait_ge(s_Y, c + 2)
                    for n, (o, p) in enumerate(halves(0, SA, pSA[s])):
                        ins = act.activation(o, p, ACT.Copy)
                    ins.then_inc(s_Sa, 1)
                    act.wait_ge(s_Y, c + 3)
                    act.wait_ge(s_yst[s], i * 32 + 32)
                    act.activation(Y[:, s], pY[s][:], ACT.Copy).then_inc(s_Yev, 1)
                    act.wait_ge(s_Yev, c + 3)
                    rows = net.sY[bass.ds(c * C, C)].rearrange("t (q h d) -> h t q d", h=2, d=128)
                    for h in range(2):
                        act.dma_start(rows[h], Y[64 * h:64 * h + 64, s]).then_inc(s_yst[s], 16)
            for n in range(2):
                act.wait_ge(s_T, n + 1)
                act.activation(St[:, 4 * n:4 * n + 4, :], pU[n][:], ACT.Copy).then_inc(s_Tev, 1)
            act.wait_ge(s_Tev, 2)
            for h in range(2):
                r = slice(64 * h, 64 * h + 64)
                act.dma_start(io["out_wkv_prompt"][0, 0].rearrange("(b h) i j -> h i b j", h=2)[h], St[r, :, r]).then_inc(s_out, 16)
            for s in range(2):
                act.wait_ge(s_yst[s], NCH // 2 * 32 + 32)
            act.wait_ge(s_out, 32)

        @block.vector
        def _(dve):
            for buf in (V[:, 0], V[:, 1], U[:], SA[:], S[:]):
                dve.memset(buf, 0.0).then_inc(s_zero, 1)
            dve.wait_ge(s_zero, 5)
            dve.sem_inc(s_S, 1)
            dve.sem_inc(s_Y, 2)
            dve.sem_inc(s_SA, 2)
            dve.sem_inc(s_Yev, 2)
            for x in (s_Ua, s_Ud, s_Sa, s_Sd):
                dve.sem_inc(x, 2)
            for s in range(2):
                dve.sem_inc(s_yst[s], 32)
            with dve.Fori(0, NCH // 2) as i:
                for s in range(2):
                    c = i * 2 + s
                    dve.wait_ge(s_U, c + 1)
                    dve.wait_ge(s_SA, c + 2)
                    for o, p in halves(1, U, pU[s]):
                        ins = dve.tensor_copy(o, p)
                    ins.then_inc(s_Ud, 1)
                    dve.wait_ge(s_SA, c + 3)
                    dve.wait_ge(s_Y, c + 2)
                    for o, p in halves(1, SA, pSA[s]):
                        ins = dve.tensor_copy(o, p)
                    ins.then_inc(s_Sd, 1)
                    dve.wait_ge(s_D, c + 1)
                    for h in range(2):
                        for o, p in halves(h, S, pD[s]):
                            ins = dve.tensor_tensor(o, p, o, ALU.add)
                            ins.then_inc(s_dv, 1)
                    dve.wait_ge(s_dv, c * 4 + 4)
                    decay = net.pend[:, :, bass.ds(c, 1)].to_broadcast([128, DB, 128])
                    dve.tensor_tensor(S[:], S[:], decay, ALU.mult).then_inc(s_S, 1)




class Project:

    def __init__(self, net, ctx, tag, w, gate):
        self.net, self.w, self.gate = net, w, gate
        self.pan = Panels(net, ctx, tag)
        self.smp = ctx.enter_context(net.nc.sbuf_tensor(f"{tag}_smp", [128, DEC], F32))
        self.s_smp = net.semaphore(f"{tag}_smp")

    def sp(self, sp):
        with sp.Fori(0, DB // 2) as j:
            for s in range(2):
                self.load(sp, j, s)

    def load(self, sp, j, s):
        self.pan.load(sp, j * 2 + s, s, panel_of(self.w, j * 256 + s * 128))

    def pool(self, pool):
        with pool.Fori(0, DB // 2) as j:
            for s in range(2):
                self.pan.split(pool, j * 2 + s, s, j)

    def pe(self, pe, ready=None):
        with pe.Fori(0, DB // 2) as j:
            for s in range(2):
                self.pan.multiply(pe, j * 2 + s, s, self.net.HH, self.net.HL, ready=ready)

    def dve_start(self, dve):
        dve.sem_inc(self.pan.low, self.pan.LOW0)
        dve.sem_inc(self.pan.done, self.pan.DONE0)
        dve.sem_inc(self.pan.free, NT)

    def dve(self, dve):
        with dve.Fori(0, DB // 2) as j:
            for s in range(2):
                m = j * 2 + s
                add_gated(dve, self.net, self.pan, m, m, self.gate, self.smp[:], self.pan.free, self.s_smp, m)


def stage_rwkv_out(net):
    nc, io = net.nc, net.io
    with ExitStack() as ctx:
        def sb(name, shape, dt=F32):
            return ctx.enter_context(nc.sbuf_tensor(f"o_{name}", shape, dt))

        def sem(name):
            return net.semaphore(f"o_{name}")

        proj = Project(net, ctx, "op", io["rw_wo"][0], mod_part(net, 0, 2))
        rows, sq = sb("rows", [128, 2, D]), sb("sq", [128, D])
        mean, var = sb("mean", [128, HEADS]), sb("var", [128, HEADS])
        yc = sb("yc", [128, DB, TOK])
        bv, g = sb("bv", [128, 2, TOK]), sb("g", [128, 2, TOK])
        tb = [ctx.enter_context(nc.psum_tensor(f"o_tb{i}", [128, 4, 128], F32)) for i in range(4)]
        s_x, s_y, s_root, s_n, s_t, s_tev = sem("x"), [sem("y0"), sem("y1")], sem("root"), sem("n"), sem("t"), sem("tev")
        s_var, s_dv = sem("var"), sem("dv")
        s_bg, s_aff, s_u, s_hi, s_lo = [sem("bg0"), sem("bg1")], sem("aff"), sem("u"), sem("hi"), sem("lo")
        ident = c_(net, "ident")
        TILES = SEQ // 128
        LINKS = 7
        block = ctx.enter_context(nc.Block())

        def over_tiles(eng, body):
            with eng.Fori(0, TILES // 2) as i:
                for s in range(2):
                    body(i * 2 + s, s, i, 128)
            body(TILES, 0, TILES // 2, DEC)

        @block.sync
        def _(sp):
            def load(t, s, i, n):
                sp.wait_ge(s_t, t * 2 + 2)
                sp.dma_start(rows[0:n, s, :], net.sY[bass.ds(t * 128, n)]).then_inc(s_y[s], 16)
            over_tiles(sp, load)
            sp.dma_start(net.X[:], net.x_saved).then_inc(s_x, 16)
            for s in range(2):
                proj.load(sp, 0, s)
            with sp.Fori(0, DB // 2) as j:
                for s in range(2):
                    sp.wait_ge(s_lo, j * 2 + s + 1)
                    sp.dma_start(bv[:, s, :], row(net.sBV, j * 2 + s)).then_inc(s_bg[s], 16)
                    sp.dma_start(g[:, s, :], row(net.sG, j * 2 + s)).then_inc(s_bg[s], 16)
            with sp.Fori(1, DB // 2) as j:
                for s in range(2):
                    proj.load(sp, j, s)

        @block.gpsimd
        def _(pool):
            proj.pool(pool)

        @block.tensor
        def _(pe):
            pe.sem_inc(s_t, 4)

            def turn(t, s, i, n):
                pe.wait_ge(s_n, t + 1)
                pe.wait_ge(s_tev, t * 2 + 1)
                pe.wait_ge(s_tev, t * 2 + 2)
                for h in range(2):
                    for q in range(4):
                        b = 4 * h + q
                        ins = pe.transpose(tb[2 * s + h][:, q, 0:n], rows[0:n, s, b * 128:(b + 1) * 128], ident[0:n, 0:n])
                    ins.then_inc(s_t, 1)
            over_tiles(pe, turn)
            proj.pe(pe, ready=(s_lo, 3))

        @block.scalar
        def _(act):
            act.sem_inc(s_tev, 4)

            def body(t, s, i, n):
                act.wait_ge(s_var, t + 1)
                act.activation(var[0:n], var[0:n], ACT.Sqrt).then_inc(s_root, 1)
                for h in range(2):
                    act.wait_ge(s_t, t * 2 + h + 5)
                    act.activation(yc[:, 4 * h:4 * h + 4, bass.ds(t * 128, n)], tb[2 * s + h][:, :, 0:n], ACT.Copy).then_inc(s_tev, 1)
            over_tiles(act, body)
            act.wait_ge(s_tev, 4 + 2 * (TILES + 1))
            with act.Fori(0, DB) as b:
                y = blk(yc, b)
                gain, shift = (net.param[:, bass.ds(b + PARAM_AT[n], 1)] for n in ("rw_lnx_g", "rw_lnx_b"))
                act.activation(y, y, ACT.Identity, bias=shift, scale=gain).then_inc(s_aff, 1)
            with act.Fori(0, DB) as b:
                act.wait_ge(s_u, b * 2 + 2)
                act.activation(blk(net.HH, b), blk(yc, b), ACT.Copy).then_inc(s_hi, 1)

        @block.vector
        def _(dve):
            proj.dve_start(dve)
            dve.sem_inc(s_lo, 2)

            def body(t, s, i, n):
                ch = Chain(dve, s_dv, LINKS, t)
                y = rows[0:n, s, :].rearrange("p (h d) -> p h d", d=HD)
                q = sq[0:n].rearrange("p (h d) -> p h d", d=HD)
                m, v = mean[0:n], var[0:n]
                bc = lambda x: x.unsqueeze(2).to_broadcast([n, HEADS, HD])
                dve.wait_ge(s_y[s], i * 16 + 16)
                ch.link(dve.tensor_reduce(m, y, AX, ALU.add))
                ch.link(dve.tensor_scalar(m, m, 1.0 / HD, None, ALU.mult))
                ch.link(dve.tensor_tensor(y, y, bc(m), ALU.subtract))
                ch.link(dve.tensor_tensor(q, y, y, ALU.mult))
                ch.link(dve.tensor_reduce(v, q, AX, ALU.add))
                dve.tensor_scalar(v, v, 1.0 / HD, LNX_EPS, ALU.mult, ALU.add).then_inc(s_var, 1)
                dve.wait_ge(s_root, t + 1)
                ch.link(dve.reciprocal(v, v))
                ch.link(dve.tensor_tensor(y, y, bc(v), ALU.mult))
                dve.sem_inc(s_n, 1)
                assert ch.n == LINKS

            over_tiles(dve, body)
            with dve.Fori(0, DB // 2) as j:
                for s in range(2):
                    b = j * 2 + s
                    y = blk(yc, b)
                    dve.wait_ge(s_aff, b + 1)
                    dve.wait_ge(s_bg[s], j * 32 + 32)
                    dve.tensor_tensor(y, y, bv[:, s, :], ALU.add).then_inc(s_u, 1)
                    dve.wait_ge(s_u, b * 2 + 1)
                    dve.tensor_tensor(y, y, g[:, s, :], ALU.mult).then_inc(s_u, 1)
                    dve.wait_ge(s_u, b * 2 + 2)
                    dve.wait_ge(s_hi, b + 1)
                    dve.tensor_tensor(blk(net.HL, b), y, blk(net.HH, b).bitcast(F32), ALU.subtract).then_inc(s_lo, 1)
            dve.wait_ge(s_x, 16)
            proj.dve(dve)




def stage_qkv(net):
    nc, io = net.nc, net.io
    with ExitStack() as nctx:
        norm = Norm(net, nctx, "qn", net.gain[:, 2], mod_part(net, 1, 0))
        block = nctx.enter_context(nc.Block())
        block.tensor(norm.pe)
        block.scalar(norm.act)
        block.vector(norm.dve)
    with ExitStack() as ctx:
        def sb(name, shape, dt=F32):
            return ctx.enter_context(nc.sbuf_tensor(f"q_{name}", shape, dt))

        def sem(name):
            return net.semaphore(f"q_{name}")

        weights(net, ctx, "q")
        pan = Panels(net, ctx, "qp")
        cos, sin = sb("cos", [128, TOK]), sb("sin", [128, TOK])
        kv = sb("kv", [128, 2, TOK])
        tmp = sb("tmp", [128, 2, TT])
        ps = ctx.enter_context(nc.psum_tensor("q_ps", [128, NT, 512], F32))
        tb = [ctx.enter_context(nc.psum_tensor(f"q_tb{i}", [128, 4, 128], F32)) for i in range(2)]
        s_ang, s_x, s_t, s_tev, s_sw, s_rot, s_dv, s_kd = sem("ang"), sem("x"), sem("t"), sem("tev"), sem("sw"), sem("rot"), sem("dv"), sem("kd")
        s_vd = sem("vd")
        ident, swap = c_(net, "ident"), c_(net, "swap")
        w = io["at_wqkv"][0]
        NQ = HEADS * HD
        KVW = KV * HD
        v_at, k_at = NQ + KVW, NQ
        block = ctx.enter_context(nc.Block())

        @block.sync
        def _(sp):
            for p in range(2):
                pan.load(sp, p, p, panel_of(w, v_at + p * 128))
            sp.dma_start(cos[:], io["const_wide"][:, TOK:2 * TOK]).then_inc(s_ang, 16)
            sp.dma_start(sin[:], io["const_wide"][:, 2 * TOK:3 * TOK]).then_inc(s_ang, 16)
            for p in range(2):
                pan.load(sp, 2 + p, p, panel_of(w, k_at + p * 128))
            with sp.Fori(0, DB // 2) as j:
                for s in range(2):
                    pan.load(sp, j * 2 + s + 4, s, panel_of(w, j * 256 + s * 128))

        @block.gpsimd
        def _(pool):
            with pool.Fori(0, DB // 2 + 2) as j:
                for s in range(2):
                    pan.split(pool, j * 2 + s, s, j)

        @block.tensor
        def _(pe):
            def turn(v):
                pe.wait_ge(s_x, v * NT + NT)
                for n in range(3):
                    pe.wait_ge(s_tev, 3 * v + n + 1)
                    for q in range(4 if n < 2 else 1):
                        cols, t = (128, (4 * n + q) * 128) if n < 2 else (DEC, SEQ)
                        ins = pe.transpose(tb[(3 * v + n) % 2][0:cols, q, :], kv[:, v, t:t + cols], ident)
                    ins.then_inc(s_t, 1)

            def partners(p, x):
                pe.wait_ge(s_x, p * NT + NT)
                for n in range(NT):
                    pe.wait_ge(s_dv, ((p - 3) * NT + n) * 3 + 2 + 3 * NT)
                    ins = pe.matmul(ps[:, n, 0:TT], swap, x[:, n * TT:(n + 1) * TT], start=True, stop=True)
                    ins.then_inc(s_sw, 1)

            pan.multiply(pe, 0, 0, net.HH, net.HL)
            pan.multiply(pe, 1, 1, net.HH, net.HL)
            turn(0)
            pan.multiply(pe, 2, 0, net.HH, net.HL)
            turn(1)
            pan.multiply(pe, 3, 1, net.HH, net.HL)
            partners(2, kv[:, 0, :])

            def body(b, s, i):
                pan.multiply(pe, b + 4, s, net.HH, net.HL)
                if isinstance(b, int) and b == 0:
                    partners(3, kv[:, 1, :])
                else:
                    partners(b + 3, blk(net.Q, b - 1))
            around(pe, body)
            partners(DB + 3, net.Q[:, DB - 1, :])

        @block.scalar
        def _(act):
            def add_bias(p, x, at):
                for n in range(NT):
                    pan.summed(act, p, n)
                    act.activation(x[:, n * TT:(n + 1) * TT], pan.acc[:, n, 0:TT], ACT.Identity, bias=net.param[:, bass.ds(at, 1)]).then_inc(s_x, 1)
                act.wait_ge(s_x, p * NT + NT)
                act.sem_inc(pan.free, NT)

            at = PARAM_AT["at_bqkv"]
            for v in range(2):
                add_bias(v, kv[:, v, :], at + v_at // 128 + v)
            for v in range(2):
                for n in range(3):
                    act.wait_ge(s_t, 3 * v + n + 1)
                    bank, cols = tb[(3 * v + n) % 2], slice(v * 128, (v + 1) * 128)
                    if n < 2:
                        act.activation(net.Vt[:, 4 * n:4 * n + 4, cols], bank[:], ACT.Copy).then_inc(s_tev, 1)
                    else:
                        act.activation(net.Vt[0:DEC, 2 * 4, cols], bank[0:DEC, 0, :], ACT.Copy).then_inc(s_tev, 1)
                act.wait_ge(s_vd, v * 4 + 4)
                add_bias(2 + v, kv[:, v, :], at + k_at // 128 + v)
            with act.Fori(0, DB) as b:
                add_bias(b + 4, blk(net.Q, b), b + at)

        @block.vector
        def _(dve):
            dve.sem_inc(pan.low, pan.LOW0)
            dve.sem_inc(pan.done, pan.DONE0)
            dve.sem_inc(pan.free, NT)
            dve.sem_inc(s_tev, 2)
            dve.sem_inc(s_dv, 3 * NT)
            for v in range(2):
                dve.wait_ge(s_x, v * NT + NT)
                for h in range(2):
                    for a in range(2):
                        dve.tensor_copy(net.Vd[64 * a:64 * a + 64, 2 * v + h, :], kv[64 * h:64 * h + 64, v, SEQ:TOK]).then_inc(s_vd, 1)
            dve.wait_ge(s_ang, 32)

            def rotate(p, x):
                dve.wait_ge(s_x, p * NT + NT)
                for n in range(NT):
                    t = slice(n * TT, (n + 1) * TT)
                    base = ((p - 2) * NT + n) * 3 + 3 * NT
                    dve.wait_ge(s_sw, (p - 2) * NT + n + 1)
                    dve.wait_ge(s_dv, base)
                    dve.tensor_tensor(tmp[:, n % 2, :], ps[:, n, 0:TT], sin[:, t], ALU.mult).then_inc(s_dv, 1)
                    dve.tensor_tensor(x[:, t], x[:, t], cos[:, t], ALU.mult).then_inc(s_dv, 1)
                    dve.wait_ge(s_dv, base + 2)
                    dve.tensor_tensor(x[:, t], x[:, t], tmp[:, n % 2, :], ALU.add).then_inc(s_dv, 1)

            for k in range(2):
                rotate(2 + k, kv[:, k, :])
                dve.wait_ge(s_dv, (k + 1) * 3 * NT + 3 * NT)
                for h in range(2):
                    for a in range(2):
                        dve.tensor_copy(net.Kd[64 * a:64 * a + 64, 2 * k + h, :], kv[64 * h:64 * h + 64, k, :]).then_inc(s_kd, 1)
            with dve.Fori(0, DB) as b:
                rotate(b + 4, blk(net.Q, b))
            dve.wait_ge(s_dv, 11 * 3 * NT)
            dve.wait_ge(s_kd, 8)


def stage_attend_samples(net):
    nc, io = net.nc, net.io
    with ExitStack() as ctx:
        def sb(name, shape, dt=F32):
            return ctx.enter_context(nc.sbuf_tensor(f"as_{name}", shape, dt))

        def sem(name):
            return net.semaphore(f"as_{name}")

        ck, cv = (sb(n, [WIN, DEC, KV, 2, HD]) for n in ("ck", "cv"))
        KT = sb("KT", [128, 2, KV, WIN])
        qd, pd = sb("qd", [128, DEC, DB, 2]), sb("pd", [128, DEC, DB, 2])
        ST, PT = sb("ST", [WIN, 128]), sb("PT", [WIN, 128])
        R = sb("R", [128, WIN + 1])
        mx, nm, es, den = (sb(n, [128, 1]) for n in ("mx", "nm", "es", "den"))
        sink = sb("sink", [128, 1])
        diag, o, o2 = sb("diag", [128, 128]), sb("o", [128, DEC, DB, 2]), sb("o2", [128, DB, DEC])
        krow, ksrow = sb("krow", [WIN, KV, HD]), sb("ksrow", [DEC, KV, HD])
        tb = [ctx.enter_context(nc.psum_tensor(f"as_tb{i}", [128, 4, 128], F32)) for i in range(2)]
        pST, pR, pB, pO, pK, pKs = (ctx.enter_context(nc.psum_tensor(f"as_p{i}", [128, 512], F32)) for i in range(6))
        s_ck, s_cv, s_sink, s_zero, s_out = sem("ck"), sem("cv"), sem("sink"), sem("zero"), sem("out")
        s_t, s_tev, s_q, s_ST, s_STev, s_R, s_dv = sem("t"), sem("tev"), sem("q"), sem("ST"), sem("STev"), sem("R"), sem("dv")
        s_e, s_P, s_PT, s_PTev, s_O, s_k, s_kev = sem("e"), sem("P"), sem("PT"), sem("PTev"), sem("O"), sem("k"), sem("kev")
        s_hi = sem("hi")
        ident, ones = c_(net, "ident"), c_(net, "ones")
        LAST = SEQ // 128 - 1
        block = ctx.enter_context(nc.Block())

        @block.sync
        def _(sp):
            for buf, name, sm in ((ck, "cache_k", s_ck), (cv, "cache_v", s_cv)):
                src = io[name][0].rearrange("s w k d -> w s k d")
                for h in range(2):
                    for s in range(DEC):
                        sp.dma_start(buf[:, s, :, h, :], src[:, s]).then_inc(sm, 16)
            for name in ("k", "v"):
                sp.dma_start(io[f"out_{name}_sample"][0, :, 0:WIN - 1].rearrange("s w k d -> s (w k d)"), io[f"cache_{name}"][0, :, 1:WIN].rearrange("s w k d -> s (w k d)")).then_inc(s_out, 16)
            sp.dma_start(io["out_v_sample"][0, :, WIN - 1].rearrange("s k d -> s (k d)"), net.Vt[0:DEC, LAST + 1, :]).then_inc(s_out, 16)
            sp.dma_start(io["out_v_prompt"][0, 0].rearrange("w k d -> w (k d)"), net.Vt[:, LAST, :]).then_inc(s_out, 16)
            sp.wait_ge(s_kev, 2)
            sp.dma_start(io["out_k_prompt"][0, 0], krow[:]).then_inc(s_out, 16)
            sp.dma_start(io["out_k_sample"][0, :, WIN - 1], ksrow[:]).then_inc(s_out, 16)
            sp.wait_ge(s_out, 96)

        @block.tensor
        def _(pe):
            for k in range(KV):
                ins = pe.transpose(pK[:, k * HD:(k + 1) * HD], net.Kd[0:64, k, LAST * 128:SEQ], ident[0:64, 0:64])
            ins.then_inc(s_k, 1)
            for k in range(KV):
                ins = pe.transpose(pKs[0:DEC, k * HD:(k + 1) * HD], net.Kd[0:64, k, SEQ:TOK], ident[0:64, 0:64])
            ins.then_inc(s_k, 1)
            pe.wait_ge(s_q, 4)
            pe.wait_ge(s_ck, 2 * DEC * 16)

            def turn(s):
                if s >= 2:
                    pe.wait_ge(s_tev, s - 1)
                for k in range(KV):
                    ins = pe.transpose(tb[s % 2][:, k, :], ck[:, s, k].rearrange("w a d -> w (a d)"), ident)
                ins.then_inc(s_t, 1)

            turn(0)
            for s in range(DEC):
                if s + 1 < DEC:
                    turn(s + 1)
                pe.wait_ge(s_tev, s + 1)
                for k in range(KV):
                    at = s * HEADS + 4 * k
                    ins = pe.matmul(pST[:, at:at + 4], KT[:, s % 2, k, :], qd[:, s, 2 * k:2 * k + 2, :].rearrange("p b a -> p (b a)"), start=True, stop=True, skip_group_check=True)
                ins.then_inc(s_ST, 1)
            pe.wait_ge(s_STev, 1)
            pe.matmul(pR[:, WIN:WIN + 1], pd[:].rearrange("p s b a -> p (s b a)"), ones[:, 0:1], start=True, stop=True)
            pe.transpose(pR[:, 0:WIN], ST[:], ident).then_inc(s_R, 1)
            pe.wait_ge(s_P, 2)
            pe.matmul(pB[:, 0:128], ones, diag[:], start=True, stop=True)
            pe.transpose(pST[:, 128:256], R[:, 0:WIN], ident).then_inc(s_PT, 1)
            pe.wait_ge(s_PTev, 1)
            pe.wait_ge(s_cv, 2 * DEC * 16)
            for s in range(DEC):
                for k in range(KV):
                    at = s * HEADS + 4 * k
                    ins = pe.matmul(pO[:, at:at + 4], cv[:, s, k].rearrange("w a d -> w (a d)"), PT[:, at:at + 4], start=True, stop=True, skip_group_check=True)
            ins.then_inc(s_O, 1)

        @block.scalar
        def _(act):
            for s in range(DEC):
                act.dma_start(sink[s * HEADS:(s + 1) * HEADS, :], io["at_sink"].rearrange("a h -> h a")).then_inc(s_sink, 16)
            act.wait_ge(s_k, 1)
            act.activation(krow[:].rearrange("w k d -> w (k d)"), pK[:, 0:KV * HD], ACT.Copy).then_inc(s_kev, 1)
            act.wait_ge(s_k, 2)
            act.activation(ksrow[:].rearrange("w k d -> w (k d)"), pKs[0:DEC, 0:KV * HD], ACT.Copy).then_inc(s_kev, 1)
            for s in range(DEC):
                act.wait_ge(s_t, s + 1)
                if s >= 2:
                    act.wait_ge(s_ST, s - 1)
                act.activation(KT[:, s % 2], tb[s % 2][:], ACT.Copy).then_inc(s_tev, 1)
            act.wait_ge(s_ST, DEC)
            act.activation(ST[:], pST[:, 0:128], ACT.Copy).then_inc(s_STev, 1)
            act.wait_ge(s_dv, 5)
            act.activation(R[:], R[:], ACT.Exp, bias=nm[:], accum_out=den[:]).then_inc(s_e, 1)
            act.activation(es[:], sink[:], ACT.Exp, bias=nm[:]).then_inc(s_e, 1)
            act.wait_ge(s_PT, 1)
            act.activation(PT[:], pST[:, 128:256], ACT.Copy).then_inc(s_PTev, 1)
            act.wait_ge(s_dv, 11)
            act.activation(net.HH[:, :, SEQ:TOK], o2[:], ACT.Copy).then_inc(s_hi, 1)

        @block.vector
        def _(dve):
            ch = Chain(dve, s_dv)
            dve.memset(qd[:], 0.0).then_inc(s_zero, 1)
            dve.memset(pd[:], 0.0).then_inc(s_zero, 1)
            dve.wait_ge(s_zero, 2)
            for a in range(2):
                r = slice(64 * a, 64 * a + 64)
                q = net.Q[r, :, SEQ:TOK].rearrange("p b s -> p s b")
                dve.tensor_copy(qd[r, :, :, a], q).then_inc(s_q, 1)
                dve.tensor_tensor(pd[r].rearrange("p s (k j) a -> p s k j a", j=2)[:, :, :, :, a], q.rearrange("p s (k j) -> p s k j", j=2),
                                  net.Kd[r, :, SEQ:TOK].rearrange("p k s -> p s k").unsqueeze(3).to_broadcast([64, DEC, KV, 2]), ALU.mult).then_inc(s_q, 1)
            dve.wait_ge(s_R, 1)
            ch.link(dve.tensor_scalar(R[:], pR[:, 0:WIN + 1], SCALE, None, ALU.mult))
            ch.link(dve.tensor_reduce(mx[:], R[:], AX, ALU.max))
            dve.wait_ge(s_sink, DEC * 16)
            ch.link(dve.tensor_tensor(mx[:], mx[:], sink[:], ALU.max))
            ch.link(dve.tensor_scalar(nm[:], mx[:], -1.0, None, ALU.mult))
            dve.sem_inc(s_dv, 1)
            ch.n += 1
            dve.wait_ge(s_e, 2)
            ch.link(dve.tensor_tensor(den[:], den[:], es[:], ALU.add))
            ch.link(dve.reciprocal(den[:], den[:]))
            dve.tensor_scalar(R[:], R[:], den[:], None, ALU.mult).then_inc(s_P, 1)
            dve.wait_ge(s_P, 1)
            dve.tensor_scalar(diag[:], ident, R[:, WIN:WIN + 1], None, ALU.mult).then_inc(s_P, 1)
            dve.wait_ge(s_O, 1)
            new = net.Vd[:].rearrange("p k s -> p s k").unsqueeze(3).to_broadcast([128, DEC, KV, 4])
            ch.link(dve.tensor_tensor(o[:].rearrange("p s (k j) a -> p s k (j a)", j=2), pB[:, 0:128].rearrange("p (s k g) -> p s k g", k=KV, g=4), new, ALU.mult))
            flat = o[:].rearrange("p s b a -> p (s b a)")
            ch.link(dve.tensor_tensor(flat, flat, pO[:, 0:128], ALU.add))
            for a in range(2):
                r = slice(64 * a, 64 * a + 64)
                ch.link(dve.tensor_copy(o2[r], o[r, :, :, a].rearrange("p s b -> p b s")))
            assert ch.n == 11
            dve.wait_ge(s_hi, 1)
            dve.tensor_tensor(net.HL[:, :, SEQ:TOK], o2[:], net.HH[:, :, SEQ:TOK].bitcast(F32), ALU.subtract).then_inc(s_q, 1)
            dve.wait_ge(s_q, 5)


def stage_attend(net):
    nc, io = net.nc, net.io
    TILES = SEQ // 128
    with ExitStack() as ctx:
        def sb(name, shape, dt=F32):
            return ctx.enter_context(nc.sbuf_tensor(f"at_{name}", shape, dt))

        def sem(name):
            return net.semaphore(f"at_{name}")

        mask, sink = sb("mask", [128, 256]), sb("sink", [128, HEADS])
        S = sb("S", [128, 2, 4, 256])
        PT = sb("PT", [128, 4, 2, 128])
        Qs, Vs = sb("Qs", [128, 2, 4, 128]), sb("Vs", [128, 2, 2, HD])
        mx, nm, es, den = (sb(n, [128, 2, 4]) for n in ("mx", "nm", "es", "den"))
        pS = [ctx.enter_context(nc.psum_tensor(f"at_pS{i}", [128, 4, 256], F32)) for i in range(2)]
        pT = ctx.enter_context(nc.psum_tensor("at_pT", [128, 4, 2, 128], F32))
        pO = [ctx.enter_context(nc.psum_tensor(f"at_pO{i}", [128, 2, 128], F32, )) for i in range(2)]
        s_qs, s_vs, s_zero = sem("qs"), sem("vs"), sem("zero")
        s_in, s_s, s_sev, s_nm, s_e, s_P = sem("in"), sem("s"), sem("sev"), sem("nm"), sem("e"), sem("P")
        s_t, s_tev, s_o, s_hi, s_lo, s_dv, s_dv2 = sem("t"), sem("tev"), sem("o"), sem("hi"), sem("lo"), sem("dv"), sem("dv2")
        ident = c_(net, "ident")
        block = ctx.enter_context(nc.Block())

        def steps(eng, work):
            def tile(t, k):
                def at(d):
                    t2, k2 = t + (k + d) // KV, (k + d) % KV
                    return None if isinstance(t, int) and not 0 <= t2 < TILES else (t2, k2)
                work(t, k, at)
            for t in (0, 1):
                for k in range(KV):
                    tile(t, k)
            with eng.Fori(2, TILES - 1) as t:
                for k in range(KV):
                    tile(t, k)
            for k in range(KV):
                tile(TILES - 1, k)

        def keys(t):
            return (1, 0) if isinstance(t, int) and t == 0 else (2, t - 1)

        @block.sync
        def _(sp):
            sp.dma_start(mask[:], io["const_mask"]).then_inc(s_in, 16)
            sp.dma_start(sink[:], io["at_sink"].to_broadcast([128, HEADS])).then_inc(s_in, 16)

        @block.gpsimd
        def _(pool):
            def queries(t, k):
                if not (isinstance(t, int) and t == 0 and k < 2):
                    pool.wait_ge(s_s, t * KV + k - 1)
                for a in range(2):
                    r = slice(64 * a, 64 * a + 64)
                    pool.tensor_copy(Qs[r, k % 2, a::2], net.Q[r, 2 * k:2 * k + 2, bass.ds(t * 128, 128)]).then_inc(s_qs, 1)
                    pool.wait_ge(s_qs, (t * KV + k) * 2 + a + 1)

            pool.memset(Qs[:], 0.0).then_inc(s_zero, 1)
            pool.wait_ge(s_zero, 1)
            queries(0, 0)
            queries(0, 1)

            def work(t, k, at):
                if at(2):
                    queries(*at(2))
                n, first = keys(t)
                if not (isinstance(t, int) and t == 0 and k < 2):
                    pool.wait_ge(s_o, t * KV + k)
                pool.tensor_copy(Vs[:, k % 2, 0:n], net.Vt[:, bass.ds(first, n), k * HD:(k + 1) * HD]).then_inc(s_vs, 1)
            steps(pool, work)

        @block.tensor
        def _(pe):
            def scores(t, k):
                n, first = keys(t)
                s = k % 2
                pe.wait_ge(s_sev, t * KV + k + 1)
                pe.wait_ge(s_qs, (t * KV + k) * 2 + 2)
                for g in range(4):
                    ins = pe.matmul(pS[s][:, g, 0:n * 128], Qs[:, s, g, :], net.Kd[:, k, bass.ds(first * 128, n * 128)], start=True, stop=True, skip_group_check=True)
                ins.then_inc(s_s, 1)

            def turn(t, k):
                n, first = keys(t)
                pe.wait_ge(s_P, t * KV + k + 1)
                pe.wait_ge(s_tev, t * KV + k + 1)
                for g in range(4):
                    for j in range(n):
                        ins = pe.transpose(pT[:, g, j, :], S[:, k % 2, g, j * 128:(j + 1) * 128], ident)
                ins.then_inc(s_t, 1)

            def values(t, k):
                n, first = keys(t)
                pe.wait_ge(s_tev, t * KV + k + 2)
                pe.wait_ge(s_vs, t * KV + k + 1)
                pe.wait_ge(s_lo, t * KV + k + 1)
                for g in range(4):
                    a = g % 2
                    for j in range(n):
                        ins = pe.matmul(pO[k % 2][64 * a:64 * a + 64, g // 2, :], Vs[:, k % 2, j, :], PT[:, g, j, :], start=(j == 0), stop=(j == n - 1), skip_group_check=True, tile_position=(0, 64 * a))
                ins.then_inc(s_o, 1)

            scores(0, 0)
            scores(0, 1)

            def work(t, k, at):
                if at(2):
                    scores(*at(2))
                if at(-1):
                    values(*at(-1))
                turn(t, k)
            steps(pe, work)
            values(TILES - 1, KV - 1)

        @block.scalar
        def _(act):
            def exps(t, k):
                n, first = keys(t)
                s = k % 2
                act.wait_ge(s_nm, (t * KV + k) * 2 + 2)
                for g in range(4):
                    x = S[:, s, g, 0:n * 128]
                    ins = act.activation(x, x, ACT.Exp, bias=nm[:, s, g:g + 1], accum_out=den[:, s, g:g + 1])
                ins.then_inc(s_e, 1)
                act.activation(es[:, s], es[:, s], ACT.Exp).then_inc(s_e, 1)

            def turned(t, k):
                n, first = keys(t)
                act.wait_ge(s_t, t * KV + k + 1)
                act.wait_ge(s_o, t * KV + k + 1)
                act.activation(PT[:, :, 0:n, :], pT[:, :, 0:n, :], ACT.Copy).then_inc(s_tev, 1)

            def high(t, k):
                act.wait_ge(s_o, t * KV + k + 2)
                act.activation(net.HH[:, 2 * k:2 * k + 2, bass.ds(t * 128, 128)], pO[k % 2][:], ACT.Copy).then_inc(s_hi, 1)

            exps(0, 0)

            def work(t, k, at):
                if at(1):
                    exps(*at(1))
                turned(t, k)
                if at(-1):
                    high(*at(-1))
            steps(act, work)
            high(TILES - 1, KV - 1)

        @block.vector
        def _(dve):
            dve.sem_inc(s_sev, 2)
            dve.sem_inc(s_tev, 1)
            dve.sem_inc(s_lo, 2)
            dve.sem_inc(s_o, 1)
            dve.wait_ge(s_in, 32)

            def masked(t, k):
                n, first = keys(t)
                s = k % 2
                u = t * KV + k
                m = mask[:, 256 - n * 128:256].unsqueeze(1).to_broadcast([128, 4, n * 128])
                dve.wait_ge(s_s, u + 1)
                if not (isinstance(t, int) and t == 0 and k < 2):
                    dve.wait_ge(s_t, u - 1)
                dve.scalar_tensor_tensor(out=S[:, s, :, 0:n * 128], in0=pS[s][:, :, 0:n * 128], scalar=SCALE, in1=m, op0=ALU.mult, op1=ALU.add).then_inc(s_sev, 1)
                dve.wait_ge(s_sev, u + 3)
                dve.tensor_reduce(mx[:, s], S[:, s, :, 0:n * 128], AX, ALU.max).then_inc(s_dv, 1)
                dve.wait_ge(s_dv, u * 2 + 1)
                dve.tensor_tensor(mx[:, s], mx[:, s], sink[:, 4 * k:4 * k + 4], ALU.max).then_inc(s_dv, 1)
                dve.wait_ge(s_dv, u * 2 + 2)
                dve.tensor_scalar(nm[:, s], mx[:, s], -1.0, None, ALU.mult).then_inc(s_nm, 1)
                dve.tensor_tensor(es[:, s], sink[:, 4 * k:4 * k + 4], mx[:, s], ALU.subtract).then_inc(s_nm, 1)

            def normal(t, k):
                n, first = keys(t)
                s = k % 2
                u = t * KV + k
                dve.wait_ge(s_e, u * 2 + 2)
                dve.tensor_tensor(den[:, s], den[:, s], es[:, s], ALU.add).then_inc(s_dv2, 1)
                dve.wait_ge(s_dv2, u * 2 + 1)
                dve.reciprocal(den[:, s], den[:, s]).then_inc(s_dv2, 1)
                dve.wait_ge(s_dv2, u * 2 + 2)
                x = S[:, s, :, 0:n * 128]
                dve.tensor_tensor(x, x, den[:, s].unsqueeze(2).to_broadcast([128, 4, n * 128]), ALU.mult).then_inc(s_P, 1)

            def low(t, k):
                dve.wait_ge(s_hi, t * KV + k + 1)
                o = lambda x: x[:, 2 * k:2 * k + 2, bass.ds(t * 128, 128)]
                dve.tensor_tensor(o(net.HL), pO[k % 2][:], o(net.HH).bitcast(F32), ALU.subtract).then_inc(s_lo, 1)

            masked(0, 0)

            def work(t, k, at):
                if at(1):
                    masked(*at(1))
                normal(t, k)
                if at(-2):
                    low(*at(-2))
            steps(dve, work)
            low(TILES - 1, KV - 2)
            low(TILES - 1, KV - 1)
            dve.wait_ge(s_lo, TILES * KV + 2)


def stage_attend_out(net):
    nc, io = net.nc, net.io
    with ExitStack() as ctx:
        weights(net, ctx, "ao")
        proj = Project(net, ctx, "aop", io["at_wo"][0], mod_part(net, 1, 2))
        block = ctx.enter_context(nc.Block())
        block.sync(proj.sp)
        block.gpsimd(proj.pool)
        block.tensor(proj.pe)

        @block.vector
        def _(dve):
            proj.dve_start(dve)
            proj.dve(dve)


def stage_final(net):
    nc, io = net.nc, net.io
    with ExitStack() as ctx:
        y = ctx.enter_context(nc.sbuf_tensor("f_y", [128, DB, TOK], F32))
        rows = ctx.enter_context(nc.sbuf_tensor("f_rows", [128, 2, D], F32))
        zero = ctx.enter_context(nc.sbuf_tensor("f_zero", [128, DB, NV], F32))
        norm = Norm(net, ctx, "fn", net.gain[:, 4], zero[:], keep=y, split=False)
        tb = [ctx.enter_context(nc.psum_tensor(f"f_tb{i}", [128, 4, 128], F32)) for i in range(4)]
        s_zero, s_t, s_tev, s_out = net.semaphore("f_zero"), net.semaphore("f_t"), net.semaphore("f_tev"), [net.semaphore("f_out0"), net.semaphore("f_out1")]
        ident = c_(net, "ident")
        TILES = SEQ // 128
        block = ctx.enter_context(nc.Block())

        def over_tiles(eng, body):
            with eng.Fori(0, TILES // 2) as i:
                for s in range(2):
                    body(i * 2 + s, s, i, 128)
            body(TILES, 0, TILES // 2, DEC)

        @block.sync
        def _(sp):
            def out(t, s, i, n):
                sp.wait_ge(s_tev, t * 2 + 6)
                if n == DEC:
                    sp.dma_start(io["out_y_sample"].rearrange("b o d -> (b o) d"), rows[0:DEC, s, :]).then_inc(s_out[s], 16)
                else:
                    sp.dma_start(io["out_y_prompt"][0, bass.ds(t * 128, 128)], rows[:, s, :]).then_inc(s_out[s], 16)
            over_tiles(sp, out)
            sp.wait_ge(s_out[0], (TILES // 2 + 1) * 16 + 16)
            sp.wait_ge(s_out[1], TILES // 2 * 16 + 16)

        @block.tensor
        def _(pe):
            norm.pe(pe)
            pe.wait_ge(norm.s_h, DB)
            pe.wait_ge(norm.s_smp, DB)

            def turn(t, s, i, n):
                for h in range(2):
                    pe.wait_ge(s_tev, t * 2 + h + 1)
                    for q in range(4):
                        ins = pe.transpose(tb[2 * s + h][0:n, q, :], y[:, 4 * h + q, t * 128:t * 128 + n], ident)
                    ins.then_inc(s_t, 1)
            for t in range(TILES + 1):
                turn(t, t % 2, t // 2, 128 if t < TILES else DEC)

        @block.scalar
        def _(act):
            act.wait_ge(s_zero, 1)
            norm.act(act)

            def body(t, s, i, n):
                act.wait_ge(s_out[s], i * 16 + 16)
                for h in range(2):
                    act.wait_ge(s_t, t * 2 + h + 1)
                    act.activation(rows[0:n, s, h * 512:(h + 1) * 512].rearrange("p (q c) -> p q c", q=4), tb[2 * s + h][0:n], ACT.Copy).then_inc(s_tev, 1)
            over_tiles(act, body)

        @block.vector
        def _(dve):
            dve.sem_inc(s_tev, 4)
            for s in range(2):
                dve.sem_inc(s_out[s], 16)
            dve.memset(zero[:], 0.0).then_inc(s_zero, 1)
            dve.wait_ge(s_zero, 1)
            norm.dve(dve)


_OUTS = [("y_prompt", (1, SEQ, D)), ("y_sample", (DEC, 1, D)), ("wkv_prompt", (1, 1, HEADS, HD, HD)), ("wkv_sample", (1, DEC, HEADS, HD, HD)),
         ("shift_prompt", (1, 1, D)), ("shift_sample", (1, DEC, D)), ("k_prompt", (1, 1, WIN, KV, HD)), ("k_sample", (1, DEC, WIN, KV, HD)),
         ("v_prompt", (1, 1, WIN, KV, HD)), ("v_sample", (1, DEC, WIN, KV, HD))]


def layout(nc, inputs):
    arrays, io = {}, {}
    for name, a in {**inputs, **shape_constants()}.items():
        a = np.ascontiguousarray(a)
        arrays[f"in_{name}"] = a
        io[name] = nc.dram_tensor(f"in_{name}", a.shape, F32, kind="ExternalInput").ap()
    for name, shape in _OUTS:
        io["out_" + name] = nc.dram_tensor(f"out_{name}", shape, F32, kind="ExternalOutput").ap()
    return arrays, io


def kernel(**inputs):
    import concourse.bacc as bacc
    from concourse.bass_utils import run_bass_kernel_spmd

    nc = bacc.Bacc("TRN2", target_bir_lowering=False, num_devices=1)
    arrays, io = layout(nc, inputs)
    build(nc, io)
    r = run_bass_kernel_spmd(nc, [arrays], core_ids=[0])
    return tuple(r.results[0][f"out_{name}"] for name, _ in _OUTS)
```

```python
from contextlib import ExitStack, contextmanager

import numpy as np

import concourse.bass as bass
from concourse import mybir

F32 = mybir.dt.float32
F32R = mybir.dt.float32r
ALU = mybir.AluOpType
ACT = mybir.ActivationFunctionType
AX = mybir.AxisListType.X

D = 1024
DB = D // 128
SEQ = 1024
DEC = 8
NV = 1 + DEC
TOK = SEQ + DEC
NT = 3
TT = TOK // NT
HD = 64
HEADS = D // HD
C = 64
NCH = SEQ // C
N_ADA = 6
FF_GROUPS = 4
KV = 4
WIN = 128
EPS = 1e-6
LNX_EPS = 64e-5
DECAY_SCALE = float(np.exp(-0.5))
SCALE = HD ** -0.5

PARAM_TABLES = [
    [("norm1_g", 16), ("norm2_g", 16), ("final_g", 8), ("rw_mix", 48), ("at_bqkv", 12)],
    [("rw_w0", 8), ("rw_a0", 8), ("rw_kk", 8), ("rw_ka", 8), ("rw_rk", 8), ("rw_lnx_g", 8), ("rw_lnx_b", 8)],
    [("ada_b", 96)],
]
PARAM_AT = {}
for _t, _rows in enumerate(PARAM_TABLES):
    _at = 128 * _t
    for _name, _n in _rows:
        PARAM_AT[_name] = _at
        _at += _n

CONST_COLS = [("ident", 128), ("ones", 128), ("headsum", 128), ("lt", 64), ("le", 64), ("one64", 64), ("swap", 128)]
CONST_AT, _at = {}, 0
for _name, _n in CONST_COLS:
    CONST_AT[_name] = _at
    _at += _n
CONST_N = _at
WIDE = ["chunkstart", "cos", "sin"]


def shape_constants():
    p = np.arange(128)
    small = {
        "ident": np.eye(128),
        "ones": np.ones((128, 128)),
        "headsum": (p[:, None] // 64 == p[None, :] // 64),
        "lt": (p[:, None] % 64 < np.arange(64)[None, :]),
        "le": (p[:, None] % 64 <= np.arange(64)[None, :]),
        "one64": np.ones((128, 64)),
    }
    d = p % 64
    partner = np.where(d < 8, p + 8, np.where(d < 16, p - 8, p))
    swap = np.zeros((128, 128))
    swap[p, partner] = 1
    small["swap"] = swap
    const = np.concatenate([np.asarray(small[n], np.float32) for n, _ in CONST_COLS], 1)
    start = np.ones((128, TOK))
    start[:, 0:SEQ:C] = 0
    start[:, SEQ:] = 0
    pos = np.concatenate([np.arange(SEQ), np.full(DEC, 2048)]).astype(np.float32)
    inv = (np.float32(500000.0) ** (-np.arange(8, dtype=np.float32) / np.float32(8))).astype(np.float32)
    ang = (pos[None, :] * inv[np.minimum(d, 15) % 8][:, None]).astype(np.float64)
    rot = (d < 16)[:, None]
    cos = np.where(rot, np.cos(ang), 1.0)
    sin = np.where(rot, np.sin(ang) * np.where(d < 8, -1.0, 1.0)[:, None], 0.0)
    wide = np.concatenate([start, cos, sin], 1).astype(np.float32)
    q, k = np.arange(128)[:, None], np.arange(256)[None, :]
    mask = np.where((k - 128 <= q) & (k - 128 >= q - WIN), 0, -1e30).astype(np.float32)
    return {"const_small": const, "const_wide": wide, "const_mask": mask}


class Chain:

    def __init__(self, eng, sem, per=0, i=0, base=0):
        self.eng, self.sem, self.n = eng, sem, 0
        self.start = i * per + base
        self.per = per

    def link(self, ins):
        ins.then_inc(self.sem, 1)
        self.n += 1
        self.eng.wait_ge(self.sem, self.start + self.n)


class Net:

    def semaphore(self, name):
        self.sems.append(self.nc.alloc_semaphore(name=name))
        return self.sems[-1]


@contextmanager
def stage(net):
    net.sems = []
    yield
    net.nc.clear_and_free_semaphores(net.sems)
    net.nc.all_engine_barrier()


def tiles(ap, n=TT):
    return ap.rearrange("p (n t) -> p n t", t=n)


def blk(ap, i):
    return ap[:, bass.ds(i, 1), :].rearrange("p a n -> p (a n)")


def build(nc, io):
    with ExitStack() as root:
        net = Net()
        net.nc, net.io = nc, io

        def sb(name, shape, dt=F32):
            return root.enter_context(nc.sbuf_tensor(name, shape, dt))

        net.const = sb("const", [128, CONST_N])
        net.param = sb("param", [128, 3 * 128])
        net.mod = sb("mod", [128, 2 * N_ADA * DB, NV])
        net.csil = sb("c_silu", [128, DB, 32])
        net.gain = sb("gain", [128, 5, DB, NV])

        def scratch(name, shape):
            return nc.dram_tensor(name, shape, F32).ap()

        net.scratch = scratch
        net.x_saved = scratch("x_saved", [128, DB, TOK])
        net.hx_saved = scratch("hx_saved", [128, DB, 1 + TOK])
        net.sL, net.sLm, net.sA, net.sG, net.sRt, net.sAt, net.sBt, net.sKt, net.sBS, net.sBV = (
            scratch("scr_" + n, [DB, 128, TOK]) for n in ("L", "Lm", "A", "G", "Rt", "At", "Bt", "Kt", "BS", "BV"))
        net.sM = scratch("scr_M", [NCH, DB, 128, C])
        net.sT = scratch("scr_T", [NCH, DB, 128, C])
        net.sV = scratch("scr_V", [TOK, D])
        net.sY = scratch("scr_Y", [TOK, D])
        net.sSmp = scratch("scr_Smp", [5, DEC, D])
        with ExitStack() as rwkv:
            net.sprev = rwkv.enter_context(nc.sbuf_tensor("sprev", [128, DB, DEC], F32))
            net.pend = rwkv.enter_context(nc.sbuf_tensor("pend", [128, DB, NCH], F32))
            net.Ps = rwkv.enter_context(nc.sbuf_tensor("Ps", [128, DB, DEC], F32))
            with ExitStack() as mixed:
                net.hx = mixed.enter_context(nc.sbuf_tensor("hx", [128, DB, 1 + TOK], F32))
                with ExitStack() as first:
                    net.X = first.enter_context(nc.sbuf_tensor("X0", [128, DB, TOK], F32))
                    with stage(net):
                        stage_start(net)
                    with stage(net):
                        stage_norm1_rwkv(net)
                operands(net, mixed, "rk")
                for which in ("w", "a", "g"):
                    with stage(net):
                        stage_lora(net, which)
                with stage(net):
                    stage_r(net)
                with stage(net):
                    stage_k(net)
            with ExitStack() as ops:
                operands(net, ops, "v")
                with stage(net):
                    stage_v(net)
            with stage(net):
                stage_scan(net)
        net.X = sb("X", [128, DB, TOK])
        with ExitStack() as ops:
            operands(net, ops, "ro")
            with stage(net):
                stage_rwkv_out(net)
            with stage(net):
                stage_mlp(net, 0)
        with ExitStack() as ops:
            operands(net, ops, "at", False)
            with ExitStack() as heads:
                def hb(name, shape):
                    return heads.enter_context(nc.sbuf_tensor(name, shape, F32))
                net.Q = hb("Q", [128, DB, TOK])
                net.Kd = hb("Kd", [128, KV, TOK])
                net.Vt = hb("Vt", [128, SEQ // 128 + 1, KV * HD])
                net.Vd = hb("Vd", [128, KV, DEC])
                with stage(net):
                    stage_qkv(net)
                with stage(net):
                    stage_attend_samples(net)
                with stage(net):
                    stage_attend(net)
            with stage(net):
                stage_attend_out(net)
        with ExitStack() as ops:
            operands(net, ops, "m1")
            with stage(net):
                stage_mlp(net, 1)
        with stage(net):
            stage_final(net)


def operands(net, ctx, tag, with_weights=True):
    nc = net.nc
    net.HH = ctx.enter_context(nc.sbuf_tensor(f"{tag}_HH", [128, DB, TOK], F32R))
    net.HL = ctx.enter_context(nc.sbuf_tensor(f"{tag}_HL", [128, DB, TOK], F32R))
    if with_weights:
        weights(net, ctx, tag)


def weights(net, ctx, tag):
    nc = net.nc
    net.wraw = ctx.enter_context(nc.sbuf_tensor(f"{tag}_wraw", [128, 2, DB, 128], F32))
    net.wH = ctx.enter_context(nc.sbuf_tensor(f"{tag}_wH", [128, 2, DB, 128], F32R))
    net.wL = ctx.enter_context(nc.sbuf_tensor(f"{tag}_wL", [128, 2, DB, 128], F32R))


def c_(net, name):
    at = CONST_AT[name]
    return net.const[:, at:at + dict(CONST_COLS)[name]]




class Ada:

    GROUP = 2048
    PER_LAYER = N_ADA * D // GROUP
    SLOTS = 4

    def __init__(self, net, ctx, tag):
        nc = net.nc
        self.net = net
        sem = lambda name: net.semaphore(f"{tag}_{name}")
        self.ring = ctx.enter_context(nc.sbuf_tensor(f"{tag}_ring", [128, self.SLOTS, self.GROUP], F32))
        self.strip = ctx.enter_context(nc.sbuf_tensor(f"{tag}_strip", [128, 512], F32))
        self.acc = ctx.enter_context(nc.psum_tensor(f"{tag}_acc", [128, 512], F32))
        self.accT = ctx.enter_context(nc.psum_tensor(f"{tag}_accT", [128, 4, 128], F32))
        self.s_w = [sem(f"w{k}") for k in range(self.SLOTS)]
        self.s_used, self.s_acc, self.s_strip, self.s_accT, self.s_mod = sem("used"), sem("acc"), sem("strip"), sem("accT"), sem("mod")

    def load(self, sp, g, layer, column):
        for k in range(DB):
            sp.wait_ge(self.s_used, g * DB + k + 1)
            w = self.net.io["ada_w"][bass.ds(layer, 1), k * 128:(k + 1) * 128, bass.ds(column, self.GROUP)]
            sp.dma_start(self.ring[:, k % self.SLOTS, :], w.rearrange("a p n -> p (a n)")).then_inc(self.s_w[k % self.SLOTS], 16)

    def multiply(self, pe, g):
        pe.wait_ge(self.s_strip, g + 1)
        for k in range(DB):
            s = k % self.SLOTS
            pe.wait_ge(self.s_w[s], g * 16 * (DB // self.SLOTS) + 16 * (k // self.SLOTS + 1))
            for q in range(4):
                ins = pe.matmul(self.acc[32 * q:32 * q + 32, :], self.net.csil[:, k, :], self.ring[:, s, 512 * q:512 * q + 512], start=(k == 0), stop=(k == DB - 1), tile_position=(0, 32 * q))
            ins.then_inc(self.s_used, 1)
        pe.wait_ge(self.s_used, (g + 1) * DB + self.SLOTS)
        pe.sem_inc(self.s_acc, 1)

    def turn(self, pe, g):
        pe.wait_ge(self.s_strip, g + 2)
        pe.wait_ge(self.s_mod, g + 1)
        for r in range(4):
            ins = pe.transpose(self.accT[:, r, :], self.strip[:, r * 128:(r + 1) * 128], c_(self.net, "ident"))
        ins.then_inc(self.s_accT, 1)

    def strips_out(self, act, g):
        act.wait_ge(self.s_acc, g + 1)
        act.activation(self.strip[:], self.acc[:], ACT.Copy).then_inc(self.s_strip, 1)

    def turned_out(self, act, g, block):
        act.wait_ge(self.s_accT, g + 1)
        for q in range(4):
            ins = act.activation(self.net.mod[:, bass.ds(block + 4 * q, 4), :], self.accT[:, :, 32 * q:32 * q + NV], ACT.Copy)
        ins.then_inc(self.s_mod, 1)


def add_ada_bias(dve, net, first, n, done):
    at = PARAM_AT["ada_b"] + first
    m = net.mod[:, first:first + n, :]
    dve.tensor_tensor(m, m, net.param[:, at:at + n].unsqueeze(2).to_broadcast([128, n, NV]), ALU.add).then_inc(done, 1)


def make_gain(dve, net, slot, done):
    layer = slot // 2
    scale = mod_part(net, layer, (1, 4)[slot % 2])
    at = PARAM_AT[("norm1_g", "norm2_g")[slot % 2]] + DB * layer
    g = net.param[:, at:at + DB].unsqueeze(2).to_broadcast([128, DB, NV])
    dve.scalar_tensor_tensor(out=net.gain[:, slot], in0=scale, scalar=1.0, in1=g, op0=ALU.add, op1=ALU.mult).then_inc(done, 1)


def stage_start(net):
    nc, io = net.nc, net.io
    with ExitStack() as ctx:
        def sb(name, shape, dt=F32):
            return ctx.enter_context(nc.sbuf_tensor(name, shape, dt))

        def sem(name):
            return net.semaphore(name)

        rows = sb("param_rows", [128, 3, 128])
        crow = sb("c_row", [NV, D])
        csig = sb("c_sig", [NV, D])
        csil = net.csil
        xrow = sb("x_rows", [128, DB, D])
        xsrow = sb("xs_rows", [DEC, D])
        ada = Ada(net, ctx, "ada0")
        tp = [ctx.enter_context(nc.psum_tensor(f"tp{i}", [128, 4, 128], F32)) for i in range(2)]

        s_const, s_param, s_c, s_x = sem("s_const"), sem("s_param"), sem("s_c"), sem("s_x")
        s_rows0 = sem("s_rows_zero")
        s_sig, s_sil, s_sil0, s_silT = sem("s_sig"), sem("s_sil"), sem("s_sil_zero"), sem("s_silT")
        s_tp, s_tp_free = sem("s_tp"), sem("s_tp_free")
        s_dv = sem("s_dv")
        ident = c_(net, "ident")
        n_param = 0
        block = ctx.enter_context(nc.Block())

        turns = [("param", None)] + [("c", i) for i in range(2)] + [("x", (t, h)) for t in range(DB) for h in range(2)] + [("xs", h) for h in range(2)]

        @block.sync
        def _(sp):
            sp.dma_start(net.const[:], io["const_small"]).then_inc(s_const, 16)
            sp.dma_start(crow[0:1, :], io["c_prompt"]).then_inc(s_c, 16)
            sp.dma_start(crow[1:NV, :], io["c_sample"]).then_inc(s_c, 16)
            sp.wait_ge(s_rows0, 1)
            for t, table in enumerate(PARAM_TABLES):
                for name, n in table:
                    at = PARAM_AT[name] - 128 * t
                    ap = io[name]
                    ap = ap.rearrange({1: "(r p) -> r p", 2: "a (r p) -> (a r) p", 3: "a b (r p) -> (a b r) p"}[len(ap.shape)], p=128) if name != "rw_rk" else ap.rearrange("a (b h) d -> (a b) (h d)", h=2)
                    sp.dma_start(rows[at:at + n, t, :], ap).then_inc(s_param, 16)
            ada.load(sp, 0, 0, 0)

        @block.gpsimd
        def _(pool):
            for t in range(DB):
                pool.dma_start(xrow[:, t, :], io["x_prompt"][0, t * 128:(t + 1) * 128, :]).then_inc(s_x, 16)
            pool.dma_start(xsrow[:], io["x_sample"].rearrange("b o d -> (b o) d")).then_inc(s_x, 16)

        @block.scalar
        def _(act):
            act.wait_ge(s_c, 32)
            nc.scalar.activation(csig[:], crow[:], ACT.Sigmoid).then_inc(s_sig, 1)
            ada.strips_out(act, 0)
            ada.turned_out(act, 0, 0)

        @block.tensor
        def _(pe):
            pe.sem_inc(ada.s_used, ada.SLOTS)
            pe.wait_ge(s_const, 16)
            for n, (what, arg) in enumerate(turns):
                bank = tp[n % 2]
                if n >= 2:
                    pe.wait_ge(s_tp_free, n - 1)
                if what == "param":
                    pe.wait_ge(s_param, 16 * sum(len(t) for t in PARAM_TABLES))
                    for t in range(3):
                        ins = pe.transpose(bank[:, t, :], rows[:, t, :], ident)
                elif what == "c":
                    pe.wait_ge(s_sil, 1)
                    for q in range(4):
                        ins = pe.transpose(bank[:, q, 0:NV], crow[:, (4 * arg + q) * 128:(4 * arg + q + 1) * 128], ident[0:NV, 0:NV])
                elif what == "x":
                    t, h = arg
                    pe.wait_ge(s_x, 16 * (DB + 1))
                    for q in range(4):
                        ins = pe.transpose(bank[:, q, :], xrow[:, t, (4 * h + q) * 128:(4 * h + q + 1) * 128], ident)
                else:
                    for q in range(4):
                        ins = pe.transpose(bank[:, q, 0:DEC], xsrow[:, (4 * arg + q) * 128:(4 * arg + q + 1) * 128], ident[0:DEC, 0:DEC])
                ins.then_inc(s_tp, 1)
            pe.wait_ge(s_silT, 2)
            ada.multiply(pe, 0)
            ada.turn(pe, 0)

        @block.vector
        def _(dve):
            dve.sem_inc(ada.s_strip, 1)
            dve.sem_inc(ada.s_mod, 1)
            dve.memset(rows[:], 0.0).then_inc(s_rows0, 1)
            dve.memset(csil[:], 0.0).then_inc(s_sil0, 1)
            dve.wait_ge(s_sig, 1)
            dve.tensor_tensor(crow[:], crow[:], csig[:], ALU.mult).then_inc(s_sil, 1)
            dve.wait_ge(s_sil0, 1)
            for n, (what, arg) in enumerate(turns):
                bank = tp[n % 2]
                dve.wait_ge(s_tp, n + 1)
                if what == "param":
                    dve.tensor_copy(net.param[:].rearrange("p (t n) -> p t n", t=3), bank[:, 0:3, :]).then_inc(s_tp_free, 1)
                elif what == "c":
                    ins = dve.tensor_copy(csil[:, 4 * arg:4 * arg + 4, 0:NV], bank[:, :, 0:NV])
                    ins.then_inc(s_silT, 1)
                    dve.wait_ge(s_silT, arg + 1)
                    dve.sem_inc(s_tp_free, 1)
                elif what == "x":
                    t, h = arg
                    dve.tensor_copy(net.X[:, 4 * h:4 * h + 4, t * 128:(t + 1) * 128], bank[:]).then_inc(s_tp_free, 1)
                else:
                    dve.tensor_copy(net.X[:, 4 * arg:4 * arg + 4, SEQ:TOK], bank[:, :, 0:DEC]).then_inc(s_tp_free, 1)
            dve.wait_ge(s_tp_free, len(turns))
            dve.wait_ge(ada.s_mod, 2)
            add_ada_bias(dve, net, 0, 2 * DB, s_dv)
            dve.wait_ge(s_dv, 1)
            make_gain(dve, net, 0, s_dv)
            at = PARAM_AT["final_g"]
            dve.tensor_copy(net.gain[:, 4], net.param[:, at:at + DB].unsqueeze(2).to_broadcast([128, DB, NV])).then_inc(s_dv, 1)
            dve.wait_ge(s_dv, 3)


def mod_part(net, layer, part):
    at = (layer * N_ADA + part) * DB
    return net.mod[:, at:at + DB, :]




class Norm:

    def __init__(self, net, ctx, tag, gain, shift, keep=None, split=True, sq=None, rs=None, ps=None):
        nc = net.nc
        self.net, self.gain, self.shift, self.keep, self.split = net, gain, shift, keep, split
        sem = lambda name: net.semaphore(f"{tag}_{name}")
        self.sq = ctx.enter_context(nc.sbuf_tensor(f"{tag}_sq", [128, 2, TOK], F32)) if sq is None else sq
        self.rs = ctx.enter_context(nc.sbuf_tensor(f"{tag}_rs", [128, TOK], F32)) if rs is None else rs
        self.ps = ctx.enter_context(nc.psum_tensor(f"{tag}_ps", [128, NT, 512], F32)) if ps is None else ps
        self.s_sq, self.s_used, self.s_sum = sem("sq"), sem("sq_used"), sem("sum")
        self.s_mean, self.s_root, self.s_rs = sem("mean"), sem("root"), sem("rs")
        self.s_xn, self.s_h, self.s_hi, self.s_lo = sem("xn"), sem("h"), sem("hi"), sem("lo")
        self.s_smp, self.s_dv = sem("smp"), sem("dv")

    def pe(self, pe):
        ones = c_(self.net, "ones")
        for b in range(DB):
            pe.wait_ge(self.s_sq, b + 1)
            for n in range(NT):
                ins = pe.matmul(self.ps[:, n, 0:TT], ones, self.sq[:, b % 2, n * TT:(n + 1) * TT], start=(b == 0), stop=(b == DB - 1))
            ins.then_inc(self.s_used, 1)

    def act(self, act):
        net = self.net
        for b in range(DB):
            if b >= 2:
                act.wait_ge(self.s_used, b - 1)
            act.activation(self.sq[:, b % 2, :], net.X[:, b, :], ACT.Square).then_inc(self.s_sq, 1)
        act.wait_ge(self.s_mean, 1)
        act.activation(self.rs[:], self.rs[:], ACT.Sqrt).then_inc(self.s_root, 1)
        for b in range(DB):
            act.wait_ge(self.s_xn, b + 1)
            h = self.h(b)
            act.activation(h[:, 0:SEQ], self.sq[:, b % 2, 0:SEQ], ACT.Identity, bias=self.shift[:, b, 0:1], scale=self.gain[:, b, 0:1]).then_inc(self.s_h, 1)
            if not self.split:
                continue
            act.wait_ge(self.s_h, b + 1)
            act.wait_ge(self.s_smp, b + 1)
            act.activation(net.HH[:, b, :], h[:, 0:TOK], ACT.Copy).then_inc(self.s_hi, 1)

    def h(self, b):
        return self.sq[:, b % 2, :] if self.keep is None else self.keep[:, b, :]

    def dve(self, dve):
        net = self.net
        dve.wait_ge(self.s_used, DB)
        dve.tensor_scalar(tiles(self.rs[:]), self.ps[:, :, 0:TT], 1.0 / D, EPS, ALU.mult, ALU.add).then_inc(self.s_mean, 1)
        dve.wait_ge(self.s_root, 1)
        dve.reciprocal(self.rs[:], self.rs[:]).then_inc(self.s_rs, 1)
        dve.wait_ge(self.s_rs, 1)
        for b in range(DB):
            if b >= 2 and self.split:
                dve.wait_ge(self.s_hi, b - 1)
                dve.wait_ge(self.s_lo, b - 1)
            elif b >= 2:
                dve.wait_ge(self.s_h, b - 1)
                dve.wait_ge(self.s_smp, b - 1)
            xn = self.sq[:, b % 2, :]
            dve.tensor_tensor(xn, net.X[:, b, :], self.rs[:], ALU.mult).then_inc(self.s_xn, 1)
            dve.wait_ge(self.s_xn, b + 1)
            h = self.h(b)
            dve.tensor_tensor(h[:, SEQ:TOK], xn[:, SEQ:TOK], self.gain[:, b, 1:NV], ALU.mult).then_inc(self.s_dv, 1)
            dve.wait_ge(self.s_dv, b + 1)
            dve.tensor_tensor(h[:, SEQ:TOK], h[:, SEQ:TOK], self.shift[:, b, 1:NV], ALU.add).then_inc(self.s_smp, 1)
            if b >= 1 and self.split:
                self.low(dve, b - 1)
        if self.split:
            self.low(dve, DB - 1)

    def low(self, dve, b):
        net = self.net
        dve.wait_ge(self.s_hi, b + 1)
        dve.wait_ge(self.s_h, b + 1)
        dve.tensor_tensor(net.HL[:, b, :], self.h(b)[:, 0:TOK], net.HH[:, b, :].bitcast(F32), ALU.subtract).then_inc(self.s_lo, 1)




class Panels:

    LOW0, DONE0 = 2, 2 * NT

    def __init__(self, net, ctx, tag, cols=128):
        nc = net.nc
        self.net, self.cols = net, cols
        sem = lambda name: net.semaphore(f"{tag}_{name}")
        self.acc = ctx.enter_context(nc.psum_tensor(f"{tag}_acc", [128, NT, 512], F32))
        self.landed = [sem("landed0"), sem("landed1")]
        self.high, self.low = sem("high"), sem("low")
        self.done, self.free = sem("acc_done"), sem("acc_free")

    def load(self, sp, p, s, src):
        sp.wait_ge(self.low, p + 1)
        sp.dma_start(self.net.wraw[:, s, :, 0:self.cols], src).then_inc(self.landed[s], 16)

    def split(self, pool, p, s, i):
        net = self.net
        raw, high = net.wraw[:, s, :, 0:self.cols], net.wH[:, s, :, 0:self.cols]
        pool.wait_ge(self.landed[s], i * 16 + 16)
        pool.wait_ge(self.done, p * NT + NT)
        one = c_(net, "ones")[:, 0:self.cols].unsqueeze(1).to_broadcast([128, DB, self.cols])
        pool.tensor_tensor(high, raw, one, ALU.mult).then_inc(self.high, 1)
        pool.wait_ge(self.high, p + 1)
        pool.tensor_tensor(net.wL[:, s, :, 0:self.cols], raw, high.bitcast(F32), ALU.subtract).then_inc(self.low, 1)

    def multiply(self, pe, p, s, hi, lo, ready=None, free=None):
        net = self.net
        pe.wait_ge(self.low, p + 1 + self.LOW0)
        for n in range(NT):
            for sem, value in free or [(self.free, p * NT + 1)]:
                pe.wait_ge(sem, value + n)
            t = slice(n * TT, (n + 1) * TT)
            for k in range(DB):
                if n == 0 and ready is not None:
                    pe.wait_ge(ready[0], ready[1] + k)
                out = self.acc[0:self.cols, n, 0:TT]
                wh, wl = net.wH[:, s, k, 0:self.cols], net.wL[:, s, k, 0:self.cols]
                pe.matmul(out, wh, hi[:, k, t], start=(k == 0), stop=False)
                pe.matmul(out, wh, lo[:, k, t], start=False, stop=False)
                ins = pe.matmul(out, wl, hi[:, k, t], start=False, stop=(k == DB - 1))
            ins.then_inc(self.done, 1)

    def summed(self, eng, p, n):
        eng.wait_ge(self.done, p * NT + n + 1 + self.DONE0)


def panel_of(w, m):
    return w[:, bass.ds(m, 128)].rearrange("(k p) m -> p k m", p=128)


def add_gated(dve, net, pan, p, m, gate, tmp, s_free, s_tmp, n_before):
    X = blk(net.X, m)
    for n in range(NT):
        pan.summed(dve, p, n)
        a, z = n * TT, min((n + 1) * TT, SEQ)
        ins = dve.scalar_tensor_tensor(out=X[:, a:z], in0=pan.acc[:, n, 0:z - a], scalar=blk(gate, m)[:, 0:1], in1=X[:, a:z], op0=ALU.mult, op1=ALU.add)
        if n < NT - 1:
            ins.then_inc(s_free, 1)
    dve.tensor_tensor(tmp, pan.acc[:, NT - 1, TT - DEC:TT], blk(gate, m)[:, 1:NV], ALU.mult).then_inc(s_tmp, 1)
    dve.wait_ge(s_tmp, n_before + 1)
    dve.tensor_tensor(X[:, SEQ:TOK], X[:, SEQ:TOK], tmp, ALU.add).then_inc(s_free, 1)


def stage_mlp(net, layer):
    nc, io = net.nc, net.io
    up = io["mlp_up"][layer]
    down = io["mlp_down"][layer]
    gate = mod_part(net, layer, 5)
    with ExitStack() as ctx:
        def sb(name, shape, dt=F32):
            return ctx.enter_context(nc.sbuf_tensor(f"mlp{layer}_{name}", shape, dt))

        def sem(name):
            return net.semaphore(f"mlp{layer}_{name}")

        GH, GL = sb("GH", [128, DB, TOK], F32R), sb("GL", [128, DB, TOK], F32R)
        act_buf = sb("relu", [128, 2, TOK])
        norm = Norm(net, ctx, f"mlpn{layer}", net.gain[:, 2 * layer + 1], mod_part(net, layer, 3), sq=act_buf)
        smp = sb("smp", [128, DEC])
        pan = Panels(net, ctx, f"mlp{layer}p")
        s_relu, s_sqr, s_gh, s_gl, s_smp = sem("relu"), sem("sqr"), sem("gh"), sem("gl"), sem("smp")
        s_added = sem("added")
        block = ctx.enter_context(nc.Block())
        GP = 2 * DB

        @block.sync
        def _(sp):
            with sp.Fori(0, FF_GROUPS) as g:
                with sp.Fori(0, DB // 2) as j:
                    for s in range(2):
                        pan.load(sp, g * GP + j * 2 + s, s, panel_of(up, g * 1024 + j * 256 + s * 128))
                with sp.Fori(0, DB // 2) as j:
                    for s in range(2):
                        pan.load(sp, g * GP + DB + j * 2 + s, s, panel_of(down[bass.ds(g * 1024, 1024), :], j * 256 + s * 128))

        @block.gpsimd
        def _(pool):
            with pool.Fori(0, FF_GROUPS * DB) as j:
                for s in range(2):
                    pan.split(pool, j * 2 + s, s, j)

        @block.tensor
        def _(pe):
            norm.pe(pe)
            with pe.Fori(0, FF_GROUPS) as g:
                with pe.Fori(0, DB // 2) as j:
                    for s in range(2):
                        pan.multiply(pe, g * GP + j * 2 + s, s, net.HH, net.HL, ready=(norm.s_lo, 1), free=[(pan.free, (g * DB + j * 2 + s) * NT + 1), (s_added, g * DB * NT + 1)])
                with pe.Fori(0, DB // 2) as j:
                    for s in range(2):
                        pan.multiply(pe, g * GP + DB + j * 2 + s, s, GH, GL, ready=(s_gl, g * DB + 3),
                                     free=[(pan.free, (g + 1) * DB * NT + 1), (s_added, (g * DB + j * 2 + s) * NT + 1)])

        @block.scalar
        def _(act):
            act.sem_inc(pan.free, NT)
            norm.act(act)
            with act.Fori(0, FF_GROUPS) as g:
                with act.Fori(0, DB // 2) as j:
                    for s in range(2):
                        h, p = g * DB + j * 2 + s, g * GP + j * 2 + s
                        act.wait_ge(s_gl, h + 1)
                        for n in range(NT):
                            pan.summed(act, p, n)
                            act.activation(act_buf[:, s, n * TT:(n + 1) * TT], pan.acc[:, n, 0:TT], ACT.Relu).then_inc(pan.free, 1)
                        act.wait_ge(s_sqr, h + 1)
                        act.activation(blk(GH, j * 2 + s), act_buf[:, s, :], ACT.Copy).then_inc(s_gh, 1)

        @block.vector
        def _(dve):
            dve.sem_inc(s_gl, 2)
            dve.sem_inc(pan.low, pan.LOW0)
            dve.sem_inc(pan.done, pan.DONE0)
            dve.sem_inc(s_added, NT)
            norm.dve(dve)
            with dve.Fori(0, FF_GROUPS) as g:
                with dve.Fori(0, DB // 2) as j:
                    for s in range(2):
                        h, p = g * DB + j * 2 + s, g * GP + j * 2 + s
                        dve.wait_ge(pan.free, h * NT + 2 * NT)
                        dve.tensor_tensor(act_buf[:, s, :], act_buf[:, s, :], act_buf[:, s, :], ALU.mult).then_inc(s_sqr, 1)
                        dve.wait_ge(s_gh, h + 1)
                        dve.wait_ge(s_sqr, h + 1)
                        dve.tensor_tensor(blk(GL, j * 2 + s), act_buf[:, s, :], blk(GH, j * 2 + s).bitcast(F32), ALU.subtract).then_inc(s_gl, 1)
                with dve.Fori(0, DB // 2) as j:
                    for s in range(2):
                        add_gated(dve, net, pan, g * GP + DB + j * 2 + s, j * 2 + s, gate, smp[:], s_added, s_smp, g * DB + j * 2 + s)





def row(scratch, b):
    return scratch[bass.ds(b, 1)].rearrange("a p t -> p (a t)")


def stage_norm1_rwkv(net):
    nc, io = net.nc, net.io
    with ExitStack() as ctx:
        norm = Norm(net, ctx, "rn", net.gain[:, 0], mod_part(net, 0, 0), keep=net.hx[:, :, 1:1 + TOK], split=False)
        sem = lambda name: net.semaphore(f"rn_{name}")
        srow = ctx.enter_context(nc.sbuf_tensor("shift_rows", [DEC, D], F32))
        last = ctx.enter_context(nc.sbuf_tensor("last_rows", [NV, D], F32))
        tp = [ctx.enter_context(nc.psum_tensor(f"rn_tp{i}", [128, 4, 128], F32)) for i in range(2)]
        s_in, s_tp, s_prev, s_last, s_out, s_zero = sem("in"), sem("tp"), sem("prev"), sem("last"), sem("out"), sem("zero")
        ident = c_(net, "ident")
        block = ctx.enter_context(nc.Block())

        @block.sync
        def _(sp):
            sp.dma_start(srow[:], io["state_shift"][0]).then_inc(s_in, 16)
            sp.dma_start(net.x_saved, net.X[:]).then_inc(s_out, 16)
            sp.wait_ge(s_last, 4)
            sp.dma_start(io["out_shift_prompt"].rearrange("a b d -> (a b) d"), last[0:1, :]).then_inc(s_out, 16)
            sp.dma_start(io["out_shift_sample"].rearrange("a b d -> (a b) d"), last[1:NV, :]).then_inc(s_out, 16)
            sp.dma_start(net.hx_saved, net.hx[:]).then_inc(s_out, 16)
            sp.wait_ge(s_out, 64)

        @block.tensor
        def _(pe):
            norm.pe(pe)
            pe.wait_ge(s_in, 16)
            for n in range(2):
                for q in range(4):
                    ins = pe.transpose(tp[n][:, q, 0:DEC], srow[:, (4 * n + q) * 128:(4 * n + q + 1) * 128], ident[0:DEC, 0:DEC])
                ins.then_inc(s_tp, 1)
            pe.wait_ge(norm.s_h, DB)
            pe.wait_ge(norm.s_smp, DB)
            for n in range(2):
                pe.wait_ge(s_prev, n + 1)
                for q in range(4):
                    ins = pe.transpose(tp[n][0:NV, q, :], net.hx[:, 4 * n + q, SEQ:SEQ + NV], ident)
                ins.then_inc(s_tp, 1)

        @block.scalar
        def _(act):
            norm.act(act)

        @block.vector
        def _(dve):
            dve.memset(net.hx[:, :, 0:1], 0.0).then_inc(s_zero, 1)
            norm.dve(dve)
            for n in range(2):
                dve.wait_ge(s_tp, n + 1)
                dve.tensor_copy(net.sprev[:, 4 * n:4 * n + 4, :], tp[n][:, :, 0:DEC]).then_inc(s_prev, 1)
            for n in range(2):
                dve.wait_ge(s_tp, n + 3)
                dve.tensor_copy(last[:, n * 512:(n + 1) * 512].rearrange("v (q c) -> v q c", q=4), tp[n][0:NV, :, :]).then_inc(s_last, 2)


class Mix:

    def __init__(self, net, ctx, tag, which, buf=None, hx=None):
        self.net, self.at, self.hx = net, PARAM_AT["rw_mix"] + 8 * which, hx
        sem = lambda name: net.semaphore(f"{tag}_{name}")
        self.buf = ctx.enter_context(net.nc.sbuf_tensor(f"{tag}_xm", [128, 2, TOK], F32)) if buf is None else buf
        self.s_hx = [sem("hx0"), sem("hx1")] if hx is not None else None
        self.s_d, self.s_xm, self.s_hi, self.s_lo = sem("d"), sem("xm"), sem("hi"), sem("lo")

    def load(self, act, b):
        act.dma_start(self.hx[:, b % 2, :], self.net.hx_saved[:, b]).then_inc(self.s_hx[b % 2], 16)

    def act(self, act):
        if self.s_hx:
            self.load(act, 0)
            self.load(act, 1)
        for b in range(DB):
            act.wait_ge(self.s_xm, b + 1)
            if self.s_hx and b + 2 < DB:
                self.load(act, b + 2)
            act.activation(self.net.HH[:, b, :], self.buf[:, b % 2, :], ACT.Copy).then_inc(self.s_hi, 1)

    def dve(self, dve):
        net = self.net

        def low(b):
            dve.wait_ge(self.s_hi, b + 1)
            dve.tensor_tensor(net.HL[:, b, :], self.buf[:, b % 2, :], net.HH[:, b, :].bitcast(F32), ALU.subtract).then_inc(self.s_lo, 1)

        for b in range(DB):
            hx = net.hx[:, b] if self.hx is None else self.hx[:, b % 2]
            d, h = self.buf[:, b % 2, :], hx[:, 1:1 + TOK]
            if b >= 2:
                dve.wait_ge(self.s_lo, b - 1)
            if self.s_hx:
                dve.wait_ge(self.s_hx[b % 2], 16 * (b // 2 + 1))
            dve.tensor_tensor(d[:, 0:SEQ], hx[:, 0:SEQ], hx[:, 1:1 + SEQ], ALU.subtract).then_inc(self.s_d, 1)
            dve.tensor_tensor(d[:, SEQ:TOK], net.sprev[:, b, :], hx[:, 1 + SEQ:1 + TOK], ALU.subtract).then_inc(self.s_d, 1)
            dve.wait_ge(self.s_d, 2 * b + 2)
            dve.scalar_tensor_tensor(out=d, in0=d, scalar=net.param[:, self.at + b:self.at + b + 1], in1=h, op0=ALU.mult, op1=ALU.add).then_inc(self.s_xm, 1)
            if b >= 1:
                low(b - 1)
        low(DB - 1)


def stage_lora(net, which):
    nc, io = net.nc, net.io
    tag = f"lora_{which}"
    R = {"w": 64, "a": 64, "g": 128}[which]
    first, second = io[f"rw_{which}1"][0], io[f"rw_{which}2"][0]
    inner = {"w": ACT.Tanh, "a": ACT.Copy, "g": ACT.Sigmoid}[which]
    stores = 2 if which == "w" else 1
    with ExitStack() as ctx:
        def sb(name, shape, dt=F32):
            return ctx.enter_context(nc.sbuf_tensor(f"{tag}_{name}", shape, dt))

        def sem(name):
            return net.semaphore(f"{tag}_{name}")

        mix = Mix(net, ctx, tag, {"w": 1, "a": 4, "g": 5}[which])
        pan = Panels(net, ctx, tag, R)
        w2 = sb("w2", [R, D])
        low_rank = sb("inner", [R, TOK])
        out = sb("out", [128, 2, TOK])
        cum = sb("cum", [128, 2, TOK]) if which == "w" else None
        start = sb("start", [128, TOK]) if which == "w" else None
        ps = ctx.enter_context(nc.psum_tensor(f"{tag}_ps", [128, NT, 512], F32))
        s_w2, s_in, s_ps, s_ps_free = sem("w2"), sem("inner"), sem("ps"), sem("ps_free")
        s_out, s_dv, s_ready = sem("sig"), sem("dv"), sem("ready")
        s_stored = [sem("stored0"), sem("stored1")]
        block = ctx.enter_context(nc.Block())

        @block.sync
        def _(sp):
            pan.load(sp, 0, 0, first.rearrange("(k p) m -> p k m", p=128))
            sp.dma_start(w2[:], second).then_inc(s_w2, 16)
            if which == "w":
                sp.dma_start(start[:], io["const_wide"][:, 0:TOK]).then_inc(s_w2, 16)
            for b in range(DB):
                s = b % 2
                if which == "w":
                    sp.wait_ge(s_ready, b + 1)
                    sp.dma_start(net.sL[b], cum[:, s, :]).then_inc(s_stored[s], 16)
                    sp.dma_start(net.sLm[b], out[:, s, :]).then_inc(s_stored[s], 16)
                else:
                    sp.wait_ge(s_out, b * NT + NT)
                    sp.dma_start({"a": net.sA, "g": net.sG}[which][b], out[:, s, :]).then_inc(s_stored[s], 16)
            for s in range(2):
                sp.wait_ge(s_stored[s], 16 * stores * (DB // 2))

        @block.gpsimd
        def _(pool):
            pan.split(pool, 0, 0, 0)

        @block.tensor
        def _(pe):
            pan.multiply(pe, 0, 0, net.HH, net.HL, ready=(mix.s_lo, 1))
            pe.wait_ge(s_in, NT)
            pe.wait_ge(s_w2, 32 if which == "w" else 16)
            for b in range(DB):
                for n in range(NT):
                    if b:
                        pe.wait_ge(s_out, (b - 1) * NT + n + 1)
                    pe.matmul(ps[:, n, 0:TT], w2[:, b * 128:(b + 1) * 128], low_rank[:, n * TT:(n + 1) * TT], start=True, stop=True).then_inc(s_ps, 1)

        @block.scalar
        def _(act):
            mix.act(act)
            for n in range(NT):
                pan.summed(act, 0, n)
                act.activation(low_rank[:, n * TT:(n + 1) * TT], pan.acc[0:R, n, 0:TT], inner).then_inc(s_in, 1)
            for b in range(DB):
                if b >= 2:
                    act.wait_ge(s_stored[b % 2], 16 * stores * (b // 2))
                for n in range(NT):
                    act.wait_ge(s_ps, b * NT + n + 1)
                    o = out[:, b % 2, n * TT:(n + 1) * TT]
                    if which == "g":
                        act.activation(o, ps[:, n, 0:TT], ACT.Copy).then_inc(s_out, 1)
                    else:
                        at = PARAM_AT[f"rw_{which}0"] + b
                        act.activation(o, ps[:, n, 0:TT], ACT.Sigmoid, bias=net.param[:, at:at + 1]).then_inc(s_out, 1)

        @block.vector
        def _(dve):
            dve.sem_inc(pan.low, pan.LOW0)
            dve.sem_inc(pan.done, pan.DONE0)
            dve.sem_inc(pan.free, NT)
            mix.dve(dve)
            if which == "w":
                chain = Chain(dve, s_dv)
                dve.wait_ge(s_w2, 32)
                for b in range(DB):
                    o, L = out[:, b % 2, :], cum[:, b % 2, :]
                    dve.wait_ge(s_out, (b + 1) * NT)
                    if b >= 2:
                        dve.wait_ge(s_stored[b % 2], 16 * stores * (b // 2))
                    chain.link(dve.tensor_scalar(o, o, -DECAY_SCALE, None, ALU.mult))
                    chain.link(dve.tensor_tensor_scan(L, start[:], o, 0.0, ALU.mult, ALU.add))
                    dve.tensor_tensor(o, L, o, ALU.subtract).then_inc(s_ready, 1)


def stage_r(net):
    nc, io = net.nc, net.io
    with ExitStack() as ctx:
        def sb(name, shape, dt=F32):
            return ctx.enter_context(nc.sbuf_tensor(f"r_{name}", shape, dt))

        def sem(name):
            return net.semaphore(f"r_{name}")

        mix = Mix(net, ctx, "r", 0)
        pan = Panels(net, ctx, "rp")
        L, Rt = sb("L", [128, 2, TOK]), sb("Rt", [128, 2, TOK])
        s_L, s_P, s_Rt, s_st = [sem("L0"), sem("L1")], sem("P"), sem("Rt"), [sem("st0"), sem("st1")]
        block = ctx.enter_context(nc.Block())
        w = io["rw_wr"][0]

        @block.sync
        def _(sp):
            with sp.Fori(0, DB // 2) as j:
                for s in range(2):
                    pan.load(sp, j * 2 + s, s, panel_of(w, j * 256 + s * 128))
                    sp.wait_ge(s_Rt, j * 2 + s + 1)
                    sp.dma_start(L[:, s, :], row(net.sL, j * 2 + s)).then_inc(s_L[s], 16)

        @block.gpsimd
        def _(pool):
            with pool.Fori(0, DB // 2) as j:
                for s in range(2):
                    pan.split(pool, j * 2 + s, s, j)

        @block.tensor
        def _(pe):
            with pe.Fori(0, DB // 2) as j:
                for s in range(2):
                    pan.multiply(pe, j * 2 + s, s, net.HH, net.HL, ready=(mix.s_lo, 1))

        @block.scalar
        def _(act):
            mix.act(act)
            with act.Fori(0, DB // 2) as j:
                for s in range(2):
                    act.wait_ge(s_L[s], j * 16 + 16)
                    act.activation(L[:, s, :], L[:, s, :], ACT.Exp).then_inc(s_P, 1)
                    act.wait_ge(s_Rt, j * 2 + s + 3)
                    act.dma_start(row(net.sRt, j * 2 + s), Rt[:, s, :]).then_inc(s_st[s], 16)
            for s in range(2):
                act.wait_ge(s_st[s], 16 * (DB // 2) + 16)

        @block.vector
        def _(dve):
            dve.sem_inc(pan.low, pan.LOW0)
            dve.sem_inc(pan.done, pan.DONE0)
            dve.sem_inc(pan.free, NT)
            dve.sem_inc(s_Rt, 2)
            for s in range(2):
                dve.sem_inc(s_st[s], 16)
            mix.dve(dve)
            with dve.Fori(0, DB // 2) as j:
                for s in range(2):
                    dve.wait_ge(s_P, j * 2 + s + 1)
                    dve.wait_ge(s_st[s], j * 16 + 16)
                    for n in range(NT):
                        pan.summed(dve, j * 2 + s, n)
                        t = slice(n * TT, (n + 1) * TT)
                        ins = dve.tensor_tensor(Rt[:, s, t], pan.acc[:, n, 0:TT], L[:, s, t], ALU.mult)
                        ins.then_inc(pan.free, 1)
                    dve.wait_ge(pan.free, (j * 2 + s) * NT + 2 * NT)
                    dve.sem_inc(s_Rt, 1)


def stage_k(net):
    nc, io = net.nc, net.io
    with ExitStack() as ctx:
        def sb(name, shape, dt=F32):
            return ctx.enter_context(nc.sbuf_tensor(f"k_{name}", shape, dt))

        def sem(name):
            return net.semaphore(f"k_{name}")

        mix = Mix(net, ctx, "k", 2)
        pan = Panels(net, ctx, "kp")
        A, L, Lm, Rt = (sb(n, [128, 2, TOK]) for n in ("a", "L", "Lm", "Rt"))
        k, sq, inv, am, bq, bs = (sb(n, [128, TOK]) for n in ("k", "sq", "inv", "am", "bq", "bs"))
        omka = sb("omka", [128, DB])
        M = sb("M", [128, NCH, C])
        pM = ctx.enter_context(nc.psum_tensor("k_pM", [128, NCH, C], F32))
        s_M, s_Mev, s_Mst = sem("M"), sem("Mev"), sem("Mst")
        ps = ctx.enter_context(nc.psum_tensor("k_ps", [128, NT, 512], F32))
        s_ld, s_st, s_bst = [sem("ld0"), sem("ld1")], [sem("st0"), sem("st1")], sem("bst")
        s_sq, s_exp, s_ln, s_inv, s_bsev = sem("sq"), sem("exp"), sem("ln"), sem("inv"), sem("bsev")
        s_m, s_out, s_bq, s_dv = sem("max"), sem("out"), sem("bonus"), sem("dv")
        s_ss, s_bsum = sem("ss"), sem("bsum")
        w = io["rw_wk"][0]
        headsum = c_(net, "headsum")
        DV = 8
        block = ctx.enter_context(nc.Block())

        def col(name, b):
            at = PARAM_AT[name]
            return net.param[:, bass.ds(b + at, 1)]

        @block.sync
        def _(sp):
            def body(b, s, i):
                pan.load(sp, b, s, panel_of(w, b * 128))
                sp.wait_ge(s_out, b + 1)
                sp.wait_ge(s_M, b + 1)
                sp.wait_ge(s_st[s], i * 48 + 48)
                for buf, src in ((A, net.sA), (L, net.sL), (Lm, net.sLm), (Rt, net.sRt)):
                    sp.dma_start(buf[:, s, :], row(src, b)).then_inc(s_ld[s], 16)
            around(sp, body)

        @block.gpsimd
        def _(pool):
            with pool.Fori(0, DB // 2) as j:
                for s in range(2):
                    pan.split(pool, j * 2 + s, s, j)

        @block.tensor
        def _(pe):
            def bonus(b, m):
                pe.wait_ge(s_bq, b + 1)
                pe.wait_ge(s_m, m)
                for n in range(NT):
                    ins = pe.matmul(ps[:, n, 0:TT], headsum, bq[:, n * TT:(n + 1) * TT], start=True, stop=True)
                ins.then_inc(s_bsum, 1)

            def systems_ready(b):
                pe.wait_ge(s_out, b + 3)
                pe.wait_ge(s_Mev, b + 1)

            def systems(b, s):
                for c in range(NCH):
                    for h in range(2):
                        r, t = slice(64 * h, 64 * h + 64), slice(c * C, (c + 1) * C)
                        ins = pe.matmul(pM[r, c, :], A[r, s, t], Lm[r, s, t], start=True, stop=True, skip_group_check=True, tile_position=(64 * h, 64 * h))
                ins.then_inc(s_M, 1)

            def squares(b):
                pe.wait_ge(s_bsev, b + 1)
                for n in range(NT):
                    pe.wait_ge(s_sq, b * NT + n + 1)
                    ins = pe.matmul(ps[:, n, 0:TT], headsum, sq[:, n * TT:(n + 1) * TT], start=True, stop=True)
                ins.then_inc(s_ss, 1)

            def body(b, s, i):
                first = isinstance(b, int) and b == 0
                pan.multiply(pe, b, s, net.HH, net.HL, ready=(mix.s_lo, 1))
                if not first:
                    systems_ready(b - 1)
                squares(b)
                if not first:
                    systems(b - 1, 1 - s)
                    bonus(b - 1, b + 2)
            around(pe, body)
            systems_ready(DB - 1)
            pe.wait_ge(s_bsev, DB + 1)
            bonus(DB - 1, DB + 1)
            systems(DB - 1, 1)

        @block.scalar
        def _(act):
            mix.act(act)

            def bonus_out(b):
                act.wait_ge(s_bsum, b + 2)
                act.wait_ge(s_bst, b * 16 + 16)
                act.activation(tiles(bs[:]), ps[:, :, 0:TT], ACT.Copy).then_inc(s_bsev, 1)
                act.wait_ge(s_bsev, b + 3)
                act.dma_start(row(net.sBS, b), bs[:]).then_inc(s_bst, 16)

            def save_systems(b):
                act.wait_ge(s_Mev, b + 2)
                act.dma_start(net.sM[:, bass.ds(b, 1)].rearrange("c a p t -> p c (a t)"), M[:]).then_inc(s_Mst, 16)

            def body(b, s, i):
                first = isinstance(b, int) and b == 0
                act.wait_ge(s_m, b + 1)
                pan.summed(act, b, NT - 1)
                for n in range(NT):
                    t = slice(n * TT, (n + 1) * TT)
                    act.activation(sq[:, t], pan.acc[:, n, 0:TT], ACT.Square, scale=col("rw_kk", b)).then_inc(s_sq, 1)
                act.wait_ge(s_out, b + 2)
                for n in range(NT):
                    t = slice(n * TT, (n + 1) * TT)
                    act.activation(k[:, t], pan.acc[:, n, 0:TT], ACT.Copy).then_inc(pan.free, 1)
                act.wait_ge(s_m, b + 2)
                act.activation(inv[:], sq[:], ACT.Ln).then_inc(s_ln, 1)
                act.wait_ge(s_ln, b + 1)
                act.activation(inv[:], inv[:], ACT.Exp, scale=-0.5).then_inc(s_inv, 1)
                act.wait_ge(s_ld[s], i * 64 + 64)
                act.activation(blk(net.pend, b), L[:, s, C - 1:SEQ:C], ACT.Exp).then_inc(s_exp, 1)
                act.activation(blk(net.Ps, b), L[:, s, SEQ:TOK], ACT.Exp).then_inc(s_exp, 1)
                act.wait_ge(s_exp, b * 4 + 2)
                act.activation(L[:, s, :], L[:, s, :], ACT.Exp, scale=-1.0).then_inc(s_exp, 1)
                act.activation(Lm[:, s, :], Lm[:, s, :], ACT.Exp).then_inc(s_exp, 1)
                if not first:
                    bonus_out(b - 1)
                act.wait_ge(s_out, b + 3)
                if not first:
                    save_systems(b - 1)
                for dst, src in ((net.sAt, Lm[:, s, :]), (net.sBt, A[:, s, :]), (net.sKt, am[:])):
                    act.dma_start(row(dst, b), src).then_inc(s_st[s], 16)
            around(act, body)
            bonus_out(DB - 1)
            save_systems(DB - 1)
            act.wait_ge(s_Mst, 16 * DB + 16)
            for s in range(2):
                act.wait_ge(s_st[s], 5 * 48)
            act.wait_ge(s_bst, 16 * DB + 16)

        @block.vector
        def _(dve):
            dve.sem_inc(pan.low, pan.LOW0)
            dve.sem_inc(pan.done, pan.DONE0)
            dve.sem_inc(pan.free, NT)
            dve.sem_inc(s_out, 2)
            dve.sem_inc(s_bsev, 2)
            dve.sem_inc(s_m, 1)
            dve.sem_inc(s_bsum, 1)
            mix.dve(dve)
            dve.sem_inc(s_bst, 16)
            dve.sem_inc(s_M, 2)
            dve.sem_inc(s_Mev, 1)
            dve.sem_inc(s_Mst, 16)
            for s in range(2):
                dve.sem_inc(s_st[s], 48)
            ka = net.param[:, PARAM_AT["rw_ka"]:PARAM_AT["rw_ka"] + DB]
            dve.tensor_scalar(omka[:], ka, -1.0, 1.0, ALU.mult, ALU.add).then_inc(s_dv, 1)

            at = CONST_AT["lt"]
            lt = net.const[:, at:at + C].unsqueeze(1).to_broadcast([128, NCH, C])

            def mask_systems(b):
                dve.wait_ge(s_M, b + 3)
                dve.wait_ge(s_Mst, b * 16 + 16)
                dve.tensor_tensor(M[:], pM[:], lt, ALU.mult).then_inc(s_Mev, 1)

            dve.wait_ge(s_dv, 1)

            def body(b, s, i):
                ch = Chain(dve, s_dv, DV, b, 1)
                a, e2, e1 = A[:, s, :], L[:, s, :], Lm[:, s, :]
                dve.wait_ge(s_ss, b + 1)
                dve.tensor_scalar(tiles(sq[:]), ps[:, :, 0:TT], 1e-24, float(2 ** 20), ALU.max, ALU.mult).then_inc(s_m, 1)
                dve.wait_ge(s_ld[s], i * 64 + 64)
                dve.wait_ge(pan.free, b * NT + 2 * NT)
                dve.wait_ge(s_st[1 - s], (i + s) * 48 + 48)
                ch.link(dve.tensor_scalar(am[:], a, col("rw_ka", b), omka[:, bass.ds(b, 1)], ALU.mult, ALU.add))
                ch.link(dve.tensor_tensor(am[:], am[:], k[:], ALU.mult))
                ch.link(dve.tensor_scalar(k[:], k[:], col("rw_kk", b), 1024.0, ALU.mult, ALU.mult))
                if not (isinstance(b, int) and b == 0):
                    mask_systems(b - 1)
                dve.wait_ge(s_inv, b + 1)
                ch.link(dve.tensor_tensor(k[:], k[:], inv[:], ALU.mult))
                dve.wait_ge(s_exp, b * 4 + 4)
                ch.link(dve.tensor_tensor(a, a, k[:], ALU.mult))
                ch.link(dve.tensor_tensor(am[:], am[:], e2, ALU.mult))
                ch.link(dve.tensor_tensor(a, a, e2, ALU.mult))
                dve.wait_ge(s_bsum, b + 1)
                dve.scalar_tensor_tensor(out=bq[:], in0=Rt[:, s, :], scalar=col("rw_rk", b), in1=am[:], op0=ALU.mult, op1=ALU.mult).then_inc(s_bq, 1)
                ch.link(dve.scalar_tensor_tensor(out=e1, in0=k[:], scalar=-1.0, in1=e1, op0=ALU.mult, op1=ALU.mult))
                dve.wait_ge(s_bq, b + 1)
                dve.sem_inc(s_out, 1)
                assert ch.n == DV
            around(dve, body)
            mask_systems(DB - 1)


def around(eng, body):
    body(0, 0, 0)
    with eng.Fori(0, DB // 2 - 1) as i:
        body(i * 2 + 1, 1, i)
        body(i * 2 + 2, 0, i + 1)
    body(DB - 1, 1, DB // 2 - 1)


def stage_v(net):
    nc, io = net.nc, net.io
    with ExitStack() as ctx:
        def sb(name, shape, dt=F32):
            return ctx.enter_context(nc.sbuf_tensor(f"v_{name}", shape, dt))

        def sem(name):
            return net.semaphore(f"v_{name}")

        pan = Panels(net, ctx, "vp")
        v, bs = sb("v", [128, 2, TOK]), sb("bs", [128, 2, TOK])
        tok, stok = sb("tok", [128, 2, 4, 128]), sb("stok", [DEC, 128])
        Z, tmp = sb("Z", [128, 2, C * C]), sb("tmp", [128, 2, 1 + TOK])
        mix = Mix(net, ctx, "v", 3, buf=v, hx=tmp)
        tb = [ctx.enter_context(nc.psum_tensor(f"v_tb{i}", [128, 4, 128], F32)) for i in range(3)]
        s_bs, s_v, s_bv, s_bvst = [sem("bs0"), sem("bs1")], sem("v"), sem("bv"), [sem("bvst0"), sem("bvst1")]
        s_t, s_tev, s_vst, s_M, s_z, s_diag, s_zst = sem("t"), sem("tev"), sem("vst"), sem("M"), sem("z"), sem("diag"), sem("zst")
        ada = Ada(net, ctx, "ada1")
        s_mod = sem("mod")
        A0 = 2
        G0 = 1
        NG = 2 * Ada.PER_LAYER - G0
        ident = c_(net, "ident")
        w = io["rw_wv"][0]
        half = NCH // 2
        systems = lambda t: t.rearrange("(g c) b (r s) t -> g (c b r) (s t)", g=2, r=2)
        block = ctx.enter_context(nc.Block())

        @block.sync
        def _(sp):

            def body(b, s, i, ada_from=None):
                sp.wait_ge(s_bvst[s], i * 16 + 16)
                sp.dma_start(bs[:, s, :], row(net.sBS, b)).then_inc(s_bs[s], 16)
                if not (isinstance(b, int) and b == DB - 1):
                    pan.load(sp, b + 1, 1 - s, panel_of(w, b * 128 + 128))
                if ada_from:
                    ada.load(sp, b - A0, *ada_from)

            pan.load(sp, 0, 0, panel_of(w, 0))
            for g in range(2):
                sp.dma_start(Z[:, g, :], systems(net.sM)[g]).then_inc(s_M, 16)
            for b in range(A0):
                body(b, b, 0)
            with sp.Fori(1, DB // 2 - 1) as i:
                for s in range(2):
                    body(i * 2 + s, s, i, (i - 1, (1 + s) * Ada.GROUP))
            body(DB - 2, 0, DB // 2 - 1, (1, 0))
            body(DB - 1, 1, DB // 2 - 1)
            for g in range(2):
                sp.wait_ge(s_z, 4 * (C - 2) - 1 + g)
                sp.wait_ge(s_diag, 1)
                sp.dma_start(systems(net.sT)[g], Z[:, g, :]).then_inc(s_zst, 16)
            sp.wait_ge(s_zst, 32)

        @block.gpsimd
        def _(pool):
            def product(b, s, i):
                pool.wait_ge(s_v, b * NT + NT)
                pool.wait_ge(s_bs[s], i * 16 + 16)
                pool.tensor_tensor(bs[:, s, :], bs[:, s, :], v[:, s, :], ALU.mult).then_inc(s_bv, 1)

            def body(b, s, i):
                pan.split(pool, b, s, i)
                if not (isinstance(b, int) and b == 0):
                    product(b - 1, 1 - s, i + s - 1)
            around(pool, body)
            product(DB - 1, 1, DB // 2 - 1)

        @block.tensor
        def _(pe):
            def turn(b, s):
                pe.wait_ge(s_v, b * NT + NT)
                for h in range(2):
                    pe.wait_ge(s_tev, b * 3 + h + 1)
                    for q in range(4):
                        t = (4 * h + q) * 128
                        ins = pe.transpose(tb[h][:, q, :], v[:, s, t:t + 128], ident)
                    ins.then_inc(s_t, 1)
                pe.wait_ge(s_tev, b * 3 + 3)
                pe.transpose(tb[2][0:DEC, 0, :], v[:, s, SEQ:TOK], ident).then_inc(s_t, 1)

            def body(b, s, with_ada=False):
                pan.multiply(pe, b, s, net.HH, net.HL, ready=(mix.s_lo, 1))
                if with_ada:
                    ada.multiply(pe, b - A0)
                if not (isinstance(b, int) and b == 0):
                    turn(b - 1, 1 - s)
                if with_ada:
                    ada.turn(pe, b - A0)

            pe.sem_inc(ada.s_used, ada.SLOTS)
            for b in range(A0):
                body(b, b)
            with pe.Fori(1, DB // 2 - 1) as i:
                for s in range(2):
                    body(i * 2 + s, s, True)
            body(DB - 2, 0, True)
            body(DB - 1, 1)
            turn(DB - 1, 1)

        @block.scalar
        def _(act):
            mix.act(act)

            def out(b):
                act.wait_ge(s_vst, b * 48 + 48)
                for h in range(2):
                    act.wait_ge(s_t, b * 3 + h + 1)
                    act.activation(tok[:, h], tb[h][:], ACT.Copy).then_inc(s_tev, 1)
                act.wait_ge(s_t, b * 3 + 3)
                act.activation(stok[:], tb[2][0:DEC, 0, :], ACT.Copy).then_inc(s_tev, 1)
                act.wait_ge(s_tev, b * 3 + 6)
                cols = net.sV[:, bass.ds(b * 128, 128)]
                for h in range(2):
                    act.dma_start(cols[512 * h:512 * h + 512].rearrange("(q p) c -> p q c", p=128), tok[:, h]).then_inc(s_vst, 16)
                act.dma_start(cols[SEQ:TOK], stok[:]).then_inc(s_vst, 16)

            def product_out(b, s):
                act.wait_ge(s_bv, b + 1)
                act.dma_start(row(net.sBV, b), bs[:, s, :]).then_inc(s_bvst[s], 16)

            def body(b, s, i, ada_to=None):
                if not (isinstance(b, int) and b < 2):
                    act.wait_ge(s_bv, b - 1)
                    act.wait_ge(s_t, b * 3 - 3)
                for n in range(NT):
                    t = slice(n * TT, (n + 1) * TT)
                    pan.summed(act, b, n)
                    act.activation(v[:, s, t], pan.acc[:, n, 0:TT], ACT.Copy).then_inc(s_v, 1)
                act.wait_ge(s_v, b * NT + NT)
                act.sem_inc(pan.free, NT)
                if ada_to is not None:
                    ada.strips_out(act, b - A0)
                if not (isinstance(b, int) and b == 0):
                    out(b - 1)
                    product_out(b - 1, 1 - s)
                if ada_to is not None:
                    ada.turned_out(act, b - A0, ada_to)

            for b in range(A0):
                body(b, b, 0)
            with act.Fori(1, DB // 2 - 1) as i:
                for s in range(2):
                    body(i * 2 + s, s, i, (i - 1) * N_ADA * DB + (1 + s) * 2 * DB)
            body(DB - 2, 0, DB // 2 - 1, N_ADA * DB)
            body(DB - 1, 1, DB // 2 - 1)
            out(DB - 1)
            product_out(DB - 1, 1)
            act.wait_ge(s_vst, DB * 48 + 48)
            for s in range(2):
                act.wait_ge(s_bvst[s], 16 * (DB // 2) + 16)

        @block.vector
        def _(dve):
            dve.sem_inc(pan.low, pan.LOW0)
            dve.sem_inc(pan.done, pan.DONE0)
            dve.sem_inc(pan.free, NT)
            dve.sem_inc(s_tev, 3)
            dve.sem_inc(s_vst, 48)
            dve.sem_inc(ada.s_strip, 1)
            dve.sem_inc(ada.s_mod, 1)
            for s in range(2):
                dve.sem_inc(s_bvst[s], 16)
            mix.dve(dve)
            dve.wait_ge(s_M, 32)
            n = 0
            for s in range(1, C - 1):
                for g in range(2):
                    z = Z[:, g, :].rearrange("p (u t) -> p u t", t=C)
                    if n >= 2:
                        dve.wait_ge(s_z, n - 1)
                    shape = [128, s, C - 1 - s]
                    p = tmp[:, g, 0:s * (C - 1 - s)].rearrange("p (u t) -> p u t", u=s)
                    dve.tensor_tensor(p, z[:, 0:s, s:s + 1].to_broadcast(shape), z[:, s:s + 1, s + 1:C].to_broadcast(shape), ALU.mult).then_inc(s_z, 1)
                    n += 1
                for g in range(2):
                    z = Z[:, g, :].rearrange("p (u t) -> p u t", t=C)
                    shape = [128, s, C - 1 - s]
                    p = tmp[:, g, 0:s * (C - 1 - s)].rearrange("p (u t) -> p u t", u=s)
                    dve.wait_ge(s_z, n - 1)
                    dve.tensor_tensor(z[:, 0:s, s + 1:C], z[:, 0:s, s + 1:C], p, ALU.add).then_inc(s_z, 1)
                    n += 1
            dve.memset(Z[:, :, 0:C * C:C + 1], 1.0).then_inc(s_diag, 1)
            dve.wait_ge(ada.s_mod, NG + 1)
            add_ada_bias(dve, net, G0 * 2 * DB, NG * 2 * DB, s_mod)
            dve.wait_ge(s_mod, 1)
            for slot in range(1, 4):
                make_gain(dve, net, slot, s_mod)
            dve.wait_ge(s_mod, 4)


class Samples:

    ROWS = HD // NCH
    LINKS = 9

    def __init__(self, net, ctx):
        nc = net.nc
        self.net = net

        def sb(name, shape):
            return ctx.enter_context(nc.sbuf_tensor(f"step_{name}", shape, F32))

        sem = lambda name: net.semaphore(f"step_{name}")
        self.cols = sb("cols", [128, 4, DB, DEC])
        self.rows = sb("rows", [DEC, 5, D])
        self.vec = sb("vec", [128, 6, HD])
        self.S = sb("S", [128, HD, HD])
        self.t1, self.t2, self.t3 = (sb(n, [128, self.ROWS, HD]) for n in ("t1", "t2", "t3"))
        self.sa, self.y = sb("sa", [128, self.ROWS]), sb("y", [128, HD])
        self.s_in, self.s_S, self.s_t, self.s_tev = sem("in"), sem("S"), sem("t"), sem("tev")
        self.s_rows, self.s_vec, self.s_dv, self.s_out = sem("rows"), sem("vec"), sem("dv"), sem("out")

    def load(self, sp):
        net = self.net
        for i, src in enumerate((net.sAt, net.sRt, net.sBt, net.sKt)):
            sp.dma_start(self.cols[:, i], src[:, :, SEQ:TOK].rearrange("b p t -> p b t")).then_inc(self.s_in, 16)
        sp.dma_start(self.S[:], net.io["state_wkv"][0].rearrange("s h i j -> (s h) i j")).then_inc(self.s_S, 16)
        sp.dma_start(self.vec[:, 5, :], net.sV[SEQ:TOK].rearrange("s (h d) -> (s h) d", d=HD)).then_inc(self.s_vec, 16)

    def turn(self, pe, banks):
        pe.wait_ge(self.s_in, 64)
        for n in range(10):
            i, h = n // 2, n % 2
            if n >= 2:
                pe.wait_ge(self.s_tev, n - 1)
            for q in range(4):
                src = self.cols[:, i, 4 * h + q, :] if i < 4 else self.net.Ps[:, 4 * h + q, :]
                ins = pe.transpose(banks[n % 2][0:DEC, q, :], src, c_(self.net, "ident"))
            ins.then_inc(self.s_t, 1)
        pe.wait_ge(self.s_tev, 10)

    def spread(self, act, banks):
        for n in range(10):
            act.wait_ge(self.s_t, n + 1)
            act.activation(self.rows[:, n // 2, (n % 2) * 512:(n % 2) * 512 + 512].rearrange("s (q c) -> s q c", q=4), banks[n % 2][0:DEC], ACT.Copy).then_inc(self.s_tev, 1)
        act.wait_ge(self.s_tev, 10)
        act.dma_start(self.net.sSmp.rearrange("i s c -> s i c"), self.rows[:]).then_inc(self.s_rows, 16)
        act.wait_ge(self.s_rows, 16)
        for i in range(5):
            act.dma_start(self.vec[:, i, :], self.net.sSmp[i].rearrange("s (h d) -> (s h) d", d=HD)).then_inc(self.s_vec, 16)

    def step(self, dve, c, part):
        At, Rt, Bt, Kt, P, V = (self.vec[:, i, :] for i in range(6))
        shape = [128, self.ROWS, HD]
        along_j = lambda x: x.unsqueeze(1).to_broadcast(shape)
        along_i = lambda x: x.unsqueeze(2).to_broadcast(shape)
        rows = bass.ds(c * self.ROWS, self.ROWS)
        S, t1, t2, t3, sa, y = self.S[:, rows, :], self.t1[:], self.t2[:], self.t3[:], self.sa[:], self.y[:, rows]
        work = [
            lambda: dve.tensor_tensor(t1, S, along_j(At), ALU.mult),
            lambda: dve.tensor_tensor(t3, along_i(V[:, rows]), along_j(Kt), ALU.mult),
            lambda: dve.tensor_reduce(sa, t1, AX, ALU.add),
            lambda: dve.tensor_tensor(S, S, t3, ALU.add),
            lambda: dve.tensor_tensor(t2, along_i(sa), along_j(Bt), ALU.mult),
            lambda: dve.tensor_tensor(S, S, t2, ALU.add),
            lambda: dve.tensor_tensor(t1, S, along_j(Rt), ALU.mult),
            lambda: dve.tensor_reduce(y, t1, AX, ALU.add),
            lambda: dve.tensor_tensor(S, S, along_j(P), ALU.mult),
        ]
        assert len(work) == self.LINKS
        reads_last = (0, 2, 3, 4, 5, 6, 7, 8)
        for n in range(3 * part, 3 * part + 3):
            if n in reads_last:
                dve.wait_ge(self.s_dv, c * self.LINKS + n + 1)
            work[n]().then_inc(self.s_dv, 1)

    def store(self, sp):
        sp.wait_ge(self.s_dv, NCH * self.LINKS + 1)
        sp.dma_start(self.net.io["out_wkv_sample"][0].rearrange("s h i j -> (s h) i j"), self.S[:]).then_inc(self.s_out, 16)
        sp.dma_start(self.net.sY[SEQ:TOK].rearrange("s (h d) -> (s h) d", d=HD), self.y[:]).then_inc(self.s_out, 16)
        sp.wait_ge(self.s_out, 32)


def stage_scan(net):
    nc, io = net.nc, net.io
    Q = DB // 2
    BODY = 4
    with ExitStack() as ctx:
        def sb(name, shape, dt=F32):
            return ctx.enter_context(nc.sbuf_tensor(f"c_{name}", shape, dt))

        def sem(name):
            return net.semaphore(f"c_{name}")

        ARI = sb("ARI", [128, 2, DB, 3, 2, C])
        BK = sb("BK", [128, 2, 2, 2, DB, 128])
        Z = sb("Z", [128, 2, 2, DB, C])
        V = sb("V", [128, 2, 2, DB, 128])
        G = sb("G", [128, 2, DB, 5, C])
        S, U, SA = sb("S", [128, DB, 128]), sb("U", [128, DB, 128]), sb("SA", [128, DB, 128])
        Sd = sb("Sd", [128, DB, 128])
        eye = sb("eye", [128, C])
        Y = sb("Y", [128, 2, Q, 128])
        St = sb("St", [128, DB, 128])
        pU, pSA, pD, pY, pB, pT = (ctx.enter_context(nc.psum_tensor(f"c_p{n}", [128, Q, 128], F32)) for n in ("U", "A", "D", "Y", "B", "T"))
        pK = ctx.enter_context(nc.psum_tensor("c_pK", [128, 2, 512], F32))
        smp = Samples(net, ctx)
        s_zero, s_zero2, s_ld = sem("zero"), sem("zero2"), [sem("ld0"), sem("ld1")]
        s_U, s_SA, s_D, s_Y, s_G, s_Gev = sem("U"), sem("SA"), sem("D"), sem("Y"), sem("G"), sem("Gev")
        s_Ua, s_Ud, s_Sa, s_Sd, s_S = sem("Ua"), sem("Ud"), sem("Sa"), sem("Sd"), sem("S")
        s_dec, s_dS, s_eye = sem("dec"), sem("dS"), sem("eye")
        s_Yev, s_yst = sem("Yev"), [sem("yst0"), sem("yst1")]
        s_T, s_Tev, s_out = sem("T"), sem("Tev"), sem("out")
        ident = c_(net, "ident")
        lt_at, le_at = CONST_AT["lt"], CONST_AT["le"]
        maskK = net.const[:, lt_at:lt_at + 192].unsqueeze(1).unsqueeze(1).to_broadcast([128, 2, 2, 192])
        maskB = net.const[:, le_at:le_at + 128].unsqueeze(1).to_broadcast([128, 4, 128])
        LOADS = 15
        Y0 = 3
        block = ctx.enter_context(nc.Block())

        def chunks(eng, work):
            with eng.Fori(0, NCH // BODY - 1) as i:
                for k in range(BODY):
                    work(i * BODY + k, k, i, False)
            for k in range(BODY):
                work(NCH - BODY + k, k, NCH // BODY - 1, k == BODY - 1)

        @block.sync
        def _(sp):
            smp.load(sp)
            sp.wait_ge(s_zero, 4)
            sp.wait_ge(s_zero2, 2)
            with sp.Fori(0, NCH // BODY) as i:
                for s in range(2):
                    two = i * 2 + s
                    sp.wait_ge(s_Y, two * 2 + 1)
                    t = bass.ds(two * 2 * C, 2 * C)
                    for n, src in enumerate((net.sAt, net.sRt)):
                        sp.dma_start(ARI[:, s, :, n].rearrange("p b c t -> p b (c t)"), src[:, :, t].rearrange("b p t -> p b t")).then_inc(s_ld[s], 16)
                    for n, src in enumerate((net.sBt, net.sKt)):
                        for h in range(2):
                            r = slice(64 * h, 64 * h + 64)
                            for c in range(2):
                                sp.dma_start(BK[r, s, c, n, :, r], src[:, r, bass.ds(two * 2 * C + c * C, C)].rearrange("b p t -> p b t")).then_inc(s_ld[s], 16)
                    for c in range(2):
                        rows = net.sV[bass.ds(two * 2 * C + c * C, C)].rearrange("t (b h d) -> h t b d", h=2, d=HD)
                        for h in range(2):
                            r = slice(64 * h, 64 * h + 64)
                            sp.dma_start(V[r, s, c, :, r], rows[h]).then_inc(s_ld[s], 16)
                    sp.dma_start(Z[:, s].rearrange("p c b t -> p (c b) t"), net.sT[bass.ds(two * 2, 2)].rearrange("c b p t -> p (c b) t")).then_inc(s_ld[s], 16)

            smp.store(sp)

        @block.gpsimd
        def _(pool):
            pool.memset(BK[:, 1], 0.0).then_inc(s_zero2, 1)
            pool.memset(V[:], 0.0).then_inc(s_zero2, 1)
            pool.wait_ge(s_eye, 2)

            def work(c, k, i, last):
                s, cc = k // 2, k % 2
                decay = net.pend[:, :, bass.ds(c, 1)]
                pool.wait_ge(s_S, c + 1)
                pool.wait_ge(s_D, c + 1)
                if not last:
                    diagonal(c + 1, (k + 1) % BODY)
                pool.tensor_tensor(Sd[:], S[:], decay.to_broadcast([128, DB, 128]), ALU.mult).then_inc(s_dS, 1)

            def diagonal(c, k):
                pool.wait_ge(s_Y, c + 1)
                pool.tensor_tensor(ARI[:, k // 2, :, 2, k % 2, :], eye[:].unsqueeze(1).to_broadcast([128, DB, C]),
                                   net.pend[:, :, bass.ds(c, 1)].to_broadcast([128, DB, C]), ALU.mult).then_inc(s_dec, 1)

            diagonal(0, 0)
            chunks(pool, work)

        @block.tensor
        def _(pe):
            def mm(out, b, lhsT, rhs, start, stop):
                h = b % 2
                return pe.matmul(out[64 * h:64 * h + 64, b // 2, :], lhsT, rhs, start=start, stop=stop, skip_group_check=True, tile_position=(0, 64 * h))

            def grams(c, k, i, half):
                s, cc = k // 2, k % 2
                if half == 0 and cc == 0:
                    pe.wait_ge(s_ld[s], i * 16 * LOADS + 16 * LOADS)
                pe.wait_ge(s_dec, c + 1)
                pe.wait_ge(s_Gev, c * 4 + half * 2 + 2)
                for q in range(4):
                    b = 4 * half + q
                    pe.matmul(pB[:, q, :], BK[:, s, cc, 0, b, :], ARI[:, s, b, 1:3, cc, :], start=True, stop=True, skip_group_check=True)
                    ins = pe.matmul(pK[:, q // 2, (q % 2) * 192:(q % 2) * 192 + 192], BK[:, s, cc, 1, b, :], ARI[:, s, b, :, cc, :], start=True, stop=True, skip_group_check=True)
                ins.then_inc(s_G, 1)

            def chunk(c, k, i, last):
                s, cc, g = k // 2, k % 2, k % 2
                pe.wait_ge(s_S, c + 1)
                pe.wait_ge(s_Ua, c + 1)
                pe.wait_ge(s_Ud, c + 1)
                for b in range(DB):
                    mm(pU, b, ARI[:, s, b, 0, cc, :], S[:, b, :], b < 2, False)
                pe.wait_ge(s_Gev, c * 4 + 6)
                for b in range(DB):
                    ins = mm(pU, b, G[:, g, b, 2, :], V[:, s, cc, b, :], False, True)
                ins.then_inc(s_U, 1)
                ahead = (c + 1, (k + 1) % BODY, i + (k + 1) // BODY)
                if not last:
                    grams(*ahead, 0)
                pe.wait_ge(s_Ua, c + 2)
                pe.wait_ge(s_Ud, c + 2)
                for b in range(DB):
                    ins = mm(pSA, b, Z[:, s, cc, b, :], U[:, b, :], b < 2, True)
                ins.then_inc(s_SA, 1)
                pe.wait_ge(s_Yev, c + 1)
                for b in range(DB):
                    mm(pD, b, G[:, g, b, 4, :], V[:, s, cc, b, :], b < 2, False)
                for b in range(DB):
                    mm(pY, b, ARI[:, s, b, 1, cc, :], S[:, b, :], b < 2, False)
                pe.wait_ge(s_Sa, c + 2)
                pe.wait_ge(s_Sd, c + 2)
                for b in range(DB):
                    ins = mm(pD, b, G[:, g, b, 1, :], SA[:, b, :], False, True)
                ins.then_inc(s_D, 1)
                for b in range(DB):
                    mm(pY, b, G[:, g, b, 3, :], V[:, s, cc, b, :], False, False)
                    ins = mm(pY, b, G[:, g, b, 0, :], SA[:, b, :], False, True)
                ins.then_inc(s_Y, 1)
                if not last:
                    grams(*ahead, 1)

            smp.turn(pe, (pT, pY))
            for half in range(2):
                grams(0, 0, 0, half)
            chunks(pe, chunk)
            pe.wait_ge(s_S, NCH + 1)
            for n in range(2):
                pe.wait_ge(s_Tev, n + 1)
                for q in range(4):
                    ins = pe.transpose(pT[:, q, :], S[:, 4 * n + q, :], ident)
                ins.then_inc(s_T, 1)

        def halves(h, out, src):
            for a in range(2):
                r = slice(64 * a, 64 * a + 64)
                yield out[r, h::2, r], src[64 * h:64 * h + 64, :, r]

        @block.scalar
        def _(act):
            smp.spread(act, (pT, pY))

            def work(c, k, i, last):
                s = k % 2
                act.wait_ge(s_U, c + 1)
                for o, p in halves(0, U, pU):
                    ins = act.activation(o, p, ACT.Copy)
                ins.then_inc(s_Ua, 1)
                act.wait_ge(s_SA, c + 1)
                for o, p in halves(0, SA, pSA):
                    ins = act.activation(o, p, ACT.Copy)
                ins.then_inc(s_Sa, 1)
                act.wait_ge(s_Y, c + 1 + Y0)
                if k < 2:
                    act.wait_ge(s_yst[s], i * 64 + 32)
                else:
                    act.wait_ge(s_yst[s], i * 64 + 64)
                act.activation(Y[:, s], pY[:], ACT.Copy).then_inc(s_Yev, 1)
                act.wait_ge(s_Yev, c + 2)
                rows = net.sY[bass.ds(c * C, C)].rearrange("t (q h d) -> h t q d", h=2, d=128)
                for h in range(2):
                    act.dma_start(rows[h], Y[64 * h:64 * h + 64, s]).then_inc(s_yst[s], 16)
            chunks(act, work)
            for n in range(2):
                act.wait_ge(s_T, n + 1)
                act.activation(St[:, 4 * n:4 * n + 4, :], pT[:], ACT.Copy).then_inc(s_Tev, 1)
            act.wait_ge(s_Tev, 3)
            for h in range(2):
                r = slice(64 * h, 64 * h + 64)
                act.dma_start(io["out_wkv_prompt"][0, 0].rearrange("(b h) i j -> h i b j", h=2)[h], St[r, :, r]).then_inc(s_out, 16)
            for s in range(2):
                act.wait_ge(s_yst[s], NCH // 2 * 32 + 32)
            act.wait_ge(s_out, 32)

        @block.vector
        def _(dve):
            for buf in (BK[:, 0], U[:], SA[:], S[:]):
                dve.memset(buf, 0.0).then_inc(s_zero, 1)
            for h in range(2):
                r = slice(64 * h, 64 * h + 64)
                dve.tensor_copy(eye[r], ident[r, r]).then_inc(s_eye, 1)
            dve.wait_ge(s_zero, 4)
            dve.sem_inc(s_S, 1)
            dve.sem_inc(s_Y, Y0)
            dve.sem_inc(s_Gev, 2)
            for x in (smp.s_dv, s_Yev, s_Ua, s_Ud, s_Sa, s_Sd, s_Tev, s_D):
                dve.sem_inc(x, 1)
            for s in range(2):
                dve.sem_inc(s_yst[s], 32)

            def masked(c, g, half):
                dve.wait_ge(s_G, c * 2 + half + 1)
                b = slice(4 * half, 4 * half + 4)
                dve.tensor_tensor(G[:, g, b, 0:2].rearrange("p b i t -> p b (i t)"), pB[:], maskB, ALU.mult).then_inc(s_Gev, 1)
                dve.tensor_tensor(G[:, g, b, 2:5].rearrange("p (q b) i t -> p q b (i t)", q=2), pK[:, :, 0:384].rearrange("p q (b x) -> p q b x", b=2), maskK, ALU.mult).then_inc(s_Gev, 1)

            def work(c, k, i, last):
                g = k % 2
                dve.wait_ge(s_U, c + 1)
                for o, p in halves(1, U, pU):
                    ins = dve.tensor_copy(o, p)
                ins.then_inc(s_Ud, 1)
                if not last:
                    dve.wait_ge(s_Y, c + Y0)
                    masked(c + 1, 1 - g, 0)
                smp.step(dve, c, 0)
                dve.wait_ge(s_SA, c + 1)
                for o, p in halves(1, SA, pSA):
                    ins = dve.tensor_copy(o, p)
                ins.then_inc(s_Sd, 1)
                smp.step(dve, c, 1)
                dve.wait_ge(s_D, c + 2)
                dve.wait_ge(s_dS, c + 1)
                for h in range(2):
                    for (o, p), (d, _) in zip(halves(h, S, pD), halves(h, Sd, pD)):
                        ins = dve.tensor_tensor(o, p, d, ALU.add)
                ins.then_inc(s_S, 1)
                if not last:
                    masked(c + 1, 1 - g, 1)
                smp.step(dve, c, 2)

            for half in range(2):
                masked(0, 0, half)
            dve.wait_ge(smp.s_S, 16)
            dve.wait_ge(smp.s_vec, 96)
            chunks(dve, work)




class Project:

    def __init__(self, net, ctx, tag, w, gate):
        self.net, self.w, self.gate = net, w, gate
        self.pan = Panels(net, ctx, tag)
        self.smp = ctx.enter_context(net.nc.sbuf_tensor(f"{tag}_smp", [128, DEC], F32))
        self.s_smp = net.semaphore(f"{tag}_smp")

    def sp(self, sp):
        with sp.Fori(0, DB // 2) as j:
            for s in range(2):
                self.load(sp, j, s)

    def load(self, sp, j, s):
        self.pan.load(sp, j * 2 + s, s, panel_of(self.w, j * 256 + s * 128))

    def pool(self, pool):
        with pool.Fori(0, DB // 2) as j:
            for s in range(2):
                self.pan.split(pool, j * 2 + s, s, j)

    def pe(self, pe, ready=None):
        with pe.Fori(0, DB // 2) as j:
            for s in range(2):
                self.pan.multiply(pe, j * 2 + s, s, self.net.HH, self.net.HL, ready=ready)

    def dve_start(self, dve):
        dve.sem_inc(self.pan.low, self.pan.LOW0)
        dve.sem_inc(self.pan.done, self.pan.DONE0)
        dve.sem_inc(self.pan.free, NT)

    def dve(self, dve):
        with dve.Fori(0, DB // 2) as j:
            for s in range(2):
                m = j * 2 + s
                add_gated(dve, self.net, self.pan, m, m, self.gate, self.smp[:], self.pan.free, self.s_smp, m)


def stage_rwkv_out(net):
    nc, io = net.nc, net.io
    with ExitStack() as ctx:
        def sb(name, shape, dt=F32):
            return ctx.enter_context(nc.sbuf_tensor(f"o_{name}", shape, dt))

        def sem(name):
            return net.semaphore(f"o_{name}")

        proj = Project(net, ctx, "op", io["rw_wo"][0], mod_part(net, 0, 2))
        rows, sq = sb("rows", [128, 2, D]), sb("sq", [128, D])
        mean, var = sb("mean", [128, HEADS]), sb("var", [128, HEADS])
        yc = sb("yc", [128, DB, TOK])
        bv, g = sb("bv", [128, 2, TOK]), sb("g", [128, 2, TOK])
        tb = [ctx.enter_context(nc.psum_tensor(f"o_tb{i}", [128, 4, 128], F32)) for i in range(4)]
        s_x, s_y, s_root, s_n, s_t, s_tev = sem("x"), [sem("y0"), sem("y1")], sem("root"), sem("n"), sem("t"), sem("tev")
        s_var, s_dv = sem("var"), sem("dv")
        s_bg, s_aff, s_u, s_hi, s_lo = [sem("bg0"), sem("bg1")], sem("aff"), sem("u"), sem("hi"), sem("lo")
        ident = c_(net, "ident")
        TILES = SEQ // 128
        LINKS = 7
        block = ctx.enter_context(nc.Block())

        def over_tiles(eng, body):
            with eng.Fori(0, TILES // 2) as i:
                for s in range(2):
                    body(i * 2 + s, s, i, 128)
            body(TILES, 0, TILES // 2, DEC)

        @block.sync
        def _(sp):
            def load(t, s, i, n):
                sp.wait_ge(s_t, t * 2 + 2)
                sp.dma_start(rows[0:n, s, :], net.sY[bass.ds(t * 128, n)]).then_inc(s_y[s], 16)
            over_tiles(sp, load)
            sp.dma_start(net.X[:], net.x_saved).then_inc(s_x, 16)
            for s in range(2):
                proj.load(sp, 0, s)
            with sp.Fori(0, DB // 2) as j:
                for s in range(2):
                    sp.wait_ge(s_lo, j * 2 + s + 1)
                    sp.dma_start(bv[:, s, :], row(net.sBV, j * 2 + s)).then_inc(s_bg[s], 16)
                    sp.dma_start(g[:, s, :], row(net.sG, j * 2 + s)).then_inc(s_bg[s], 16)
            with sp.Fori(1, DB // 2) as j:
                for s in range(2):
                    proj.load(sp, j, s)

        @block.gpsimd
        def _(pool):
            proj.pool(pool)

        @block.tensor
        def _(pe):
            pe.sem_inc(s_t, 4)

            def turn(t, s, i, n):
                pe.wait_ge(s_n, t + 1)
                pe.wait_ge(s_tev, t * 2 + 1)
                pe.wait_ge(s_tev, t * 2 + 2)
                for h in range(2):
                    for q in range(4):
                        b = 4 * h + q
                        ins = pe.transpose(tb[2 * s + h][:, q, 0:n], rows[0:n, s, b * 128:(b + 1) * 128], ident[0:n, 0:n])
                    ins.then_inc(s_t, 1)
            over_tiles(pe, turn)
            proj.pe(pe, ready=(s_lo, 3))

        @block.scalar
        def _(act):
            act.sem_inc(s_tev, 4)

            def body(t, s, i, n):
                act.wait_ge(s_var, t + 1)
                act.activation(var[0:n], var[0:n], ACT.Sqrt).then_inc(s_root, 1)
                for h in range(2):
                    act.wait_ge(s_t, t * 2 + h + 5)
                    act.activation(yc[:, 4 * h:4 * h + 4, bass.ds(t * 128, n)], tb[2 * s + h][:, :, 0:n], ACT.Copy).then_inc(s_tev, 1)
            over_tiles(act, body)
            act.wait_ge(s_tev, 4 + 2 * (TILES + 1))
            with act.Fori(0, DB) as b:
                y = blk(yc, b)
                gain, shift = (net.param[:, bass.ds(b + PARAM_AT[n], 1)] for n in ("rw_lnx_g", "rw_lnx_b"))
                act.activation(y, y, ACT.Identity, bias=shift, scale=gain).then_inc(s_aff, 1)
            with act.Fori(0, DB) as b:
                act.wait_ge(s_u, b * 2 + 2)
                act.activation(blk(net.HH, b), blk(yc, b), ACT.Copy).then_inc(s_hi, 1)

        @block.vector
        def _(dve):
            proj.dve_start(dve)
            dve.sem_inc(s_lo, 2)

            def body(t, s, i, n):
                ch = Chain(dve, s_dv, LINKS, t)
                y = rows[0:n, s, :].rearrange("p (h d) -> p h d", d=HD)
                q = sq[0:n].rearrange("p (h d) -> p h d", d=HD)
                m, v = mean[0:n], var[0:n]
                bc = lambda x: x.unsqueeze(2).to_broadcast([n, HEADS, HD])
                dve.wait_ge(s_y[s], i * 16 + 16)
                ch.link(dve.tensor_reduce(m, y, AX, ALU.add))
                ch.link(dve.tensor_scalar(m, m, 1.0 / HD, None, ALU.mult))
                ch.link(dve.tensor_tensor(y, y, bc(m), ALU.subtract))
                ch.link(dve.tensor_tensor(q, y, y, ALU.mult))
                ch.link(dve.tensor_reduce(v, q, AX, ALU.add))
                dve.tensor_scalar(v, v, 1.0 / HD, LNX_EPS, ALU.mult, ALU.add).then_inc(s_var, 1)
                dve.wait_ge(s_root, t + 1)
                ch.link(dve.reciprocal(v, v))
                ch.link(dve.tensor_tensor(y, y, bc(v), ALU.mult))
                dve.sem_inc(s_n, 1)
                assert ch.n == LINKS

            over_tiles(dve, body)
            with dve.Fori(0, DB // 2) as j:
                for s in range(2):
                    b = j * 2 + s
                    y = blk(yc, b)
                    dve.wait_ge(s_aff, b + 1)
                    dve.wait_ge(s_bg[s], j * 32 + 32)
                    dve.tensor_tensor(y, y, bv[:, s, :], ALU.add).then_inc(s_u, 1)
                    dve.wait_ge(s_u, b * 2 + 1)
                    dve.tensor_tensor(y, y, g[:, s, :], ALU.mult).then_inc(s_u, 1)
                    dve.wait_ge(s_u, b * 2 + 2)
                    dve.wait_ge(s_hi, b + 1)
                    dve.tensor_tensor(blk(net.HL, b), y, blk(net.HH, b).bitcast(F32), ALU.subtract).then_inc(s_lo, 1)
            dve.wait_ge(s_x, 16)
            proj.dve(dve)




def stage_qkv(net):
    nc, io = net.nc, net.io
    with ExitStack() as ctx:
        def sb(name, shape, dt=F32):
            return ctx.enter_context(nc.sbuf_tensor(f"q_{name}", shape, dt))

        def sem(name):
            return net.semaphore(f"q_{name}")

        weights(net, ctx, "q")
        pan = Panels(net, ctx, "qp")
        cos, sin = sb("cos", [128, TOK]), sb("sin", [128, TOK])
        kv = sb("kv", [128, 2, TOK])
        tmp = sb("tmp", [128, 2, TT])
        ps = ctx.enter_context(nc.psum_tensor("q_ps", [128, NT, 512], F32))
        norm = Norm(net, ctx, "qn", net.gain[:, 2], mod_part(net, 1, 0), sq=kv, rs=cos, ps=ps)
        tb = [ctx.enter_context(nc.psum_tensor(f"q_tb{i}", [128, 4, 128], F32)) for i in range(2)]
        s_ang, s_x, s_t, s_tev, s_sw, s_rot, s_dv, s_kd = sem("ang"), sem("x"), sem("t"), sem("tev"), sem("sw"), sem("rot"), sem("dv"), sem("kd")
        s_vd = sem("vd")
        ident, swap = c_(net, "ident"), c_(net, "swap")
        w = io["at_wqkv"][0]
        NQ = HEADS * HD
        KVW = KV * HD
        v_at, k_at = NQ + KVW, NQ
        block = ctx.enter_context(nc.Block())

        @block.sync
        def _(sp):
            for p in range(2):
                pan.load(sp, p, p, panel_of(w, v_at + p * 128))
            sp.wait_ge(norm.s_lo, DB)
            sp.dma_start(cos[:], io["const_wide"][:, TOK:2 * TOK]).then_inc(s_ang, 16)
            sp.dma_start(sin[:], io["const_wide"][:, 2 * TOK:3 * TOK]).then_inc(s_ang, 16)
            for p in range(2):
                pan.load(sp, 2 + p, p, panel_of(w, k_at + p * 128))
            with sp.Fori(0, DB // 2) as j:
                for s in range(2):
                    pan.load(sp, j * 2 + s + 4, s, panel_of(w, j * 256 + s * 128))

        @block.gpsimd
        def _(pool):
            with pool.Fori(0, DB // 2 + 2) as j:
                for s in range(2):
                    pan.split(pool, j * 2 + s, s, j)

        @block.tensor
        def _(pe):
            def turn(v):
                pe.wait_ge(s_x, v * NT + NT)
                for n in range(3):
                    pe.wait_ge(s_tev, 3 * v + n + 1)
                    for q in range(4 if n < 2 else 1):
                        cols, t = (128, (4 * n + q) * 128) if n < 2 else (DEC, SEQ)
                        ins = pe.transpose(tb[(3 * v + n) % 2][0:cols, q, :], kv[:, v, t:t + cols], ident)
                    ins.then_inc(s_t, 1)

            def partners(p, x):
                pe.wait_ge(s_x, p * NT + NT)
                for n in range(NT):
                    pe.wait_ge(s_dv, ((p - 3) * NT + n) * 3 + 2 + 3 * NT)
                    ins = pe.matmul(ps[:, n, 0:TT], swap, x[:, n * TT:(n + 1) * TT], start=True, stop=True)
                    ins.then_inc(s_sw, 1)

            norm.pe(pe)
            pan.multiply(pe, 0, 0, net.HH, net.HL, ready=(norm.s_lo, 1))
            pan.multiply(pe, 1, 1, net.HH, net.HL)
            turn(0)
            pan.multiply(pe, 2, 0, net.HH, net.HL)
            turn(1)
            pan.multiply(pe, 3, 1, net.HH, net.HL)
            partners(2, kv[:, 0, :])

            def body(b, s, i):
                pan.multiply(pe, b + 4, s, net.HH, net.HL)
                if isinstance(b, int) and b == 0:
                    partners(3, kv[:, 1, :])
                else:
                    partners(b + 3, blk(net.Q, b - 1))
            around(pe, body)
            partners(DB + 3, net.Q[:, DB - 1, :])

        @block.scalar
        def _(act):
            def add_bias(p, x, at):
                for n in range(NT):
                    pan.summed(act, p, n)
                    act.activation(x[:, n * TT:(n + 1) * TT], pan.acc[:, n, 0:TT], ACT.Identity, bias=net.param[:, bass.ds(at, 1)]).then_inc(s_x, 1)
                act.wait_ge(s_x, p * NT + NT)
                act.sem_inc(pan.free, NT)

            norm.act(act)
            at = PARAM_AT["at_bqkv"]
            for v in range(2):
                add_bias(v, kv[:, v, :], at + v_at // 128 + v)
            for v in range(2):
                for n in range(3):
                    act.wait_ge(s_t, 3 * v + n + 1)
                    bank, cols = tb[(3 * v + n) % 2], slice(v * 128, (v + 1) * 128)
                    if n < 2:
                        act.activation(net.Vt[:, 4 * n:4 * n + 4, cols], bank[:], ACT.Copy).then_inc(s_tev, 1)
                    else:
                        act.activation(net.Vt[0:DEC, 2 * 4, cols], bank[0:DEC, 0, :], ACT.Copy).then_inc(s_tev, 1)
                act.wait_ge(s_vd, v * 4 + 4)
                add_bias(2 + v, kv[:, v, :], at + k_at // 128 + v)
            with act.Fori(0, DB) as b:
                add_bias(b + 4, blk(net.Q, b), b + at)

        @block.vector
        def _(dve):
            dve.sem_inc(pan.low, pan.LOW0)
            dve.sem_inc(pan.done, pan.DONE0)
            dve.sem_inc(pan.free, NT)
            dve.sem_inc(s_tev, 2)
            dve.sem_inc(s_dv, 3 * NT)
            norm.dve(dve)
            for v in range(2):
                dve.wait_ge(s_x, v * NT + NT)
                for h in range(2):
                    for a in range(2):
                        dve.tensor_copy(net.Vd[64 * a:64 * a + 64, 2 * v + h, :], kv[64 * h:64 * h + 64, v, SEQ:TOK]).then_inc(s_vd, 1)
            dve.wait_ge(s_ang, 32)

            def rotate(p, x):
                dve.wait_ge(s_x, p * NT + NT)
                for n in range(NT):
                    t = slice(n * TT, (n + 1) * TT)
                    base = ((p - 2) * NT + n) * 3 + 3 * NT
                    dve.wait_ge(s_sw, (p - 2) * NT + n + 1)
                    dve.wait_ge(s_dv, base)
                    dve.tensor_tensor(tmp[:, n % 2, :], ps[:, n, 0:TT], sin[:, t], ALU.mult).then_inc(s_dv, 1)
                    dve.tensor_tensor(x[:, t], x[:, t], cos[:, t], ALU.mult).then_inc(s_dv, 1)
                    dve.wait_ge(s_dv, base + 2)
                    dve.tensor_tensor(x[:, t], x[:, t], tmp[:, n % 2, :], ALU.add).then_inc(s_dv, 1)

            for k in range(2):
                rotate(2 + k, kv[:, k, :])
                dve.wait_ge(s_dv, (k + 1) * 3 * NT + 3 * NT)
                for h in range(2):
                    for a in range(2):
                        dve.tensor_copy(net.Kd[64 * a:64 * a + 64, 2 * k + h, :], kv[64 * h:64 * h + 64, k, :]).then_inc(s_kd, 1)
            with dve.Fori(0, DB) as b:
                rotate(b + 4, blk(net.Q, b))
            dve.wait_ge(s_dv, 11 * 3 * NT)
            dve.wait_ge(s_kd, 8)


def stage_attend_samples(net):
    nc, io = net.nc, net.io
    with ExitStack() as ctx:
        def sb(name, shape, dt=F32):
            return ctx.enter_context(nc.sbuf_tensor(f"as_{name}", shape, dt))

        def sem(name):
            return net.semaphore(f"as_{name}")

        ck, cv = (sb(n, [WIN, DEC, KV, 2, HD]) for n in ("ck", "cv"))
        KT = sb("KT", [128, 2, KV, WIN])
        qd, pd = sb("qd", [128, DEC, DB, 2]), sb("pd", [128, DEC, DB, 2])
        ST, PT = sb("ST", [WIN, 128]), sb("PT", [WIN, 128])
        R = sb("R", [128, WIN + 1])
        mx, nm, es, den = (sb(n, [128, 1]) for n in ("mx", "nm", "es", "den"))
        sink = sb("sink", [128, 1])
        diag, o, o2 = sb("diag", [128, 128]), sb("o", [128, DEC, DB, 2]), sb("o2", [128, DB, DEC])
        krow, ksrow = sb("krow", [WIN, KV, HD]), sb("ksrow", [DEC, KV, HD])
        tb = [ctx.enter_context(nc.psum_tensor(f"as_tb{i}", [128, 4, 128], F32)) for i in range(2)]
        pST, pR, pB, pO, pK, pKs = (ctx.enter_context(nc.psum_tensor(f"as_p{i}", [128, 512], F32)) for i in range(6))
        s_ck, s_cv, s_sink, s_zero, s_out = sem("ck"), sem("cv"), sem("sink"), sem("zero"), sem("out")
        s_t, s_tev, s_q, s_ST, s_STev, s_R, s_dv = sem("t"), sem("tev"), sem("q"), sem("ST"), sem("STev"), sem("R"), sem("dv")
        s_e, s_P, s_PT, s_PTev, s_O, s_k, s_kev = sem("e"), sem("P"), sem("PT"), sem("PTev"), sem("O"), sem("k"), sem("kev")
        s_hi = sem("hi")
        ident, ones = c_(net, "ident"), c_(net, "ones")
        LAST = SEQ // 128 - 1
        block = ctx.enter_context(nc.Block())

        @block.sync
        def _(sp):
            for buf, name, sm in ((ck, "cache_k", s_ck), (cv, "cache_v", s_cv)):
                src = io[name][0].rearrange("s w k d -> w s k d")
                for h in range(2):
                    for s in range(DEC):
                        sp.dma_start(buf[:, s, :, h, :], src[:, s]).then_inc(sm, 16)
            for name in ("k", "v"):
                sp.dma_start(io[f"out_{name}_sample"][0, :, 0:WIN - 1].rearrange("s w k d -> s (w k d)"), io[f"cache_{name}"][0, :, 1:WIN].rearrange("s w k d -> s (w k d)")).then_inc(s_out, 16)
            sp.dma_start(io["out_v_sample"][0, :, WIN - 1].rearrange("s k d -> s (k d)"), net.Vt[0:DEC, LAST + 1, :]).then_inc(s_out, 16)
            sp.dma_start(io["out_v_prompt"][0, 0].rearrange("w k d -> w (k d)"), net.Vt[:, LAST, :]).then_inc(s_out, 16)
            sp.wait_ge(s_kev, 2)
            sp.dma_start(io["out_k_prompt"][0, 0], krow[:]).then_inc(s_out, 16)
            sp.dma_start(io["out_k_sample"][0, :, WIN - 1], ksrow[:]).then_inc(s_out, 16)
            sp.wait_ge(s_out, 96)

        @block.tensor
        def _(pe):
            for k in range(KV):
                ins = pe.transpose(pK[:, k * HD:(k + 1) * HD], net.Kd[0:64, k, LAST * 128:SEQ], ident[0:64, 0:64])
            ins.then_inc(s_k, 1)
            for k in range(KV):
                ins = pe.transpose(pKs[0:DEC, k * HD:(k + 1) * HD], net.Kd[0:64, k, SEQ:TOK], ident[0:64, 0:64])
            ins.then_inc(s_k, 1)
            pe.wait_ge(s_q, 4)
            pe.wait_ge(s_ck, 2 * DEC * 16)

            def turn(s):
                if s >= 2:
                    pe.wait_ge(s_tev, s - 1)
                for k in range(KV):
                    ins = pe.transpose(tb[s % 2][:, k, :], ck[:, s, k].rearrange("w a d -> w (a d)"), ident)
                ins.then_inc(s_t, 1)

            turn(0)
            for s in range(DEC):
                if s + 1 < DEC:
                    turn(s + 1)
                pe.wait_ge(s_tev, s + 1)
                for k in range(KV):
                    at = s * HEADS + 4 * k
                    ins = pe.matmul(pST[:, at:at + 4], KT[:, s % 2, k, :], qd[:, s, 2 * k:2 * k + 2, :].rearrange("p b a -> p (b a)"), start=True, stop=True, skip_group_check=True)
                ins.then_inc(s_ST, 1)
            pe.wait_ge(s_STev, 1)
            pe.matmul(pR[:, WIN:WIN + 1], pd[:].rearrange("p s b a -> p (s b a)"), ones[:, 0:1], start=True, stop=True)
            pe.transpose(pR[:, 0:WIN], ST[:], ident).then_inc(s_R, 1)
            pe.wait_ge(s_P, 2)
            pe.matmul(pB[:, 0:128], ones, diag[:], start=True, stop=True)
            pe.transpose(pST[:, 128:256], R[:, 0:WIN], ident).then_inc(s_PT, 1)
            pe.wait_ge(s_PTev, 1)
            pe.wait_ge(s_cv, 2 * DEC * 16)
            for s in range(DEC):
                for k in range(KV):
                    at = s * HEADS + 4 * k
                    ins = pe.matmul(pO[:, at:at + 4], cv[:, s, k].rearrange("w a d -> w (a d)"), PT[:, at:at + 4], start=True, stop=True, skip_group_check=True)
            ins.then_inc(s_O, 1)

        @block.scalar
        def _(act):
            for s in range(DEC):
                act.dma_start(sink[s * HEADS:(s + 1) * HEADS, :], io["at_sink"].rearrange("a h -> h a")).then_inc(s_sink, 16)
            act.wait_ge(s_k, 1)
            act.activation(krow[:].rearrange("w k d -> w (k d)"), pK[:, 0:KV * HD], ACT.Copy).then_inc(s_kev, 1)
            act.wait_ge(s_k, 2)
            act.activation(ksrow[:].rearrange("w k d -> w (k d)"), pKs[0:DEC, 0:KV * HD], ACT.Copy).then_inc(s_kev, 1)
            for s in range(DEC):
                act.wait_ge(s_t, s + 1)
                if s >= 2:
                    act.wait_ge(s_ST, s - 1)
                act.activation(KT[:, s % 2], tb[s % 2][:], ACT.Copy).then_inc(s_tev, 1)
            act.wait_ge(s_ST, DEC)
            act.activation(ST[:], pST[:, 0:128], ACT.Copy).then_inc(s_STev, 1)
            act.wait_ge(s_dv, 5)
            act.activation(R[:], R[:], ACT.Exp, bias=nm[:], accum_out=den[:]).then_inc(s_e, 1)
            act.activation(es[:], sink[:], ACT.Exp, bias=nm[:]).then_inc(s_e, 1)
            act.wait_ge(s_PT, 1)
            act.activation(PT[:], pST[:, 128:256], ACT.Copy).then_inc(s_PTev, 1)
            act.wait_ge(s_dv, 11)
            act.activation(net.HH[:, :, SEQ:TOK], o2[:], ACT.Copy).then_inc(s_hi, 1)

        @block.vector
        def _(dve):
            ch = Chain(dve, s_dv)
            dve.memset(qd[:], 0.0).then_inc(s_zero, 1)
            dve.memset(pd[:], 0.0).then_inc(s_zero, 1)
            dve.wait_ge(s_zero, 2)
            for a in range(2):
                r = slice(64 * a, 64 * a + 64)
                q = net.Q[r, :, SEQ:TOK].rearrange("p b s -> p s b")
                dve.tensor_copy(qd[r, :, :, a], q).then_inc(s_q, 1)
                dve.tensor_tensor(pd[r].rearrange("p s (k j) a -> p s k j a", j=2)[:, :, :, :, a], q.rearrange("p s (k j) -> p s k j", j=2),
                                  net.Kd[r, :, SEQ:TOK].rearrange("p k s -> p s k").unsqueeze(3).to_broadcast([64, DEC, KV, 2]), ALU.mult).then_inc(s_q, 1)
            dve.wait_ge(s_R, 1)
            ch.link(dve.tensor_scalar(R[:], pR[:, 0:WIN + 1], SCALE, None, ALU.mult))
            ch.link(dve.tensor_reduce(mx[:], R[:], AX, ALU.max))
            dve.wait_ge(s_sink, DEC * 16)
            ch.link(dve.tensor_tensor(mx[:], mx[:], sink[:], ALU.max))
            ch.link(dve.tensor_scalar(nm[:], mx[:], -1.0, None, ALU.mult))
            dve.sem_inc(s_dv, 1)
            ch.n += 1
            dve.wait_ge(s_e, 2)
            ch.link(dve.tensor_tensor(den[:], den[:], es[:], ALU.add))
            ch.link(dve.reciprocal(den[:], den[:]))
            dve.tensor_scalar(R[:], R[:], den[:], None, ALU.mult).then_inc(s_P, 1)
            dve.wait_ge(s_P, 1)
            dve.tensor_scalar(diag[:], ident, R[:, WIN:WIN + 1], None, ALU.mult).then_inc(s_P, 1)
            dve.wait_ge(s_O, 1)
            new = net.Vd[:].rearrange("p k s -> p s k").unsqueeze(3).to_broadcast([128, DEC, KV, 4])
            ch.link(dve.tensor_tensor(o[:].rearrange("p s (k j) a -> p s k (j a)", j=2), pB[:, 0:128].rearrange("p (s k g) -> p s k g", k=KV, g=4), new, ALU.mult))
            flat = o[:].rearrange("p s b a -> p (s b a)")
            ch.link(dve.tensor_tensor(flat, flat, pO[:, 0:128], ALU.add))
            for a in range(2):
                r = slice(64 * a, 64 * a + 64)
                ch.link(dve.tensor_copy(o2[r], o[r, :, :, a].rearrange("p s b -> p b s")))
            assert ch.n == 11
            dve.wait_ge(s_hi, 1)
            dve.tensor_tensor(net.HL[:, :, SEQ:TOK], o2[:], net.HH[:, :, SEQ:TOK].bitcast(F32), ALU.subtract).then_inc(s_q, 1)
            dve.wait_ge(s_q, 5)


def stage_attend(net):
    nc, io = net.nc, net.io
    TILES = SEQ // 128
    with ExitStack() as ctx:
        def sb(name, shape, dt=F32):
            return ctx.enter_context(nc.sbuf_tensor(f"at_{name}", shape, dt))

        def sem(name):
            return net.semaphore(f"at_{name}")

        mask, sink = sb("mask", [128, 256]), sb("sink", [128, HEADS])
        S = sb("S", [128, 2, 4, 256])
        PT = sb("PT", [128, 4, 2, 128])
        Qs, Vs = sb("Qs", [128, 2, 4, 128]), sb("Vs", [128, 2, 2, HD])
        mx, nm, es, den = (sb(n, [128, 2, 4]) for n in ("mx", "nm", "es", "den"))
        pS = [ctx.enter_context(nc.psum_tensor(f"at_pS{i}", [128, 4, 256], F32)) for i in range(2)]
        pT = ctx.enter_context(nc.psum_tensor("at_pT", [128, 4, 2, 128], F32))
        pO = [ctx.enter_context(nc.psum_tensor(f"at_pO{i}", [128, 2, 128], F32, )) for i in range(2)]
        s_qs, s_vs, s_zero = sem("qs"), sem("vs"), sem("zero")
        s_in, s_s, s_sev, s_nm, s_e, s_P = sem("in"), sem("s"), sem("sev"), sem("nm"), sem("e"), sem("P")
        s_t, s_tev, s_o, s_hi, s_lo, s_dv, s_dv2 = sem("t"), sem("tev"), sem("o"), sem("hi"), sem("lo"), sem("dv"), sem("dv2")
        ident = c_(net, "ident")
        block = ctx.enter_context(nc.Block())

        def steps(eng, work):
            def tile(t, k):
                def at(d):
                    t2, k2 = t + (k + d) // KV, (k + d) % KV
                    return None if isinstance(t, int) and not 0 <= t2 < TILES else (t2, k2)
                work(t, k, at)
            for t in (0, 1):
                for k in range(KV):
                    tile(t, k)
            with eng.Fori(2, TILES - 1) as t:
                for k in range(KV):
                    tile(t, k)
            for k in range(KV):
                tile(TILES - 1, k)

        def keys(t):
            return (1, 0) if isinstance(t, int) and t == 0 else (2, t - 1)

        @block.sync
        def _(sp):
            sp.dma_start(mask[:], io["const_mask"]).then_inc(s_in, 16)
            sp.dma_start(sink[:], io["at_sink"].to_broadcast([128, HEADS])).then_inc(s_in, 16)

        @block.gpsimd
        def _(pool):
            def queries(t, k):
                if not (isinstance(t, int) and t == 0 and k < 2):
                    pool.wait_ge(s_s, t * KV + k - 1)
                for a in range(2):
                    r = slice(64 * a, 64 * a + 64)
                    pool.tensor_copy(Qs[r, k % 2, a::2], net.Q[r, 2 * k:2 * k + 2, bass.ds(t * 128, 128)]).then_inc(s_qs, 1)
                    pool.wait_ge(s_qs, (t * KV + k) * 2 + a + 1)

            pool.memset(Qs[:], 0.0).then_inc(s_zero, 1)
            pool.wait_ge(s_zero, 1)
            queries(0, 0)
            queries(0, 1)

            def work(t, k, at):
                if at(2):
                    queries(*at(2))
                n, first = keys(t)
                if not (isinstance(t, int) and t == 0 and k < 2):
                    pool.wait_ge(s_o, t * KV + k)
                pool.tensor_copy(Vs[:, k % 2, 0:n], net.Vt[:, bass.ds(first, n), k * HD:(k + 1) * HD]).then_inc(s_vs, 1)
            steps(pool, work)

        @block.tensor
        def _(pe):
            def scores(t, k):
                n, first = keys(t)
                s = k % 2
                pe.wait_ge(s_sev, t * KV + k + 1)
                pe.wait_ge(s_qs, (t * KV + k) * 2 + 2)
                for g in range(4):
                    ins = pe.matmul(pS[s][:, g, 0:n * 128], Qs[:, s, g, :], net.Kd[:, k, bass.ds(first * 128, n * 128)], start=True, stop=True, skip_group_check=True)
                ins.then_inc(s_s, 1)

            def turn(t, k):
                n, first = keys(t)
                pe.wait_ge(s_P, t * KV + k + 1)
                pe.wait_ge(s_tev, t * KV + k + 1)
                for g in range(4):
                    for j in range(n):
                        ins = pe.transpose(pT[:, g, j, :], S[:, k % 2, g, j * 128:(j + 1) * 128], ident)
                ins.then_inc(s_t, 1)

            def values(t, k):
                n, first = keys(t)
                pe.wait_ge(s_tev, t * KV + k + 2)
                pe.wait_ge(s_vs, t * KV + k + 1)
                pe.wait_ge(s_lo, t * KV + k + 1)
                for g in range(4):
                    a = g % 2
                    for j in range(n):
                        ins = pe.matmul(pO[k % 2][64 * a:64 * a + 64, g // 2, :], Vs[:, k % 2, j, :], PT[:, g, j, :], start=(j == 0), stop=(j == n - 1), skip_group_check=True, tile_position=(0, 64 * a))
                ins.then_inc(s_o, 1)

            scores(0, 0)
            scores(0, 1)

            def work(t, k, at):
                if at(2):
                    scores(*at(2))
                if at(-1):
                    values(*at(-1))
                turn(t, k)
            steps(pe, work)
            values(TILES - 1, KV - 1)

        @block.scalar
        def _(act):
            def exps(t, k):
                n, first = keys(t)
                s = k % 2
                act.wait_ge(s_nm, (t * KV + k) * 2 + 2)
                for g in range(4):
                    x = S[:, s, g, 0:n * 128]
                    ins = act.activation(x, x, ACT.Exp, bias=nm[:, s, g:g + 1], accum_out=den[:, s, g:g + 1])
                ins.then_inc(s_e, 1)
                act.activation(es[:, s], es[:, s], ACT.Exp).then_inc(s_e, 1)

            def turned(t, k):
                n, first = keys(t)
                act.wait_ge(s_t, t * KV + k + 1)
                act.wait_ge(s_o, t * KV + k + 1)
                act.activation(PT[:, :, 0:n, :], pT[:, :, 0:n, :], ACT.Copy).then_inc(s_tev, 1)

            def high(t, k):
                act.wait_ge(s_o, t * KV + k + 2)
                act.activation(net.HH[:, 2 * k:2 * k + 2, bass.ds(t * 128, 128)], pO[k % 2][:], ACT.Copy).then_inc(s_hi, 1)

            exps(0, 0)

            def work(t, k, at):
                if at(1):
                    exps(*at(1))
                turned(t, k)
                if at(-1):
                    high(*at(-1))
            steps(act, work)
            high(TILES - 1, KV - 1)

        @block.vector
        def _(dve):
            dve.sem_inc(s_sev, 2)
            dve.sem_inc(s_tev, 1)
            dve.sem_inc(s_lo, 2)
            dve.sem_inc(s_o, 1)
            dve.wait_ge(s_in, 32)

            def masked(t, k):
                n, first = keys(t)
                s = k % 2
                u = t * KV + k
                m = mask[:, 256 - n * 128:256].unsqueeze(1).to_broadcast([128, 4, n * 128])
                dve.wait_ge(s_s, u + 1)
                if not (isinstance(t, int) and t == 0 and k < 2):
                    dve.wait_ge(s_t, u - 1)
                dve.scalar_tensor_tensor(out=S[:, s, :, 0:n * 128], in0=pS[s][:, :, 0:n * 128], scalar=SCALE, in1=m, op0=ALU.mult, op1=ALU.add).then_inc(s_sev, 1)
                dve.wait_ge(s_sev, u + 3)
                dve.tensor_reduce(mx[:, s], S[:, s, :, 0:n * 128], AX, ALU.max).then_inc(s_dv, 1)
                dve.wait_ge(s_dv, u * 2 + 1)
                dve.tensor_tensor(mx[:, s], mx[:, s], sink[:, 4 * k:4 * k + 4], ALU.max).then_inc(s_dv, 1)
                dve.wait_ge(s_dv, u * 2 + 2)
                dve.tensor_scalar(nm[:, s], mx[:, s], -1.0, None, ALU.mult).then_inc(s_nm, 1)
                dve.tensor_tensor(es[:, s], sink[:, 4 * k:4 * k + 4], mx[:, s], ALU.subtract).then_inc(s_nm, 1)

            def normal(t, k):
                n, first = keys(t)
                s = k % 2
                u = t * KV + k
                dve.wait_ge(s_e, u * 2 + 2)
                dve.tensor_tensor(den[:, s], den[:, s], es[:, s], ALU.add).then_inc(s_dv2, 1)
                dve.wait_ge(s_dv2, u * 2 + 1)
                dve.reciprocal(den[:, s], den[:, s]).then_inc(s_dv2, 1)
                dve.wait_ge(s_dv2, u * 2 + 2)
                x = S[:, s, :, 0:n * 128]
                dve.tensor_tensor(x, x, den[:, s].unsqueeze(2).to_broadcast([128, 4, n * 128]), ALU.mult).then_inc(s_P, 1)

            def low(t, k):
                dve.wait_ge(s_hi, t * KV + k + 1)
                o = lambda x: x[:, 2 * k:2 * k + 2, bass.ds(t * 128, 128)]
                dve.tensor_tensor(o(net.HL), pO[k % 2][:], o(net.HH).bitcast(F32), ALU.subtract).then_inc(s_lo, 1)

            masked(0, 0)

            def work(t, k, at):
                if at(1):
                    masked(*at(1))
                normal(t, k)
                if at(-2):
                    low(*at(-2))
            steps(dve, work)
            low(TILES - 1, KV - 2)
            low(TILES - 1, KV - 1)
            dve.wait_ge(s_lo, TILES * KV + 2)


def stage_attend_out(net):
    nc, io = net.nc, net.io
    with ExitStack() as ctx:
        weights(net, ctx, "ao")
        proj = Project(net, ctx, "aop", io["at_wo"][0], mod_part(net, 1, 2))
        block = ctx.enter_context(nc.Block())
        block.sync(proj.sp)
        block.gpsimd(proj.pool)
        block.tensor(proj.pe)

        @block.vector
        def _(dve):
            proj.dve_start(dve)
            proj.dve(dve)


def stage_final(net):
    nc, io = net.nc, net.io
    with ExitStack() as ctx:
        y = ctx.enter_context(nc.sbuf_tensor("f_y", [128, DB, TOK], F32))
        rows = ctx.enter_context(nc.sbuf_tensor("f_rows", [128, 2, D], F32))
        zero = ctx.enter_context(nc.sbuf_tensor("f_zero", [128, DB, NV], F32))
        norm = Norm(net, ctx, "fn", net.gain[:, 4], zero[:], keep=y, split=False)
        tb = [ctx.enter_context(nc.psum_tensor(f"f_tb{i}", [128, 4, 128], F32)) for i in range(4)]
        s_zero, s_t, s_tev, s_out = net.semaphore("f_zero"), net.semaphore("f_t"), net.semaphore("f_tev"), [net.semaphore("f_out0"), net.semaphore("f_out1")]
        ident = c_(net, "ident")
        TILES = SEQ // 128
        block = ctx.enter_context(nc.Block())

        def over_tiles(eng, body):
            with eng.Fori(0, TILES // 2) as i:
                for s in range(2):
                    body(i * 2 + s, s, i, 128)
            body(TILES, 0, TILES // 2, DEC)

        @block.sync
        def _(sp):
            def out(t, s, i, n):
                sp.wait_ge(s_tev, t * 2 + 6)
                if n == DEC:
                    sp.dma_start(io["out_y_sample"].rearrange("b o d -> (b o) d"), rows[0:DEC, s, :]).then_inc(s_out[s], 16)
                else:
                    sp.dma_start(io["out_y_prompt"][0, bass.ds(t * 128, 128)], rows[:, s, :]).then_inc(s_out[s], 16)
            over_tiles(sp, out)
            sp.wait_ge(s_out[0], (TILES // 2 + 1) * 16 + 16)
            sp.wait_ge(s_out[1], TILES // 2 * 16 + 16)

        @block.tensor
        def _(pe):
            norm.pe(pe)
            pe.wait_ge(norm.s_h, DB)
            pe.wait_ge(norm.s_smp, DB)

            def turn(t, s, i, n):
                for h in range(2):
                    pe.wait_ge(s_tev, t * 2 + h + 1)
                    for q in range(4):
                        ins = pe.transpose(tb[2 * s + h][0:n, q, :], y[:, 4 * h + q, t * 128:t * 128 + n], ident)
                    ins.then_inc(s_t, 1)
            for t in range(TILES + 1):
                turn(t, t % 2, t // 2, 128 if t < TILES else DEC)

        @block.scalar
        def _(act):
            act.wait_ge(s_zero, 1)
            norm.act(act)

            def body(t, s, i, n):
                act.wait_ge(s_out[s], i * 16 + 16)
                for h in range(2):
                    act.wait_ge(s_t, t * 2 + h + 1)
                    act.activation(rows[0:n, s, h * 512:(h + 1) * 512].rearrange("p (q c) -> p q c", q=4), tb[2 * s + h][0:n], ACT.Copy).then_inc(s_tev, 1)
            over_tiles(act, body)

        @block.vector
        def _(dve):
            dve.sem_inc(s_tev, 4)
            for s in range(2):
                dve.sem_inc(s_out[s], 16)
            dve.memset(zero[:], 0.0).then_inc(s_zero, 1)
            dve.wait_ge(s_zero, 1)
            norm.dve(dve)


_OUTS = [("y_prompt", (1, SEQ, D)), ("y_sample", (DEC, 1, D)), ("wkv_prompt", (1, 1, HEADS, HD, HD)), ("wkv_sample", (1, DEC, HEADS, HD, HD)),
         ("shift_prompt", (1, 1, D)), ("shift_sample", (1, DEC, D)), ("k_prompt", (1, 1, WIN, KV, HD)), ("k_sample", (1, DEC, WIN, KV, HD)),
         ("v_prompt", (1, 1, WIN, KV, HD)), ("v_sample", (1, DEC, WIN, KV, HD))]


def layout(nc, inputs):
    arrays, io = {}, {}
    for name, a in {**inputs, **shape_constants()}.items():
        a = np.ascontiguousarray(a)
        arrays[f"in_{name}"] = a
        io[name] = nc.dram_tensor(f"in_{name}", a.shape, F32, kind="ExternalInput").ap()
    for name, shape in _OUTS:
        io["out_" + name] = nc.dram_tensor(f"out_{name}", shape, F32, kind="ExternalOutput").ap()
    return arrays, io


def kernel(**inputs):
    import concourse.bacc as bacc
    from concourse.bass_utils import run_bass_kernel_spmd

    nc = bacc.Bacc("TRN2", target_bir_lowering=False, num_devices=1)
    arrays, io = layout(nc, inputs)
    build(nc, io)
    r = run_bass_kernel_spmd(nc, [arrays], core_ids=[0])
    return tuple(r.results[0][f"out_{name}"] for name, _ in _OUTS)
```

```python
from contextlib import ExitStack, contextmanager

import numpy as np

import concourse.bass as bass
from concourse import mybir

F32 = mybir.dt.float32
F32R = mybir.dt.float32r
ALU = mybir.AluOpType
ACT = mybir.ActivationFunctionType
AX = mybir.AxisListType.X

D = 1024
DB = D // 128
SEQ = 1024
DEC = 8
NV = 1 + DEC
TOK = SEQ + DEC
NT = 3
TT = TOK // NT
HD = 64
HEADS = D // HD
C = 64
NCH = SEQ // C
Y_LAG = 3
Y_PAD = Y_LAG + 1
N_ADA = 6
FF_GROUPS = 4
KV = 4
WIN = 128
EPS = 1e-6
LNX_EPS = 64e-5
DECAY_SCALE = float(np.exp(-0.5))
SCALE = HD ** -0.5

PARAM_TABLES = [
    [("norm1_g", 16), ("norm2_g", 16), ("rw_mix", 48), ("at_bqkv", 12)],
    [("rw_w0", 8), ("rw_a0", 8), ("rw_kk", 8), ("rw_ka", 8), ("rw_rk", 8), ("rw_lnx_g", 8), ("rw_lnx_b", 8)],
    [("ada_b", 96)],
]
PARAM_AT = {}
for _t, _rows in enumerate(PARAM_TABLES):
    _at = 128 * _t
    for _name, _n in _rows:
        PARAM_AT[_name] = _at
        _at += _n

CONST_COLS = [("ident", 128), ("ones", 128), ("headsum", 128), ("lt", 64), ("le", 64), ("one64", 64), ("swap", 128)]
CONST_AT, _at = {}, 0
for _name, _n in CONST_COLS:
    CONST_AT[_name] = _at
    _at += _n
CONST_N = _at


def shape_constants():
    p = np.arange(128)
    small = {
        "ident": np.eye(128),
        "ones": np.ones((128, 128)),
        "headsum": (p[:, None] // 64 == p[None, :] // 64),
        "lt": (p[:, None] % 64 < np.arange(64)[None, :]),
        "le": (p[:, None] % 64 <= np.arange(64)[None, :]),
        "one64": np.ones((128, 64)),
    }
    d = p % 64
    partner = np.where(d < 8, p + 8, np.where(d < 16, p - 8, p))
    swap = np.zeros((128, 128))
    swap[p, partner] = 1
    small["swap"] = swap
    const = np.concatenate([np.asarray(small[n], np.float32) for n, _ in CONST_COLS], 1)
    start = np.ones((128, TOK))
    start[:, 0:SEQ:C] = 0
    start[:, SEQ:] = 0
    pos = np.concatenate([np.arange(SEQ), np.full(DEC, 2048)]).astype(np.float32)
    inv = (np.float32(500000.0) ** (-np.arange(8, dtype=np.float32) / np.float32(8))).astype(np.float32)
    ang = (pos[None, :] * inv[np.minimum(d, 15) % 8][:, None]).astype(np.float64)
    rot = (d < 16)[:, None]
    cos = np.where(rot, np.cos(ang), 1.0)
    sin = np.where(rot, np.sin(ang) * np.where(d < 8, -1.0, 1.0)[:, None], 0.0)
    wide = np.concatenate([start, cos, sin], 1).astype(np.float32)
    q, k = np.arange(128)[:, None], np.arange(256)[None, :]
    mask = np.where((k - 128 <= q) & (k - 128 >= q - WIN), 0, -1e30).astype(np.float32)
    return {"const_small": const, "const_wide": wide, "const_mask": mask}


class Chain:

    def __init__(self, eng, sem, per=0, i=0, base=0):
        self.eng, self.sem, self.n = eng, sem, 0
        self.start = i * per + base
        self.per = per

    def link(self, ins):
        ins.then_inc(self.sem, 1)
        self.n += 1
        self.eng.wait_ge(self.sem, self.start + self.n)


class Net:

    def semaphore(self, name):
        self.sems.append(self.nc.alloc_semaphore(name=name))
        return self.sems[-1]


@contextmanager
def stage(net):
    net.sems = []
    yield
    net.nc.clear_and_free_semaphores(net.sems)
    net.nc.all_engine_barrier()


def tiles(ap, n=TT):
    return ap.rearrange("p (n t) -> p n t", t=n)


def blk(ap, i):
    return ap[:, bass.ds(i, 1), :].rearrange("p a n -> p (a n)")


def build(nc, io):
    with ExitStack() as root:
        net = Net()
        net.nc, net.io = nc, io

        def sb(name, shape, dt=F32):
            return root.enter_context(nc.sbuf_tensor(name, shape, dt))

        net.const = sb("const", [128, CONST_N])
        net.param = sb("param", [128, 3 * 128])
        net.mod = sb("mod", [128, 2 * N_ADA * DB, NV])
        net.csil = sb("c_silu", [128, DB, 32])
        net.gain = sb("gain", [128, 4, DB, NV])

        def scratch(name, shape):
            return nc.dram_tensor(name, shape, F32).ap()

        net.scratch = scratch
        net.x_saved = scratch("x_saved", [128, DB, TOK])
        net.hx_saved = scratch("hx_saved", [128, DB, 1 + TOK])
        net.sL, net.sLm, net.sA, net.sG, net.sRt, net.sAt, net.sBt, net.sKt, net.sBS, net.sBV = (
            scratch("scr_" + n, [DB, 128, TOK]) for n in ("L", "Lm", "A", "G", "Rt", "At", "Bt", "Kt", "BS", "BV"))
        net.sM = scratch("scr_M", [NCH, DB, 128, C])
        net.sT = scratch("scr_T", [NCH, DB, 128, C])
        net.sV = scratch("scr_V", [TOK, D])
        net.sY = scratch("scr_Y", [DEC, D])
        net.sYc = scratch("scr_Yc", [DB, 128, Y_PAD * C + SEQ])
        net.sSmp = scratch("scr_Smp", [5, DEC, D])
        with ExitStack() as rwkv:
            net.sprev = rwkv.enter_context(nc.sbuf_tensor("sprev", [128, DB, DEC], F32))
            net.pend = rwkv.enter_context(nc.sbuf_tensor("pend", [128, DB, NCH], F32))
            net.Ps = rwkv.enter_context(nc.sbuf_tensor("Ps", [128, DB, DEC], F32))
            with ExitStack() as mixed:
                net.hx = mixed.enter_context(nc.sbuf_tensor("hx", [128, DB, 1 + TOK], F32))
                with ExitStack() as first:
                    net.X = first.enter_context(nc.sbuf_tensor("X0", [128, DB, TOK], F32))
                    with stage(net):
                        stage_start(net)
                    with stage(net):
                        stage_norm1_rwkv(net)
                operands(net, mixed, "rk")
                with stage(net):
                    stage_loras(net)
                with stage(net):
                    stage_r(net)
                with stage(net):
                    stage_k(net)
            with ExitStack() as ops:
                operands(net, ops, "v")
                with stage(net):
                    stage_v(net)
            with stage(net):
                stage_scan(net)
        net.X = sb("X", [128, DB, TOK])
        with ExitStack() as ops:
            operands(net, ops, "ro")
            with stage(net):
                stage_rwkv_out(net)
            with stage(net):
                stage_mlp(net, 0)
        with ExitStack() as ops:
            operands(net, ops, "at", False)
            with ExitStack() as heads:
                def hb(name, shape):
                    return heads.enter_context(nc.sbuf_tensor(name, shape, F32))
                net.Q = hb("Q", [128, DB, TOK])
                net.Kd = hb("Kd", [128, KV, TOK])
                net.Vt = hb("Vt", [128, SEQ // 128 + 1, KV * HD])
                net.Vd = hb("Vd", [128, KV, DEC])
                with stage(net):
                    stage_qkv(net)
                with stage(net):
                    stage_attend_samples(net)
                with stage(net):
                    stage_attend(net)
            with stage(net):
                stage_attend_out(net)
        with ExitStack() as ops:
            operands(net, ops, "m1")
            with stage(net):
                stage_mlp(net, 1)
        with stage(net):
            stage_final(net)


def operands(net, ctx, tag, with_weights=True):
    nc = net.nc
    net.HH = ctx.enter_context(nc.sbuf_tensor(f"{tag}_HH", [128, DB, TOK], F32R))
    net.HL = ctx.enter_context(nc.sbuf_tensor(f"{tag}_HL", [128, DB, TOK], F32R))
    if with_weights:
        weights(net, ctx, tag)


def weights(net, ctx, tag):
    nc = net.nc
    net.wraw = ctx.enter_context(nc.sbuf_tensor(f"{tag}_wraw", [128, 2, DB, 128], F32))
    net.wH = ctx.enter_context(nc.sbuf_tensor(f"{tag}_wH", [128, 2, DB, 128], F32R))
    net.wL = ctx.enter_context(nc.sbuf_tensor(f"{tag}_wL", [128, 2, DB, 128], F32R))


def c_(net, name):
    at = CONST_AT[name]
    return net.const[:, at:at + dict(CONST_COLS)[name]]




class Ada:

    GROUP = 2048
    PER_LAYER = N_ADA * D // GROUP
    SLOTS = 4

    def __init__(self, net, ctx, tag):
        nc = net.nc
        self.net = net
        sem = lambda name: net.semaphore(f"{tag}_{name}")
        self.ring = ctx.enter_context(nc.sbuf_tensor(f"{tag}_ring", [128, self.SLOTS, self.GROUP], F32))
        self.strip = ctx.enter_context(nc.sbuf_tensor(f"{tag}_strip", [128, 512], F32))
        self.acc = ctx.enter_context(nc.psum_tensor(f"{tag}_acc", [128, 512], F32))
        self.accT = ctx.enter_context(nc.psum_tensor(f"{tag}_accT", [128, 4, 128], F32))
        self.s_w = [sem(f"w{k}") for k in range(self.SLOTS)]
        self.s_used, self.s_acc, self.s_strip, self.s_accT, self.s_mod = sem("used"), sem("acc"), sem("strip"), sem("accT"), sem("mod")

    def load(self, sp, g, layer, column):
        for k in range(DB):
            sp.wait_ge(self.s_used, g * DB + k + 1)
            w = self.net.io["ada_w"][bass.ds(layer, 1), k * 128:(k + 1) * 128, bass.ds(column, self.GROUP)]
            sp.dma_start(self.ring[:, k % self.SLOTS, :], w.rearrange("a p n -> p (a n)")).then_inc(self.s_w[k % self.SLOTS], 16)

    def multiply(self, pe, g):
        pe.wait_ge(self.s_strip, g + 1)
        for k in range(DB):
            s = k % self.SLOTS
            pe.wait_ge(self.s_w[s], g * 16 * (DB // self.SLOTS) + 16 * (k // self.SLOTS + 1))
            for q in range(4):
                ins = pe.matmul(self.acc[32 * q:32 * q + 32, :], self.net.csil[:, k, :], self.ring[:, s, 512 * q:512 * q + 512], start=(k == 0), stop=(k == DB - 1), tile_position=(0, 32 * q))
            ins.then_inc(self.s_used, 1)
        pe.wait_ge(self.s_used, (g + 1) * DB + self.SLOTS)
        pe.sem_inc(self.s_acc, 1)

    def turn(self, pe, g):
        pe.wait_ge(self.s_strip, g + 2)
        pe.wait_ge(self.s_mod, g + 1)
        for r in range(4):
            ins = pe.transpose(self.accT[:, r, :], self.strip[:, r * 128:(r + 1) * 128], c_(self.net, "ident"))
        ins.then_inc(self.s_accT, 1)

    def strips_out(self, act, g):
        act.wait_ge(self.s_acc, g + 1)
        act.activation(self.strip[:], self.acc[:], ACT.Copy).then_inc(self.s_strip, 1)

    def turned_out(self, act, g, block):
        act.wait_ge(self.s_accT, g + 1)
        for q in range(4):
            ins = act.activation(self.net.mod[:, bass.ds(block + 4 * q, 4), :], self.accT[:, :, 32 * q:32 * q + NV], ACT.Copy)
        ins.then_inc(self.s_mod, 1)


def add_ada_bias(dve, net, first, n, done):
    at = PARAM_AT["ada_b"] + first
    m = net.mod[:, first:first + n, :]
    dve.tensor_tensor(m, m, net.param[:, at:at + n].unsqueeze(2).to_broadcast([128, n, NV]), ALU.add).then_inc(done, 1)


def make_gain(dve, net, slot, done):
    layer = slot // 2
    scale = mod_part(net, layer, (1, 4)[slot % 2])
    at = PARAM_AT[("norm1_g", "norm2_g")[slot % 2]] + DB * layer
    g = net.param[:, at:at + DB].unsqueeze(2).to_broadcast([128, DB, NV])
    dve.scalar_tensor_tensor(out=net.gain[:, slot], in0=scale, scalar=1.0, in1=g, op0=ALU.add, op1=ALU.mult).then_inc(done, 1)


def stage_start(net):
    nc, io = net.nc, net.io
    with ExitStack() as ctx:
        def sb(name, shape, dt=F32):
            return ctx.enter_context(nc.sbuf_tensor(name, shape, dt))

        def sem(name):
            return net.semaphore(name)

        rows = sb("param_rows", [128, 3, 128])
        crow = sb("c_row", [NV, D])
        csig = sb("c_sig", [NV, D])
        csil = net.csil
        xrow = sb("x_rows", [128, DB, D])
        xsrow = sb("xs_rows", [DEC, D])
        ada = Ada(net, ctx, "ada0")
        tp = [ctx.enter_context(nc.psum_tensor(f"tp{i}", [128, 4, 128], F32)) for i in range(2)]

        s_const, s_param, s_c, s_x = sem("s_const"), sem("s_param"), sem("s_c"), sem("s_x")
        s_rows0 = sem("s_rows_zero")
        s_sig, s_sil, s_sil0, s_silT = sem("s_sig"), sem("s_sil"), sem("s_sil_zero"), sem("s_silT")
        s_tp, s_tp_free = sem("s_tp"), sem("s_tp_free")
        s_dv = sem("s_dv")
        ident = c_(net, "ident")
        n_param = 0
        block = ctx.enter_context(nc.Block())

        turns = [("param", None)] + [("c", i) for i in range(2)] + [("x", (t, h)) for t in range(DB) for h in range(2)] + [("xs", h) for h in range(2)]

        @block.sync
        def _(sp):
            sp.dma_start(net.const[:], io["const_small"]).then_inc(s_const, 16)
            sp.dma_start(crow[0:1, :], io["c_prompt"]).then_inc(s_c, 16)
            sp.dma_start(crow[1:NV, :], io["c_sample"]).then_inc(s_c, 16)
            sp.wait_ge(s_rows0, 1)
            for t, table in enumerate(PARAM_TABLES):
                for name, n in table:
                    at = PARAM_AT[name] - 128 * t
                    ap = io[name]
                    ap = ap.rearrange({1: "(r p) -> r p", 2: "a (r p) -> (a r) p", 3: "a b (r p) -> (a b r) p"}[len(ap.shape)], p=128) if name != "rw_rk" else ap.rearrange("a (b h) d -> (a b) (h d)", h=2)
                    sp.dma_start(rows[at:at + n, t, :], ap).then_inc(s_param, 16)
            ada.load(sp, 0, 0, 0)

        @block.gpsimd
        def _(pool):
            for t in range(DB):
                pool.dma_start(xrow[:, t, :], io["x_prompt"][0, t * 128:(t + 1) * 128, :]).then_inc(s_x, 16)
            pool.dma_start(xsrow[:], io["x_sample"].rearrange("b o d -> (b o) d")).then_inc(s_x, 16)

        @block.scalar
        def _(act):
            act.wait_ge(s_c, 32)
            nc.scalar.activation(csig[:], crow[:], ACT.Sigmoid).then_inc(s_sig, 1)
            ada.strips_out(act, 0)
            ada.turned_out(act, 0, 0)

        @block.tensor
        def _(pe):
            pe.sem_inc(ada.s_used, ada.SLOTS)
            pe.wait_ge(s_const, 16)
            for n, (what, arg) in enumerate(turns):
                bank = tp[n % 2]
                if n >= 2:
                    pe.wait_ge(s_tp_free, n - 1)
                if what == "param":
                    pe.wait_ge(s_param, 16 * sum(len(t) for t in PARAM_TABLES))
                    for t in range(3):
                        ins = pe.transpose(bank[:, t, :], rows[:, t, :], ident)
                elif what == "c":
                    pe.wait_ge(s_sil, 1)
                    for q in range(4):
                        ins = pe.transpose(bank[:, q, 0:NV], crow[:, (4 * arg + q) * 128:(4 * arg + q + 1) * 128], ident[0:NV, 0:NV])
                elif what == "x":
                    t, h = arg
                    pe.wait_ge(s_x, 16 * (DB + 1))
                    for q in range(4):
                        ins = pe.transpose(bank[:, q, :], xrow[:, t, (4 * h + q) * 128:(4 * h + q + 1) * 128], ident)
                else:
                    for q in range(4):
                        ins = pe.transpose(bank[:, q, 0:DEC], xsrow[:, (4 * arg + q) * 128:(4 * arg + q + 1) * 128], ident[0:DEC, 0:DEC])
                ins.then_inc(s_tp, 1)
            pe.wait_ge(s_silT, 2)
            ada.multiply(pe, 0)
            ada.turn(pe, 0)

        @block.vector
        def _(dve):
            dve.sem_inc(ada.s_strip, 1)
            dve.sem_inc(ada.s_mod, 1)
            dve.memset(rows[:], 0.0).then_inc(s_rows0, 1)
            dve.memset(csil[:], 0.0).then_inc(s_sil0, 1)
            dve.wait_ge(s_sig, 1)
            dve.tensor_tensor(crow[:], crow[:], csig[:], ALU.mult).then_inc(s_sil, 1)
            dve.wait_ge(s_sil0, 1)
            for n, (what, arg) in enumerate(turns):
                bank = tp[n % 2]
                dve.wait_ge(s_tp, n + 1)
                if what == "param":
                    dve.tensor_copy(net.param[:].rearrange("p (t n) -> p t n", t=3), bank[:, 0:3, :]).then_inc(s_tp_free, 1)
                elif what == "c":
                    ins = dve.tensor_copy(csil[:, 4 * arg:4 * arg + 4, 0:NV], bank[:, :, 0:NV])
                    ins.then_inc(s_silT, 1)
                    dve.wait_ge(s_silT, arg + 1)
                    dve.sem_inc(s_tp_free, 1)
                elif what == "x":
                    t, h = arg
                    dve.tensor_copy(net.X[:, 4 * h:4 * h + 4, t * 128:(t + 1) * 128], bank[:]).then_inc(s_tp_free, 1)
                else:
                    dve.tensor_copy(net.X[:, 4 * arg:4 * arg + 4, SEQ:TOK], bank[:, :, 0:DEC]).then_inc(s_tp_free, 1)
            dve.wait_ge(s_tp_free, len(turns))
            dve.wait_ge(ada.s_mod, 2)
            add_ada_bias(dve, net, 0, 2 * DB, s_dv)
            dve.wait_ge(s_dv, 1)
            make_gain(dve, net, 0, s_dv)
            dve.wait_ge(s_dv, 2)


def mod_part(net, layer, part):
    at = (layer * N_ADA + part) * DB
    return net.mod[:, at:at + DB, :]




class Norm:

    def __init__(self, net, ctx, tag, gain, shift, keep=None, split=True, sq=None, rs=None, ps=None):
        nc = net.nc
        self.net, self.gain, self.shift, self.keep, self.split = net, gain, shift, keep, split
        sem = lambda name: net.semaphore(f"{tag}_{name}")
        self.sq = ctx.enter_context(nc.sbuf_tensor(f"{tag}_sq", [128, 2, TOK], F32)) if sq is None else sq
        self.rs = ctx.enter_context(nc.sbuf_tensor(f"{tag}_rs", [128, TOK], F32)) if rs is None else rs
        self.ps = ctx.enter_context(nc.psum_tensor(f"{tag}_ps", [128, NT, 512], F32)) if ps is None else ps
        self.s_sq, self.s_used, self.s_sum = sem("sq"), sem("sq_used"), sem("sum")
        self.s_mean, self.s_root, self.s_rs = sem("mean"), sem("root"), sem("rs")
        self.s_xn, self.s_h, self.s_hi, self.s_lo = sem("xn"), sem("h"), sem("hi"), sem("lo")
        self.s_smp, self.s_dv = sem("smp"), sem("dv")

    def pe(self, pe):
        ones = c_(self.net, "ones")
        for b in range(DB):
            pe.wait_ge(self.s_sq, b + 1)
            for n in range(NT):
                ins = pe.matmul(self.ps[:, n, 0:TT], ones, self.sq[:, b % 2, n * TT:(n + 1) * TT], start=(b == 0), stop=(b == DB - 1))
            ins.then_inc(self.s_used, 1)

    def act(self, act):
        net = self.net
        for b in range(DB):
            if b >= 2:
                act.wait_ge(self.s_used, b - 1)
            act.activation(self.sq[:, b % 2, :], net.X[:, b, :], ACT.Square).then_inc(self.s_sq, 1)
        act.wait_ge(self.s_mean, 1)
        act.activation(self.rs[:], self.rs[:], ACT.Sqrt).then_inc(self.s_root, 1)
        for b in range(DB):
            act.wait_ge(self.s_xn, b + 1)
            h = self.h(b)
            act.activation(h[:, 0:SEQ], self.sq[:, b % 2, 0:SEQ], ACT.Identity, bias=self.shift[:, b, 0:1], scale=self.gain[:, b, 0:1]).then_inc(self.s_h, 1)
            if not self.split:
                continue
            act.wait_ge(self.s_h, b + 1)
            act.wait_ge(self.s_smp, b + 1)
            act.activation(net.HH[:, b, :], h[:, 0:TOK], ACT.Copy).then_inc(self.s_hi, 1)

    def h(self, b):
        return self.sq[:, b % 2, :] if self.keep is None else self.keep[:, b, :]

    def dve(self, dve):
        net = self.net
        dve.wait_ge(self.s_used, DB)
        dve.tensor_scalar(tiles(self.rs[:]), self.ps[:, :, 0:TT], 1.0 / D, EPS, ALU.mult, ALU.add).then_inc(self.s_mean, 1)
        dve.wait_ge(self.s_root, 1)
        dve.reciprocal(self.rs[:], self.rs[:]).then_inc(self.s_rs, 1)
        dve.wait_ge(self.s_rs, 1)
        for b in range(DB):
            if b >= 2 and self.split:
                dve.wait_ge(self.s_hi, b - 1)
                dve.wait_ge(self.s_lo, b - 1)
            elif b >= 2:
                dve.wait_ge(self.s_h, b - 1)
                dve.wait_ge(self.s_smp, b - 1)
            xn = self.sq[:, b % 2, :]
            dve.tensor_tensor(xn, net.X[:, b, :], self.rs[:], ALU.mult).then_inc(self.s_xn, 1)
            dve.wait_ge(self.s_xn, b + 1)
            h = self.h(b)
            dve.tensor_tensor(h[:, SEQ:TOK], xn[:, SEQ:TOK], self.gain[:, b, 1:NV], ALU.mult).then_inc(self.s_dv, 1)
            dve.wait_ge(self.s_dv, b + 1)
            dve.tensor_tensor(h[:, SEQ:TOK], h[:, SEQ:TOK], self.shift[:, b, 1:NV], ALU.add).then_inc(self.s_smp, 1)
            if b >= 1 and self.split:
                self.low(dve, b - 1)
        if self.split:
            self.low(dve, DB - 1)

    def low(self, dve, b):
        net = self.net
        dve.wait_ge(self.s_hi, b + 1)
        dve.wait_ge(self.s_h, b + 1)
        dve.tensor_tensor(net.HL[:, b, :], self.h(b)[:, 0:TOK], net.HH[:, b, :].bitcast(F32), ALU.subtract).then_inc(self.s_lo, 1)




class Panels:

    LOW0, DONE0 = 2, 2 * NT

    def __init__(self, net, ctx, tag, cols=128):
        nc = net.nc
        self.net, self.cols = net, cols
        sem = lambda name: net.semaphore(f"{tag}_{name}")
        self.acc = ctx.enter_context(nc.psum_tensor(f"{tag}_acc", [128, NT, 512], F32))
        self.landed = [sem("landed0"), sem("landed1")]
        self.high, self.low = sem("high"), sem("low")
        self.done, self.free = sem("acc_done"), sem("acc_free")

    def load(self, sp, p, s, src, cols=None):
        sp.wait_ge(self.low, p + 1)
        sp.dma_start(self.net.wraw[:, s, :, 0:cols or self.cols], src).then_inc(self.landed[s], 16)

    def split(self, pool, p, s, i, cols=None):
        net = self.net
        cols = cols or self.cols
        raw, high = net.wraw[:, s, :, 0:cols], net.wH[:, s, :, 0:cols]
        pool.wait_ge(self.landed[s], i * 16 + 16)
        pool.wait_ge(self.done, p * NT + NT)
        one = c_(net, "ones")[:, 0:cols].unsqueeze(1).to_broadcast([128, DB, cols])
        pool.tensor_tensor(high, raw, one, ALU.mult).then_inc(self.high, 1)
        pool.wait_ge(self.high, p + 1)
        pool.tensor_tensor(net.wL[:, s, :, 0:cols], raw, high.bitcast(F32), ALU.subtract).then_inc(self.low, 1)

    def multiply(self, pe, p, s, hi, lo, ready=None, free=None):
        net = self.net
        pe.wait_ge(self.low, p + 1 + self.LOW0)
        for n in range(NT):
            for sem, value in free or [(self.free, p * NT + 1)]:
                pe.wait_ge(sem, value + n)
            t = slice(n * TT, (n + 1) * TT)
            for k in range(DB):
                if n == 0 and ready is not None:
                    pe.wait_ge(ready[0], ready[1] + k)
                out = self.acc[0:self.cols, n, 0:TT]
                wh, wl = net.wH[:, s, k, 0:self.cols], net.wL[:, s, k, 0:self.cols]
                pe.matmul(out, wh, hi[:, k, t], start=(k == 0), stop=False)
                pe.matmul(out, wh, lo[:, k, t], start=False, stop=False)
                ins = pe.matmul(out, wl, hi[:, k, t], start=False, stop=(k == DB - 1))
            ins.then_inc(self.done, 1)

    def multiply_by_block(self, pe, p, s, cols, lo, used, before=None):
        net = self.net
        pe.wait_ge(self.low, p + 1 + self.LOW0)
        pe.wait_ge(self.free, p * NT + NT)
        for k in range(DB):
            if before:
                before(k)
            pe.wait_ge(lo[0], lo[1] + k)
            for w, x in ((net.wH, net.HH), (net.wH, net.HL), (net.wL, net.HH)):
                for n in range(NT):
                    ins = pe.matmul(self.acc[0:cols, n, 0:TT], w[:, s, k, 0:cols], x[:, k, n * TT:(n + 1) * TT],
                                    start=(k == 0 and w is net.wH and x is net.HH), stop=(k == DB - 1 and w is net.wL))
            ins.then_inc(used, 1)
        for n in range(NT):
            pe.wait_ge(used, lo[1] + DB - 1)
            pe.sem_inc(self.done, 1)

    def summed(self, eng, p, n):
        eng.wait_ge(self.done, p * NT + n + 1 + self.DONE0)


def panel_of(w, m):
    return w[:, bass.ds(m, 128)].rearrange("(k p) m -> p k m", p=128)


def add_gated(dve, net, pan, p, m, gate, tmp, s_free, s_tmp, n_before):
    X = blk(net.X, m)
    for n in range(NT):
        pan.summed(dve, p, n)
        a, z = n * TT, min((n + 1) * TT, SEQ)
        ins = dve.scalar_tensor_tensor(out=X[:, a:z], in0=pan.acc[:, n, 0:z - a], scalar=blk(gate, m)[:, 0:1], in1=X[:, a:z], op0=ALU.mult, op1=ALU.add)
        if n < NT - 1:
            ins.then_inc(s_free, 1)
    dve.tensor_tensor(tmp, pan.acc[:, NT - 1, TT - DEC:TT], blk(gate, m)[:, 1:NV], ALU.mult).then_inc(s_tmp, 1)
    dve.wait_ge(s_tmp, n_before + 1)
    dve.tensor_tensor(X[:, SEQ:TOK], X[:, SEQ:TOK], tmp, ALU.add).then_inc(s_free, 1)


def stage_mlp(net, layer):
    nc, io = net.nc, net.io
    up = io["mlp_up"][layer]
    down = io["mlp_down"][layer]
    gate = mod_part(net, layer, 5)
    with ExitStack() as ctx:
        def sb(name, shape, dt=F32):
            return ctx.enter_context(nc.sbuf_tensor(f"mlp{layer}_{name}", shape, dt))

        def sem(name):
            return net.semaphore(f"mlp{layer}_{name}")

        GH, GL = sb("GH", [128, DB, TOK], F32R), sb("GL", [128, DB, TOK], F32R)
        act_buf = sb("relu", [128, 2, TOK])
        norm = Norm(net, ctx, f"mlpn{layer}", net.gain[:, 2 * layer + 1], mod_part(net, layer, 3), sq=act_buf)
        smp = sb("smp", [128, DEC])
        pan = Panels(net, ctx, f"mlp{layer}p")
        s_relu, s_sqr, s_gh, s_gl, s_smp = sem("relu"), sem("sqr"), sem("gh"), sem("gl"), sem("smp")
        s_added = sem("added")
        block = ctx.enter_context(nc.Block())
        GP = 2 * DB

        @block.sync
        def _(sp):
            with sp.Fori(0, FF_GROUPS) as g:
                with sp.Fori(0, DB // 2) as j:
                    for s in range(2):
                        pan.load(sp, g * GP + j * 2 + s, s, panel_of(up, g * 1024 + j * 256 + s * 128))
                with sp.Fori(0, DB // 2) as j:
                    for s in range(2):
                        pan.load(sp, g * GP + DB + j * 2 + s, s, panel_of(down[bass.ds(g * 1024, 1024), :], j * 256 + s * 128))

        @block.gpsimd
        def _(pool):
            with pool.Fori(0, FF_GROUPS * DB) as j:
                for s in range(2):
                    pan.split(pool, j * 2 + s, s, j)

        @block.tensor
        def _(pe):
            norm.pe(pe)
            with pe.Fori(0, FF_GROUPS) as g:
                with pe.Fori(0, DB // 2) as j:
                    for s in range(2):
                        pan.multiply(pe, g * GP + j * 2 + s, s, net.HH, net.HL, ready=(norm.s_lo, 1), free=[(pan.free, (g * DB + j * 2 + s) * NT + 1), (s_added, g * DB * NT + 1)])
                with pe.Fori(0, DB // 2) as j:
                    for s in range(2):
                        pan.multiply(pe, g * GP + DB + j * 2 + s, s, GH, GL, ready=(s_gl, g * DB + 3),
                                     free=[(pan.free, (g + 1) * DB * NT + 1), (s_added, (g * DB + j * 2 + s) * NT + 1)])

        @block.scalar
        def _(act):
            act.sem_inc(pan.free, NT)
            norm.act(act)
            with act.Fori(0, FF_GROUPS) as g:
                with act.Fori(0, DB // 2) as j:
                    for s in range(2):
                        h, p = g * DB + j * 2 + s, g * GP + j * 2 + s
                        act.wait_ge(s_gl, h + 1)
                        for n in range(NT):
                            pan.summed(act, p, n)
                            act.activation(act_buf[:, s, n * TT:(n + 1) * TT], pan.acc[:, n, 0:TT], ACT.Relu).then_inc(pan.free, 1)
                        act.wait_ge(s_sqr, h + 1)
                        act.activation(blk(GH, j * 2 + s), act_buf[:, s, :], ACT.Copy).then_inc(s_gh, 1)

        @block.vector
        def _(dve):
            dve.sem_inc(s_gl, 2)
            dve.sem_inc(pan.low, pan.LOW0)
            dve.sem_inc(pan.done, pan.DONE0)
            dve.sem_inc(s_added, NT)
            norm.dve(dve)
            with dve.Fori(0, FF_GROUPS) as g:
                with dve.Fori(0, DB // 2) as j:
                    for s in range(2):
                        h, p = g * DB + j * 2 + s, g * GP + j * 2 + s
                        dve.wait_ge(pan.free, h * NT + 2 * NT)
                        dve.tensor_tensor(act_buf[:, s, :], act_buf[:, s, :], act_buf[:, s, :], ALU.mult).then_inc(s_sqr, 1)
                        dve.wait_ge(s_gh, h + 1)
                        dve.wait_ge(s_sqr, h + 1)
                        dve.tensor_tensor(blk(GL, j * 2 + s), act_buf[:, s, :], blk(GH, j * 2 + s).bitcast(F32), ALU.subtract).then_inc(s_gl, 1)
                with dve.Fori(0, DB // 2) as j:
                    for s in range(2):
                        add_gated(dve, net, pan, g * GP + DB + j * 2 + s, j * 2 + s, gate, smp[:], s_added, s_smp, g * DB + j * 2 + s)





def row(scratch, b):
    return scratch[bass.ds(b, 1)].rearrange("a p t -> p (a t)")


def stage_norm1_rwkv(net):
    nc, io = net.nc, net.io
    with ExitStack() as ctx:
        norm = Norm(net, ctx, "rn", net.gain[:, 0], mod_part(net, 0, 0), keep=net.hx[:, :, 1:1 + TOK], split=False)
        sem = lambda name: net.semaphore(f"rn_{name}")
        srow = ctx.enter_context(nc.sbuf_tensor("shift_rows", [DEC, D], F32))
        last = ctx.enter_context(nc.sbuf_tensor("last_rows", [NV, D], F32))
        tp = [ctx.enter_context(nc.psum_tensor(f"rn_tp{i}", [128, 4, 128], F32)) for i in range(2)]
        s_in, s_tp, s_prev, s_last, s_out, s_zero = sem("in"), sem("tp"), sem("prev"), sem("last"), sem("out"), sem("zero")
        ident = c_(net, "ident")
        block = ctx.enter_context(nc.Block())

        @block.sync
        def _(sp):
            sp.dma_start(srow[:], io["state_shift"][0]).then_inc(s_in, 16)
            sp.dma_start(net.x_saved, net.X[:]).then_inc(s_out, 16)
            sp.wait_ge(s_last, 4)
            sp.dma_start(io["out_shift_prompt"].rearrange("a b d -> (a b) d"), last[0:1, :]).then_inc(s_out, 16)
            sp.dma_start(io["out_shift_sample"].rearrange("a b d -> (a b) d"), last[1:NV, :]).then_inc(s_out, 16)
            sp.dma_start(net.hx_saved, net.hx[:]).then_inc(s_out, 16)
            sp.wait_ge(s_out, 64)

        @block.tensor
        def _(pe):
            norm.pe(pe)
            pe.wait_ge(s_in, 16)
            for n in range(2):
                for q in range(4):
                    ins = pe.transpose(tp[n][:, q, 0:DEC], srow[:, (4 * n + q) * 128:(4 * n + q + 1) * 128], ident[0:DEC, 0:DEC])
                ins.then_inc(s_tp, 1)
            pe.wait_ge(norm.s_h, DB)
            pe.wait_ge(norm.s_smp, DB)
            for n in range(2):
                pe.wait_ge(s_prev, n + 1)
                for q in range(4):
                    ins = pe.transpose(tp[n][0:NV, q, :], net.hx[:, 4 * n + q, SEQ:SEQ + NV], ident)
                ins.then_inc(s_tp, 1)

        @block.scalar
        def _(act):
            norm.act(act)

        @block.vector
        def _(dve):
            dve.memset(net.hx[:, :, 0:1], 0.0).then_inc(s_zero, 1)
            norm.dve(dve)
            for n in range(2):
                dve.wait_ge(s_tp, n + 1)
                dve.tensor_copy(net.sprev[:, 4 * n:4 * n + 4, :], tp[n][:, :, 0:DEC]).then_inc(s_prev, 1)
            for n in range(2):
                dve.wait_ge(s_tp, n + 3)
                dve.tensor_copy(last[:, n * 512:(n + 1) * 512].rearrange("v (q c) -> v q c", q=4), tp[n][0:NV, :, :]).then_inc(s_last, 2)


class Mix:

    def __init__(self, net, ctx, tag, which, buf=None, hx=None):
        self.net, self.at, self.hx = net, PARAM_AT["rw_mix"] + 8 * which, hx
        sem = lambda name: net.semaphore(f"{tag}_{name}")
        self.buf = ctx.enter_context(net.nc.sbuf_tensor(f"{tag}_xm", [128, 2, TOK], F32)) if buf is None else buf
        self.s_hx = [sem("hx0"), sem("hx1")] if hx is not None else None
        self.s_d, self.s_xm, self.s_hi, self.s_lo = sem("d"), sem("xm"), sem("hi"), sem("lo")

    def load(self, act, b):
        act.dma_start(self.hx[:, b % 2, :], self.net.hx_saved[:, b]).then_inc(self.s_hx[b % 2], 16)

    def act(self, act):
        if self.s_hx:
            self.load(act, 0)
            self.load(act, 1)
        for b in range(DB):
            act.wait_ge(self.s_xm, b + 1)
            if self.s_hx and b + 2 < DB:
                self.load(act, b + 2)
            act.activation(self.net.HH[:, b, :], self.buf[:, b % 2, :], ACT.Copy).then_inc(self.s_hi, 1)

    def dve(self, dve):
        net = self.net

        def low(b):
            dve.wait_ge(self.s_hi, b + 1)
            dve.tensor_tensor(net.HL[:, b, :], self.buf[:, b % 2, :], net.HH[:, b, :].bitcast(F32), ALU.subtract).then_inc(self.s_lo, 1)

        for b in range(DB):
            hx = net.hx[:, b] if self.hx is None else self.hx[:, b % 2]
            d, h = self.buf[:, b % 2, :], hx[:, 1:1 + TOK]
            if b >= 2:
                dve.wait_ge(self.s_lo, b - 1)
            if self.s_hx:
                dve.wait_ge(self.s_hx[b % 2], 16 * (b // 2 + 1))
            dve.tensor_tensor(d[:, 0:SEQ], hx[:, 0:SEQ], hx[:, 1:1 + SEQ], ALU.subtract).then_inc(self.s_d, 1)
            dve.tensor_tensor(d[:, SEQ:TOK], net.sprev[:, b, :], hx[:, 1 + SEQ:1 + TOK], ALU.subtract).then_inc(self.s_d, 1)
            dve.wait_ge(self.s_d, 2 * b + 2)
            dve.scalar_tensor_tensor(out=d, in0=d, scalar=net.param[:, self.at + b:self.at + b + 1], in1=h, op0=ALU.mult, op1=ALU.add).then_inc(self.s_xm, 1)
            if b >= 1:
                low(b - 1)
        low(DB - 1)


class Mixes:

    def __init__(self, net, ctx, tag, which):
        self.net, self.which = net, which
        sem = lambda name: net.semaphore(f"{tag}_{name}")
        self.buf = ctx.enter_context(net.nc.sbuf_tensor(f"{tag}_xm", [128, 2, TOK], F32))
        self.s_d, self.s_xm, self.s_hi, self.s_lo, self.s_used = sem("d"), sem("xm"), sem("hi"), sem("lo"), sem("used")

    def act(self, act, p, b):
        q = p * DB + b
        act.wait_ge(self.s_xm, q + 1)
        if p:
            act.wait_ge(self.s_used, q - DB + 1)
        act.activation(self.net.HH[:, b, :], self.buf[:, b % 2, :], ACT.Copy).then_inc(self.s_hi, 1)

    def pool(self, pool, p):
        for b in range(DB):
            q = p * DB + b
            pool.wait_ge(self.s_hi, q + 1)
            pool.tensor_tensor(self.net.HL[:, b, :], self.buf[:, b % 2, :], self.net.HH[:, b, :].bitcast(F32), ALU.subtract).then_inc(self.s_lo, 1)

    def dve(self, dve, p):
        net = self.net
        at = PARAM_AT["rw_mix"] + DB * self.which[p]
        for b in range(DB):
            q = p * DB + b
            d, h = self.buf[:, b % 2, :], net.hx[:, b, 1:1 + TOK]
            if q >= 2:
                dve.wait_ge(self.s_lo, q - 1)
            dve.tensor_tensor(d[:, 0:SEQ], net.hx[:, b, 0:SEQ], net.hx[:, b, 1:1 + SEQ], ALU.subtract).then_inc(self.s_d, 1)
            dve.tensor_tensor(d[:, SEQ:TOK], net.sprev[:, b, :], net.hx[:, b, 1 + SEQ:1 + TOK], ALU.subtract).then_inc(self.s_d, 1)
            dve.wait_ge(self.s_d, 2 * q + 2)
            dve.scalar_tensor_tensor(out=d, in0=d, scalar=net.param[:, at + b:at + b + 1], in1=h, op0=ALU.mult, op1=ALU.add).then_inc(self.s_xm, 1)


def stage_loras(net):
    nc, io = net.nc, net.io
    BRANCHES = [("g", 128, 5, ACT.Sigmoid), ("a", 64, 4, ACT.Copy), ("w", 64, 1, ACT.Tanh)]
    with ExitStack() as ctx:
        def sb(name, shape, dt=F32):
            return ctx.enter_context(nc.sbuf_tensor(f"lora_{name}", shape, dt))

        def sem(name):
            return net.semaphore(f"lora_{name}")

        mixes = Mixes(net, ctx, "lora", [mix for _, _, mix, _ in BRANCHES])
        pan = Panels(net, ctx, "lorap")
        w2 = [sb(f"{name}2", [rank, D]) for name, rank, _, _ in BRANCHES]
        low_rank = sb("inner", [128, TOK])
        out, cum, start = sb("out", [128, 2, TOK]), sb("cum", [128, 2, TOK]), sb("start", [128, TOK])
        ps = ctx.enter_context(nc.psum_tensor("lora_ps", [128, NT, 512], F32))
        s_w2, s_in, s_ps, s_out, s_dv, s_ready = sem("w2"), sem("inner"), sem("ps"), sem("out"), sem("dv"), sem("ready")
        s_stored, s_cum = [sem("stored0"), sem("stored1")], [sem("cum0"), sem("cum1")]
        W = len(BRANCHES) - 1
        block = ctx.enter_context(nc.Block())

        @block.sync
        def _(sp):
            for p, (name, rank, _, _) in enumerate(BRANCHES):
                pan.load(sp, p, p % 2, io[f"rw_{name}1"][0].rearrange("(k p) m -> p k m", p=128), rank)
                sp.dma_start(w2[p][:], io[f"rw_{name}2"][0]).then_inc(s_w2, 16)
            sp.dma_start(start[:], io["const_wide"][:, 0:TOK]).then_inc(s_w2, 16)
            for p, (name, _, _, _) in enumerate(BRANCHES):
                for b in range(DB):
                    s = b % 2
                    if p == W:
                        sp.wait_ge(s_ready, b + 1)
                        sp.dma_start(net.sL[b], cum[:, s, :]).then_inc(s_cum[s], 16)
                        sp.dma_start(net.sLm[b], out[:, s, :]).then_inc(s_stored[s], 16)
                    else:
                        sp.wait_ge(s_out, (p * DB + b + 1) * NT)
                        sp.dma_start({"a": net.sA, "g": net.sG}[name][b], out[:, s, :]).then_inc(s_stored[s], 16)
            for s in range(2):
                sp.wait_ge(s_stored[s], 16 * len(BRANCHES) * (DB // 2))
                sp.wait_ge(s_cum[s], 16 * (DB // 2))

        @block.gpsimd
        def _(pool):
            for p, (_, rank, _, _) in enumerate(BRANCHES):
                pan.split(pool, p, p % 2, p // 2, rank)
                mixes.pool(pool, p)

        @block.tensor
        def _(pe):
            def second(p, b):
                rank = BRANCHES[p][1]
                pe.wait_ge(s_in, (p + 1) * NT)
                for n in range(NT):
                    q = (p * DB + b) * NT + n
                    if q >= NT:
                        pe.wait_ge(s_out, q - NT + 1)
                    pe.matmul(ps[:, n, 0:TT], w2[p][:, b * 128:(b + 1) * 128], low_rank[0:rank, n * TT:(n + 1) * TT], start=True, stop=True).then_inc(s_ps, 1)

            pe.wait_ge(s_w2, 16 * (len(BRANCHES) + 1))
            for p, (_, rank, _, _) in enumerate(BRANCHES):
                pan.multiply_by_block(pe, p, p % 2, rank, (mixes.s_lo, p * DB + 1), mixes.s_used,
                                      before=(lambda b: second(p - 1, b)) if p else None)
            for b in range(DB):
                second(W, b)

        @block.scalar
        def _(act):
            def out_of(p, b):
                name = BRANCHES[p][0]
                q = p * DB + b
                if q >= 2:
                    act.wait_ge(s_stored[b % 2], 16 * (q // 2))
                for n in range(NT):
                    act.wait_ge(s_ps, q * NT + n + 1)
                    o = out[:, b % 2, n * TT:(n + 1) * TT]
                    if name == "g":
                        act.activation(o, ps[:, n, 0:TT], ACT.Copy).then_inc(s_out, 1)
                    else:
                        at = PARAM_AT[f"rw_{name}0"] + b
                        act.activation(o, ps[:, n, 0:TT], ACT.Sigmoid, bias=net.param[:, at:at + 1]).then_inc(s_out, 1)

            for p, (name, rank, _, inner) in enumerate(BRANCHES):
                for b in range(DB):
                    mixes.act(act, p, b)
                    if p:
                        out_of(p - 1, b)
                for n in range(NT):
                    pan.summed(act, p, n)
                    act.activation(low_rank[0:rank, n * TT:(n + 1) * TT], pan.acc[0:rank, n, 0:TT], inner).then_inc(s_in, 1)
                act.wait_ge(s_in, (p + 1) * NT)
                act.sem_inc(pan.free, NT)
            for b in range(DB):
                out_of(W, b)

        @block.vector
        def _(dve):
            dve.sem_inc(pan.low, pan.LOW0)
            dve.sem_inc(pan.done, pan.DONE0)
            dve.sem_inc(pan.free, NT)
            for p in range(len(BRANCHES)):
                mixes.dve(dve, p)
            chain = Chain(dve, s_dv)
            dve.wait_ge(s_w2, 16 * (len(BRANCHES) + 1))
            for b in range(DB):
                o, L = out[:, b % 2, :], cum[:, b % 2, :]
                dve.wait_ge(s_out, (W * DB + b + 1) * NT)
                if b >= 2:
                    dve.wait_ge(s_cum[b % 2], 16 * (b // 2))
                chain.link(dve.tensor_scalar(o, o, -DECAY_SCALE, None, ALU.mult))
                chain.link(dve.tensor_tensor_scan(L, start[:], o, 0.0, ALU.mult, ALU.add))
                dve.tensor_tensor(o, L, o, ALU.subtract).then_inc(s_ready, 1)


def stage_r(net):
    nc, io = net.nc, net.io
    with ExitStack() as ctx:
        def sb(name, shape, dt=F32):
            return ctx.enter_context(nc.sbuf_tensor(f"r_{name}", shape, dt))

        def sem(name):
            return net.semaphore(f"r_{name}")

        mix = Mix(net, ctx, "r", 0)
        pan = Panels(net, ctx, "rp")
        L, Rt = sb("L", [128, 2, TOK]), sb("Rt", [128, 2, TOK])
        s_L, s_P, s_Rt, s_st = [sem("L0"), sem("L1")], sem("P"), sem("Rt"), [sem("st0"), sem("st1")]
        block = ctx.enter_context(nc.Block())
        w = io["rw_wr"][0]

        @block.sync
        def _(sp):
            with sp.Fori(0, DB // 2) as j:
                for s in range(2):
                    pan.load(sp, j * 2 + s, s, panel_of(w, j * 256 + s * 128))
                    sp.wait_ge(s_Rt, j * 2 + s + 1)
                    sp.dma_start(L[:, s, :], row(net.sL, j * 2 + s)).then_inc(s_L[s], 16)

        @block.gpsimd
        def _(pool):
            with pool.Fori(0, DB // 2) as j:
                for s in range(2):
                    pan.split(pool, j * 2 + s, s, j)

        @block.tensor
        def _(pe):
            with pe.Fori(0, DB // 2) as j:
                for s in range(2):
                    pan.multiply(pe, j * 2 + s, s, net.HH, net.HL, ready=(mix.s_lo, 1))

        @block.scalar
        def _(act):
            mix.act(act)
            with act.Fori(0, DB // 2) as j:
                for s in range(2):
                    act.wait_ge(s_L[s], j * 16 + 16)
                    act.activation(L[:, s, :], L[:, s, :], ACT.Exp).then_inc(s_P, 1)
                    act.wait_ge(s_Rt, j * 2 + s + 3)
                    act.dma_start(row(net.sRt, j * 2 + s), Rt[:, s, :]).then_inc(s_st[s], 16)
            for s in range(2):
                act.wait_ge(s_st[s], 16 * (DB // 2) + 16)

        @block.vector
        def _(dve):
            dve.sem_inc(pan.low, pan.LOW0)
            dve.sem_inc(pan.done, pan.DONE0)
            dve.sem_inc(pan.free, NT)
            dve.sem_inc(s_Rt, 2)
            for s in range(2):
                dve.sem_inc(s_st[s], 16)
            mix.dve(dve)
            with dve.Fori(0, DB // 2) as j:
                for s in range(2):
                    dve.wait_ge(s_P, j * 2 + s + 1)
                    dve.wait_ge(s_st[s], j * 16 + 16)
                    for n in range(NT):
                        pan.summed(dve, j * 2 + s, n)
                        t = slice(n * TT, (n + 1) * TT)
                        ins = dve.tensor_tensor(Rt[:, s, t], pan.acc[:, n, 0:TT], L[:, s, t], ALU.mult)
                        ins.then_inc(pan.free, 1)
                    dve.wait_ge(pan.free, (j * 2 + s) * NT + 2 * NT)
                    dve.sem_inc(s_Rt, 1)


def stage_k(net):
    nc, io = net.nc, net.io
    with ExitStack() as ctx:
        def sb(name, shape, dt=F32):
            return ctx.enter_context(nc.sbuf_tensor(f"k_{name}", shape, dt))

        def sem(name):
            return net.semaphore(f"k_{name}")

        mix = Mix(net, ctx, "k", 2)
        pan = Panels(net, ctx, "kp")
        A, L, Lm, Rt = (sb(n, [128, 2, TOK]) for n in ("a", "L", "Lm", "Rt"))
        k, sq, inv, am, bq, bs = (sb(n, [128, TOK]) for n in ("k", "sq", "inv", "am", "bq", "bs"))
        omka = sb("omka", [128, DB])
        M = sb("M", [128, NCH, C])
        pM = ctx.enter_context(nc.psum_tensor("k_pM", [128, NCH, C], F32))
        s_M, s_Mev, s_Mst = sem("M"), sem("Mev"), sem("Mst")
        ps = ctx.enter_context(nc.psum_tensor("k_ps", [128, NT, 512], F32))
        s_ld, s_st, s_bst = [sem("ld0"), sem("ld1")], [sem("st0"), sem("st1")], sem("bst")
        s_sq, s_exp, s_ln, s_inv, s_bsev = sem("sq"), sem("exp"), sem("ln"), sem("inv"), sem("bsev")
        s_m, s_out, s_bq, s_dv = sem("max"), sem("out"), sem("bonus"), sem("dv")
        s_ss, s_bsum = sem("ss"), sem("bsum")
        w = io["rw_wk"][0]
        headsum = c_(net, "headsum")
        DV = 8
        block = ctx.enter_context(nc.Block())

        def col(name, b):
            at = PARAM_AT[name]
            return net.param[:, bass.ds(b + at, 1)]

        @block.sync
        def _(sp):
            def body(b, s, i):
                pan.load(sp, b, s, panel_of(w, b * 128))
                sp.wait_ge(s_out, b + 1)
                sp.wait_ge(s_M, b + 1)
                sp.wait_ge(s_st[s], i * 48 + 48)
                for buf, src in ((A, net.sA), (L, net.sL), (Lm, net.sLm), (Rt, net.sRt)):
                    sp.dma_start(buf[:, s, :], row(src, b)).then_inc(s_ld[s], 16)
            around(sp, body)

        @block.gpsimd
        def _(pool):
            with pool.Fori(0, DB // 2) as j:
                for s in range(2):
                    pan.split(pool, j * 2 + s, s, j)

        @block.tensor
        def _(pe):
            def bonus(b, m):
                pe.wait_ge(s_bq, b + 1)
                pe.wait_ge(s_m, m)
                for n in range(NT):
                    ins = pe.matmul(ps[:, n, 0:TT], headsum, bq[:, n * TT:(n + 1) * TT], start=True, stop=True)
                ins.then_inc(s_bsum, 1)

            def systems_ready(b):
                pe.wait_ge(s_out, b + 3)
                pe.wait_ge(s_Mev, b + 1)

            def systems(b, s):
                for c in range(NCH):
                    for h in range(2):
                        r, t = slice(64 * h, 64 * h + 64), slice(c * C, (c + 1) * C)
                        ins = pe.matmul(pM[r, c, :], A[r, s, t], Lm[r, s, t], start=True, stop=True, skip_group_check=True, tile_position=(64 * h, 64 * h))
                ins.then_inc(s_M, 1)

            def squares(b):
                pe.wait_ge(s_bsev, b + 1)
                for n in range(NT):
                    pe.wait_ge(s_sq, b * NT + n + 1)
                    ins = pe.matmul(ps[:, n, 0:TT], headsum, sq[:, n * TT:(n + 1) * TT], start=True, stop=True)
                ins.then_inc(s_ss, 1)

            def body(b, s, i):
                first = isinstance(b, int) and b == 0
                pan.multiply(pe, b, s, net.HH, net.HL, ready=(mix.s_lo, 1))
                if not first:
                    systems_ready(b - 1)
                squares(b)
                if not first:
                    systems(b - 1, 1 - s)
                    bonus(b - 1, b + 2)
            around(pe, body)
            systems_ready(DB - 1)
            pe.wait_ge(s_bsev, DB + 1)
            bonus(DB - 1, DB + 1)
            systems(DB - 1, 1)

        @block.scalar
        def _(act):
            mix.act(act)

            def bonus_out(b):
                act.wait_ge(s_bsum, b + 2)
                act.wait_ge(s_bst, b * 16 + 16)
                act.activation(tiles(bs[:]), ps[:, :, 0:TT], ACT.Copy).then_inc(s_bsev, 1)
                act.wait_ge(s_bsev, b + 3)
                act.dma_start(row(net.sBS, b), bs[:]).then_inc(s_bst, 16)

            def save_systems(b):
                act.wait_ge(s_Mev, b + 2)
                act.dma_start(net.sM[:, bass.ds(b, 1)].rearrange("c a p t -> p c (a t)"), M[:]).then_inc(s_Mst, 16)

            def body(b, s, i):
                first = isinstance(b, int) and b == 0
                act.wait_ge(s_m, b + 1)
                pan.summed(act, b, NT - 1)
                for n in range(NT):
                    t = slice(n * TT, (n + 1) * TT)
                    act.activation(sq[:, t], pan.acc[:, n, 0:TT], ACT.Square, scale=col("rw_kk", b)).then_inc(s_sq, 1)
                act.wait_ge(s_out, b + 2)
                for n in range(NT):
                    t = slice(n * TT, (n + 1) * TT)
                    act.activation(k[:, t], pan.acc[:, n, 0:TT], ACT.Copy).then_inc(pan.free, 1)
                act.wait_ge(s_m, b + 2)
                act.activation(inv[:], sq[:], ACT.Ln).then_inc(s_ln, 1)
                act.wait_ge(s_ln, b + 1)
                act.activation(inv[:], inv[:], ACT.Exp, scale=-0.5).then_inc(s_inv, 1)
                act.wait_ge(s_ld[s], i * 64 + 64)
                act.activation(blk(net.pend, b), L[:, s, C - 1:SEQ:C], ACT.Exp).then_inc(s_exp, 1)
                act.activation(blk(net.Ps, b), L[:, s, SEQ:TOK], ACT.Exp).then_inc(s_exp, 1)
                act.wait_ge(s_exp, b * 4 + 2)
                act.activation(L[:, s, :], L[:, s, :], ACT.Exp, scale=-1.0).then_inc(s_exp, 1)
                act.activation(Lm[:, s, :], Lm[:, s, :], ACT.Exp).then_inc(s_exp, 1)
                if not first:
                    bonus_out(b - 1)
                act.wait_ge(s_out, b + 3)
                if not first:
                    save_systems(b - 1)
                for dst, src in ((net.sAt, Lm[:, s, :]), (net.sBt, A[:, s, :]), (net.sKt, am[:])):
                    act.dma_start(row(dst, b), src).then_inc(s_st[s], 16)
            around(act, body)
            bonus_out(DB - 1)
            save_systems(DB - 1)
            act.wait_ge(s_Mst, 16 * DB + 16)
            for s in range(2):
                act.wait_ge(s_st[s], 5 * 48)
            act.wait_ge(s_bst, 16 * DB + 16)

        @block.vector
        def _(dve):
            dve.sem_inc(pan.low, pan.LOW0)
            dve.sem_inc(pan.done, pan.DONE0)
            dve.sem_inc(pan.free, NT)
            dve.sem_inc(s_out, 2)
            dve.sem_inc(s_bsev, 2)
            dve.sem_inc(s_m, 1)
            dve.sem_inc(s_bsum, 1)
            mix.dve(dve)
            dve.sem_inc(s_bst, 16)
            dve.sem_inc(s_M, 2)
            dve.sem_inc(s_Mev, 1)
            dve.sem_inc(s_Mst, 16)
            for s in range(2):
                dve.sem_inc(s_st[s], 48)
            ka = net.param[:, PARAM_AT["rw_ka"]:PARAM_AT["rw_ka"] + DB]
            dve.tensor_scalar(omka[:], ka, -1.0, 1.0, ALU.mult, ALU.add).then_inc(s_dv, 1)

            at = CONST_AT["lt"]
            lt = net.const[:, at:at + C].unsqueeze(1).to_broadcast([128, NCH, C])

            def mask_systems(b):
                dve.wait_ge(s_M, b + 3)
                dve.wait_ge(s_Mst, b * 16 + 16)
                dve.tensor_tensor(M[:], pM[:], lt, ALU.mult).then_inc(s_Mev, 1)

            dve.wait_ge(s_dv, 1)

            def body(b, s, i):
                ch = Chain(dve, s_dv, DV, b, 1)
                a, e2, e1 = A[:, s, :], L[:, s, :], Lm[:, s, :]
                dve.wait_ge(s_ss, b + 1)
                dve.tensor_scalar(tiles(sq[:]), ps[:, :, 0:TT], 1e-24, float(2 ** 20), ALU.max, ALU.mult).then_inc(s_m, 1)
                dve.wait_ge(s_ld[s], i * 64 + 64)
                dve.wait_ge(pan.free, b * NT + 2 * NT)
                dve.wait_ge(s_st[1 - s], (i + s) * 48 + 48)
                ch.link(dve.tensor_scalar(am[:], a, col("rw_ka", b), omka[:, bass.ds(b, 1)], ALU.mult, ALU.add))
                ch.link(dve.tensor_tensor(am[:], am[:], k[:], ALU.mult))
                ch.link(dve.tensor_scalar(k[:], k[:], col("rw_kk", b), 1024.0, ALU.mult, ALU.mult))
                if not (isinstance(b, int) and b == 0):
                    mask_systems(b - 1)
                dve.wait_ge(s_inv, b + 1)
                ch.link(dve.tensor_tensor(k[:], k[:], inv[:], ALU.mult))
                dve.wait_ge(s_exp, b * 4 + 4)
                ch.link(dve.tensor_tensor(a, a, k[:], ALU.mult))
                ch.link(dve.tensor_tensor(am[:], am[:], e2, ALU.mult))
                ch.link(dve.tensor_tensor(a, a, e2, ALU.mult))
                dve.wait_ge(s_bsum, b + 1)
                dve.scalar_tensor_tensor(out=bq[:], in0=Rt[:, s, :], scalar=col("rw_rk", b), in1=am[:], op0=ALU.mult, op1=ALU.mult).then_inc(s_bq, 1)
                ch.link(dve.scalar_tensor_tensor(out=e1, in0=k[:], scalar=-1.0, in1=e1, op0=ALU.mult, op1=ALU.mult))
                dve.wait_ge(s_bq, b + 1)
                dve.sem_inc(s_out, 1)
                assert ch.n == DV
            around(dve, body)
            mask_systems(DB - 1)


def around(eng, body):
    body(0, 0, 0)
    with eng.Fori(0, DB // 2 - 1) as i:
        body(i * 2 + 1, 1, i)
        body(i * 2 + 2, 0, i + 1)
    body(DB - 1, 1, DB // 2 - 1)


def stage_v(net):
    nc, io = net.nc, net.io
    with ExitStack() as ctx:
        def sb(name, shape, dt=F32):
            return ctx.enter_context(nc.sbuf_tensor(f"v_{name}", shape, dt))

        def sem(name):
            return net.semaphore(f"v_{name}")

        pan = Panels(net, ctx, "vp")
        v, bs = sb("v", [128, 2, TOK]), sb("bs", [128, 2, TOK])
        tok, stok = sb("tok", [128, 2, 4, 128]), sb("stok", [DEC, 128])
        Z, tmp = sb("Z", [128, 2, C * C]), sb("tmp", [128, 2, 1 + TOK])
        mix = Mix(net, ctx, "v", 3, buf=v, hx=tmp)
        tb = [ctx.enter_context(nc.psum_tensor(f"v_tb{i}", [128, 4, 128], F32)) for i in range(3)]
        s_bs, s_v, s_bv, s_bvst = [sem("bs0"), sem("bs1")], sem("v"), sem("bv"), [sem("bvst0"), sem("bvst1")]
        s_t, s_tev, s_vst, s_M, s_z, s_diag, s_zst = sem("t"), sem("tev"), sem("vst"), sem("M"), sem("z"), sem("diag"), sem("zst")
        ada = Ada(net, ctx, "ada1")
        s_mod = sem("mod")
        A0 = 1
        G0 = 1
        NG = 2 * Ada.PER_LAYER - G0
        ident = c_(net, "ident")
        w = io["rw_wv"][0]
        half = NCH // 2
        systems = lambda t: t.rearrange("(g c) b (r s) t -> g (c b r) (s t)", g=2, r=2)
        block = ctx.enter_context(nc.Block())

        @block.sync
        def _(sp):

            def body(b, s, i, ada_from=None):
                if not (isinstance(b, int) and b == DB - 1):
                    pan.load(sp, b + 1, 1 - s, panel_of(w, b * 128 + 128))
                if ada_from:
                    ada.load(sp, b - A0, *ada_from)
                sp.wait_ge(s_bvst[s], i * 16 + 16)
                sp.dma_start(bs[:, s, :], row(net.sBS, b)).then_inc(s_bs[s], 16)

            pan.load(sp, 0, 0, panel_of(w, 0))
            for g in range(2):
                sp.dma_start(Z[:, g, :], systems(net.sM)[g]).then_inc(s_M, 16)
            body(0, 0, 0)
            body(1, 1, 0, (1, 0))
            with sp.Fori(1, DB // 2 - 1) as i:
                for s in range(2):
                    body(i * 2 + s, s, i, (i - 1, (1 + s) * Ada.GROUP))
            body(DB - 2, 0, DB // 2 - 1)
            body(DB - 1, 1, DB // 2 - 1)
            for g in range(2):
                sp.wait_ge(s_z, 4 * (C - 2) - 1 + g)
                sp.wait_ge(s_diag, 1)
                sp.dma_start(systems(net.sT)[g], Z[:, g, :]).then_inc(s_zst, 16)
            sp.wait_ge(s_zst, 32)

        @block.gpsimd
        def _(pool):
            def product(b, s, i):
                pool.wait_ge(s_v, b * NT + NT)
                pool.wait_ge(s_bs[s], i * 16 + 16)
                pool.tensor_tensor(bs[:, s, :], bs[:, s, :], v[:, s, :], ALU.mult).then_inc(s_bv, 1)

            def body(b, s, i):
                pan.split(pool, b, s, i)
                if not (isinstance(b, int) and b == 0):
                    product(b - 1, 1 - s, i + s - 1)
            around(pool, body)
            product(DB - 1, 1, DB // 2 - 1)

        @block.tensor
        def _(pe):
            def turn(b, s):
                pe.wait_ge(s_v, b * NT + NT)
                for h in range(2):
                    pe.wait_ge(s_tev, b * 3 + h + 1)
                    for q in range(4):
                        t = (4 * h + q) * 128
                        ins = pe.transpose(tb[h][:, q, :], v[:, s, t:t + 128], ident)
                    ins.then_inc(s_t, 1)
                pe.wait_ge(s_tev, b * 3 + 3)
                pe.transpose(tb[2][0:DEC, 0, :], v[:, s, SEQ:TOK], ident).then_inc(s_t, 1)

            def body(b, s, with_ada=False):
                pan.multiply(pe, b, s, net.HH, net.HL, ready=(mix.s_lo, 1))
                if with_ada:
                    ada.multiply(pe, b - A0)
                if not (isinstance(b, int) and b == 0):
                    turn(b - 1, 1 - s)
                if with_ada:
                    ada.turn(pe, b - A0)

            pe.sem_inc(ada.s_used, ada.SLOTS)
            body(0, 0)
            body(1, 1, True)
            with pe.Fori(1, DB // 2 - 1) as i:
                for s in range(2):
                    body(i * 2 + s, s, True)
            body(DB - 2, 0)
            body(DB - 1, 1)
            turn(DB - 1, 1)

        @block.scalar
        def _(act):
            mix.act(act)

            def out(b):
                act.wait_ge(s_vst, b * 48 + 48)
                for h in range(2):
                    act.wait_ge(s_t, b * 3 + h + 1)
                    act.activation(tok[:, h], tb[h][:], ACT.Copy).then_inc(s_tev, 1)
                act.wait_ge(s_t, b * 3 + 3)
                act.activation(stok[:], tb[2][0:DEC, 0, :], ACT.Copy).then_inc(s_tev, 1)
                act.wait_ge(s_tev, b * 3 + 6)
                cols = net.sV[:, bass.ds(b * 128, 128)]
                for h in range(2):
                    act.dma_start(cols[512 * h:512 * h + 512].rearrange("(q p) c -> p q c", p=128), tok[:, h]).then_inc(s_vst, 16)
                act.dma_start(cols[SEQ:TOK], stok[:]).then_inc(s_vst, 16)

            def product_out(b, s):
                act.wait_ge(s_bv, b + 1)
                act.dma_start(row(net.sBV, b), bs[:, s, :]).then_inc(s_bvst[s], 16)

            def body(b, s, i, ada_to=None):
                if not (isinstance(b, int) and b < 2):
                    act.wait_ge(s_bv, b - 1)
                    act.wait_ge(s_t, b * 3 - 3)
                for n in range(NT):
                    t = slice(n * TT, (n + 1) * TT)
                    pan.summed(act, b, n)
                    act.activation(v[:, s, t], pan.acc[:, n, 0:TT], ACT.Copy).then_inc(s_v, 1)
                act.wait_ge(s_v, b * NT + NT)
                act.sem_inc(pan.free, NT)
                if not (isinstance(b, int) and b == 0):
                    product_out(b - 1, 1 - s)
                if ada_to is not None:
                    ada.strips_out(act, b - A0)
                if not (isinstance(b, int) and b == 0):
                    out(b - 1)
                if ada_to is not None:
                    ada.turned_out(act, b - A0, ada_to)

            body(0, 0, 0)
            body(1, 1, 0, N_ADA * DB)
            with act.Fori(1, DB // 2 - 1) as i:
                for s in range(2):
                    body(i * 2 + s, s, i, (i - 1) * N_ADA * DB + (1 + s) * 2 * DB)
            body(DB - 2, 0, DB // 2 - 1)
            body(DB - 1, 1, DB // 2 - 1)
            out(DB - 1)
            product_out(DB - 1, 1)
            act.wait_ge(s_vst, DB * 48 + 48)
            for s in range(2):
                act.wait_ge(s_bvst[s], 16 * (DB // 2) + 16)

        @block.vector
        def _(dve):
            dve.sem_inc(pan.low, pan.LOW0)
            dve.sem_inc(pan.done, pan.DONE0)
            dve.sem_inc(pan.free, NT)
            dve.sem_inc(s_tev, 3)
            dve.sem_inc(s_vst, 48)
            dve.sem_inc(ada.s_strip, 1)
            dve.sem_inc(ada.s_mod, 1)
            for s in range(2):
                dve.sem_inc(s_bvst[s], 16)
            mix.dve(dve)
            dve.wait_ge(s_M, 32)
            n = 0
            for s in range(1, C - 1):
                for g in range(2):
                    z = Z[:, g, :].rearrange("p (u t) -> p u t", t=C)
                    if n >= 2:
                        dve.wait_ge(s_z, n - 1)
                    shape = [128, s, C - 1 - s]
                    p = tmp[:, g, 0:s * (C - 1 - s)].rearrange("p (u t) -> p u t", u=s)
                    dve.tensor_tensor(p, z[:, 0:s, s:s + 1].to_broadcast(shape), z[:, s:s + 1, s + 1:C].to_broadcast(shape), ALU.mult).then_inc(s_z, 1)
                    n += 1
                for g in range(2):
                    z = Z[:, g, :].rearrange("p (u t) -> p u t", t=C)
                    shape = [128, s, C - 1 - s]
                    p = tmp[:, g, 0:s * (C - 1 - s)].rearrange("p (u t) -> p u t", u=s)
                    dve.wait_ge(s_z, n - 1)
                    dve.tensor_tensor(z[:, 0:s, s + 1:C], z[:, 0:s, s + 1:C], p, ALU.add).then_inc(s_z, 1)
                    n += 1
            dve.memset(Z[:, :, 0:C * C:C + 1], 1.0).then_inc(s_diag, 1)
            dve.wait_ge(ada.s_mod, NG + 1)
            add_ada_bias(dve, net, G0 * 2 * DB, NG * 2 * DB, s_mod)
            dve.wait_ge(s_mod, 1)
            for slot in range(1, 4):
                make_gain(dve, net, slot, s_mod)
            dve.wait_ge(s_mod, 4)


class Samples:

    ROWS = HD // NCH
    LINKS = 9

    def __init__(self, net, ctx):
        nc = net.nc
        self.net = net

        def sb(name, shape):
            return ctx.enter_context(nc.sbuf_tensor(f"step_{name}", shape, F32))

        sem = lambda name: net.semaphore(f"step_{name}")
        self.cols = sb("cols", [128, 4, DB, DEC])
        self.rows = sb("rows", [DEC, 5, D])
        self.vec = sb("vec", [128, 6, HD])
        self.S = sb("S", [128, HD, HD])
        self.t1, self.t2, self.t3 = (sb(n, [128, self.ROWS, HD]) for n in ("t1", "t2", "t3"))
        self.sa, self.y = sb("sa", [128, self.ROWS]), sb("y", [128, HD])
        self.s_in, self.s_S, self.s_t, self.s_tev = sem("in"), sem("S"), sem("t"), sem("tev")
        self.s_rows, self.s_vec, self.s_dv, self.s_out = sem("rows"), sem("vec"), sem("dv"), sem("out")

    def load(self, sp):
        net = self.net
        for i, src in enumerate((net.sAt, net.sRt, net.sBt, net.sKt)):
            sp.dma_start(self.cols[:, i], src[:, :, SEQ:TOK].rearrange("b p t -> p b t")).then_inc(self.s_in, 16)
        sp.dma_start(self.vec[:, 5, :], net.sV[SEQ:TOK].rearrange("s (h d) -> (s h) d", d=HD)).then_inc(self.s_vec, 16)

    def turn(self, pe, banks):
        pe.wait_ge(self.s_in, 64)
        for n in range(10):
            i, h = n // 2, n % 2
            if n >= 2:
                pe.wait_ge(self.s_tev, n - 1)
            for q in range(4):
                src = self.cols[:, i, 4 * h + q, :] if i < 4 else self.net.Ps[:, 4 * h + q, :]
                ins = pe.transpose(banks[n % 2][0:DEC, q, :], src, c_(self.net, "ident"))
            ins.then_inc(self.s_t, 1)
        pe.wait_ge(self.s_tev, 10)

    def spread(self, act, banks):
        act.dma_start(self.S[:], self.net.io["state_wkv"][0].rearrange("s h i j -> (s h) i j")).then_inc(self.s_S, 16)
        for n in range(10):
            act.wait_ge(self.s_t, n + 1)
            act.activation(self.rows[:, n // 2, (n % 2) * 512:(n % 2) * 512 + 512].rearrange("s (q c) -> s q c", q=4), banks[n % 2][0:DEC], ACT.Copy).then_inc(self.s_tev, 1)
        act.wait_ge(self.s_tev, 10)
        act.dma_start(self.net.sSmp.rearrange("i s c -> s i c"), self.rows[:]).then_inc(self.s_rows, 16)
        act.wait_ge(self.s_rows, 16)
        for i in range(5):
            act.dma_start(self.vec[:, i, :], self.net.sSmp[i].rearrange("s (h d) -> (s h) d", d=HD)).then_inc(self.s_vec, 16)

    def step(self, dve, c, part):
        At, Rt, Bt, Kt, P, V = (self.vec[:, i, :] for i in range(6))
        shape = [128, self.ROWS, HD]
        along_j = lambda x: x.unsqueeze(1).to_broadcast(shape)
        along_i = lambda x: x.unsqueeze(2).to_broadcast(shape)
        rows = bass.ds(c * self.ROWS, self.ROWS)
        S, t1, t2, t3, sa, y = self.S[:, rows, :], self.t1[:], self.t2[:], self.t3[:], self.sa[:], self.y[:, rows]
        work = [
            lambda: dve.tensor_tensor(t1, S, along_j(At), ALU.mult),
            lambda: dve.tensor_tensor(t3, along_i(V[:, rows]), along_j(Kt), ALU.mult),
            lambda: dve.tensor_reduce(sa, t1, AX, ALU.add),
            lambda: dve.tensor_tensor(S, S, t3, ALU.add),
            lambda: dve.tensor_tensor(t2, along_i(sa), along_j(Bt), ALU.mult),
            lambda: dve.tensor_tensor(S, S, t2, ALU.add),
            lambda: dve.tensor_tensor(t1, S, along_j(Rt), ALU.mult),
            lambda: dve.tensor_reduce(y, t1, AX, ALU.add),
            lambda: dve.tensor_tensor(S, S, along_j(P), ALU.mult),
        ]
        assert len(work) == self.LINKS
        reads_last = (0, 2, 3, 4, 5, 6, 7, 8)
        for n in range(3 * part, 3 * part + 3):
            if n in reads_last:
                dve.wait_ge(self.s_dv, c * self.LINKS + n + 1)
            work[n]().then_inc(self.s_dv, 1)

    def store(self, sp):
        sp.wait_ge(self.s_dv, NCH * self.LINKS + 1)
        sp.dma_start(self.net.io["out_wkv_sample"][0].rearrange("s h i j -> (s h) i j"), self.S[:]).then_inc(self.s_out, 16)
        sp.dma_start(self.net.sY.rearrange("s (h d) -> (s h) d", d=HD), self.y[:]).then_inc(self.s_out, 16)
        sp.wait_ge(self.s_out, 32)


def stage_scan(net):
    nc, io = net.nc, net.io
    Q = DB // 2
    BODY = 4
    with ExitStack() as ctx:
        def sb(name, shape, dt=F32):
            return ctx.enter_context(nc.sbuf_tensor(f"c_{name}", shape, dt))

        def sem(name):
            return net.semaphore(f"c_{name}")

        ARI = sb("ARI", [128, 2, DB, 3, 2, C])
        BK = sb("BK", [128, 2, 2, 2, DB, 128])
        Z = sb("Z", [128, 2, 2, DB, C])
        V = sb("V", [128, 2, 2, DB, 128])
        G = sb("G", [128, 2, DB, 5, C])
        S, U, SA = sb("S", [128, DB, 128]), sb("U", [128, DB, 128]), sb("SA", [128, DB, 128])
        Sd = sb("Sd", [128, DB, 128])
        eye = sb("eye", [128, C])
        Y = sb("Y", [128, BODY, Q, 128])
        ysq = sb("ysq", [128, Q * 2, HD])
        ym, yv, yi = (sb(n, [128, Q * 2]) for n in ("ym", "yv", "yi"))
        Yt = sb("Yt", [128, 2, DB, 2, C])
        St = sb("St", [128, DB, 128])
        pU, pSA, pD, pY, pB, pT = (ctx.enter_context(nc.psum_tensor(f"c_p{n}", [128, Q, 128], F32)) for n in ("U", "A", "D", "Y", "B", "T"))
        pK = ctx.enter_context(nc.psum_tensor("c_pK", [128, 2, 512], F32))
        smp = Samples(net, ctx)
        s_zero, s_zero2, s_ld = sem("zero"), sem("zero2"), [sem("ld0"), sem("ld1")]
        s_U, s_SA, s_D, s_Y, s_G, s_Gev = sem("U"), sem("SA"), sem("D"), sem("Y"), sem("G"), sem("Gev")
        s_Ua, s_Ud, s_Sa, s_Sd, s_S = sem("Ua"), sem("Ud"), sem("Sa"), sem("Sd"), sem("S")
        s_dec, s_dS, s_eye = sem("dec"), sem("dS"), sem("eye")
        s_ym, s_yc, s_ysq, s_yv, s_yr, s_yi, s_yn = sem("ym"), sem("yc"), sem("ysq"), sem("yv"), sem("yr"), sem("yi"), sem("yn")
        s_yT, s_yTe, s_ydv, s_yz = sem("yT"), sem("yTe"), sem("ydv"), sem("yz")
        s_Yev, s_yst = sem("Yev"), [sem("yst0"), sem("yst1")]
        s_T, s_Tev, s_out = sem("T"), sem("Tev"), sem("out")
        ident = c_(net, "ident")
        lt_at, le_at = CONST_AT["lt"], CONST_AT["le"]
        maskK = net.const[:, lt_at:lt_at + 192].unsqueeze(1).unsqueeze(1).to_broadcast([128, 2, 2, 192])
        maskB = net.const[:, le_at:le_at + 128].unsqueeze(1).to_broadcast([128, 4, 128])
        LOADS = 15
        Y0 = 3
        block = ctx.enter_context(nc.Block())

        def chunks(eng, work):
            with eng.Fori(0, NCH // BODY - 1) as i:
                for k in range(BODY):
                    work(i * BODY + k, k, i, False)
            for k in range(BODY):
                work(NCH - BODY + k, k, NCH // BODY - 1, k == BODY - 1)

        heads = lambda y: y.rearrange("p q (a d) -> p (q a) d", a=2)
        each = lambda x: x.unsqueeze(2).to_broadcast([128, Q * 2, HD])

        @block.sync
        def _(sp):
            smp.load(sp)
            with sp.Fori(0, NCH // BODY) as i:
                for s in range(2):
                    two = i * 2 + s
                    sp.wait_ge(s_Y, two * 2 + 1)
                    t = bass.ds(two * 2 * C, 2 * C)
                    for n, src in enumerate((net.sAt, net.sRt)):
                        sp.dma_start(ARI[:, s, :, n].rearrange("p b c t -> p b (c t)"), src[:, :, t].rearrange("b p t -> p b t")).then_inc(s_ld[s], 16)
                    sp.dma_start(Z[:, s].rearrange("p c b t -> p (c b) t"), net.sT[bass.ds(two * 2, 2)].rearrange("c b p t -> p (c b) t")).then_inc(s_ld[s], 16)
                    sp.wait_ge(s_zero, 4)
                    sp.wait_ge(s_zero2, 2)
                    for n, src in enumerate((net.sBt, net.sKt)):
                        for h in range(2):
                            r = slice(64 * h, 64 * h + 64)
                            for c in range(2):
                                sp.dma_start(BK[r, s, c, n, :, r], src[:, r, bass.ds(two * 2 * C + c * C, C)].rearrange("b p t -> p b t")).then_inc(s_ld[s], 16)
                    for c in range(2):
                        rows = net.sV[bass.ds(two * 2 * C + c * C, C)].rearrange("t (b h d) -> h t b d", h=2, d=HD)
                        for h in range(2):
                            r = slice(64 * h, 64 * h + 64)
                            sp.dma_start(V[r, s, c, :, r], rows[h]).then_inc(s_ld[s], 16)

            smp.store(sp)

        @block.gpsimd
        def _(pool):
            pool.memset(BK[:, 1], 0.0).then_inc(s_zero2, 1)
            pool.memset(V[:], 0.0).then_inc(s_zero2, 1)
            pool.wait_ge(s_eye, 2)

            def work(c, k, i, last):
                s, cc = k // 2, k % 2
                decay = net.pend[:, :, bass.ds(c, 1)]
                pool.wait_ge(s_S, c + 1)
                pool.wait_ge(s_D, c + 1)
                if not last:
                    diagonal(c + 1, (k + 1) % BODY)
                pool.tensor_tensor(Sd[:], S[:], decay.to_broadcast([128, DB, 128]), ALU.mult).then_inc(s_dS, 1)
                normalise(c, k)

            def normalise(c, k):
                y = heads(Y[:, (k - 3) % BODY])
                pool.wait_ge(s_yi, c + 1)
                pool.tensor_tensor(y, y, each(yi[:]), ALU.mult).then_inc(s_yn, 1)
                y = heads(Y[:, (k - 1) % BODY])
                pool.wait_ge(s_ym, c + 1)
                pool.tensor_tensor(y, y, each(ym[:]), ALU.subtract).then_inc(s_yc, 1)
                pool.wait_ge(s_yc, c + 2)
                pool.wait_ge(s_yv, c + 1)
                pool.tensor_tensor(ysq[:], y, y, ALU.mult).then_inc(s_ysq, 1)

            def diagonal(c, k):
                pool.wait_ge(s_Y, c + 1)
                pool.tensor_tensor(ARI[:, k // 2, :, 2, k % 2, :], eye[:].unsqueeze(1).to_broadcast([128, DB, C]),
                                   net.pend[:, :, bass.ds(c, 1)].to_broadcast([128, DB, C]), ALU.mult).then_inc(s_dec, 1)

            diagonal(0, 0)
            chunks(pool, work)
            for k in range(Y_LAG):
                normalise(NCH + k, k)

        @block.tensor
        def _(pe):
            def mm(out, b, lhsT, rhs, start, stop):
                h = b % 2
                return pe.matmul(out[64 * h:64 * h + 64, b // 2, :], lhsT, rhs, start=start, stop=stop, skip_group_check=True, tile_position=(0, 64 * h))

            def grams(c, k, i, half):
                s, cc = k // 2, k % 2
                if half == 0 and cc == 0:
                    pe.wait_ge(s_ld[s], i * 16 * LOADS + 16 * LOADS)
                pe.wait_ge(s_dec, c + 1)
                pe.wait_ge(s_Gev, c * 4 + half * 2 + 2)
                for q in range(4):
                    b = 4 * half + q
                    pe.matmul(pB[:, q, :], BK[:, s, cc, 0, b, :], ARI[:, s, b, 1:3, cc, :], start=True, stop=True, skip_group_check=True)
                    ins = pe.matmul(pK[:, q // 2, (q % 2) * 192:(q % 2) * 192 + 192], BK[:, s, cc, 1, b, :], ARI[:, s, b, :, cc, :], start=True, stop=True, skip_group_check=True)
                ins.then_inc(s_G, 1)

            def chunk(c, k, i, last):
                s, cc, g = k // 2, k % 2, k % 2
                pe.wait_ge(s_S, c + 1)
                pe.wait_ge(s_Ua, c + 1)
                pe.wait_ge(s_Ud, c + 1)
                for b in range(DB):
                    mm(pU, b, ARI[:, s, b, 0, cc, :], S[:, b, :], b < 2, False)
                pe.wait_ge(s_Gev, c * 4 + 6)
                for b in range(DB):
                    ins = mm(pU, b, G[:, g, b, 2, :], V[:, s, cc, b, :], False, True)
                ins.then_inc(s_U, 1)
                ahead = (c + 1, (k + 1) % BODY, i + (k + 1) // BODY)
                if not last:
                    grams(*ahead, 0)
                pe.wait_ge(s_Ua, c + 2)
                pe.wait_ge(s_Ud, c + 2)
                for b in range(DB):
                    ins = mm(pSA, b, Z[:, s, cc, b, :], U[:, b, :], b < 2, True)
                ins.then_inc(s_SA, 1)
                pe.wait_ge(s_Yev, c + 1)
                for b in range(DB):
                    mm(pD, b, G[:, g, b, 4, :], V[:, s, cc, b, :], b < 2, False)
                for b in range(DB):
                    mm(pY, b, ARI[:, s, b, 1, cc, :], S[:, b, :], b < 2, False)
                pe.wait_ge(s_Sa, c + 2)
                pe.wait_ge(s_Sd, c + 2)
                for b in range(DB):
                    ins = mm(pD, b, G[:, g, b, 1, :], SA[:, b, :], False, True)
                ins.then_inc(s_D, 1)
                for b in range(DB):
                    mm(pY, b, G[:, g, b, 3, :], V[:, s, cc, b, :], False, False)
                    ins = mm(pY, b, G[:, g, b, 0, :], SA[:, b, :], False, True)
                ins.then_inc(s_Y, 1)
                if not last:
                    grams(*ahead, 1)
                turn(c, k)

            def turn(c, k):
                pe.wait_ge(s_yn, c + 2)
                pe.wait_ge(s_yTe, c + 1)
                for q in range(Q):
                    ins = pe.transpose(pT[:, q, :], Y[:, (k - Y_LAG) % BODY, q, :], ident)
                ins.then_inc(s_yT, 1)

            smp.turn(pe, (pT, pY))
            for half in range(2):
                grams(0, 0, 0, half)
            pe.wait_ge(s_yz, 1)
            chunks(pe, chunk)
            for k in range(Y_LAG):
                turn(NCH + k, k)
            pe.wait_ge(s_yTe, NCH + Y_LAG + 1)
            pe.wait_ge(s_S, NCH + 1)
            for n in range(2):
                pe.wait_ge(s_Tev, n + 1)
                for q in range(4):
                    ins = pe.transpose(pT[:, q, :], S[:, 4 * n + q, :], ident)
                ins.then_inc(s_T, 1)

        def halves(h, out, src):
            for a in range(2):
                r = slice(64 * a, 64 * a + 64)
                yield out[r, h::2, r], src[64 * h:64 * h + 64, :, r]

        @block.scalar
        def _(act):
            smp.spread(act, (pT, pY))

            def work(c, k, i, last):
                act.wait_ge(s_U, c + 1)
                for o, p in halves(0, U, pU):
                    ins = act.activation(o, p, ACT.Copy)
                ins.then_inc(s_Ua, 1)
                act.wait_ge(s_SA, c + 1)
                for o, p in halves(0, SA, pSA):
                    ins = act.activation(o, p, ACT.Copy)
                ins.then_inc(s_Sa, 1)
                root(c)
                act.wait_ge(s_Y, c + 1 + Y0)
                act.activation(Y[:, k], pY[:], ACT.Copy).then_inc(s_Yev, 1)
                turned(c, k, i)

            def turned(c, k, i):
                e = (k - Y_LAG) % BODY
                slot, place = e // 2, e % 2
                act.wait_ge(s_yT, c + 1)
                if k == 1:
                    act.wait_ge(s_yst[1], i * 16 + 16)
                elif k == 3:
                    act.wait_ge(s_yst[0], i * 16 + 16)
                act.activation(Yt[:, slot, :, place, :].rearrange("p (q h) t -> p q h t", h=2), pT[:].rearrange("p q (h t) -> p q h t", h=2), ACT.Copy).then_inc(s_yTe, 1)
                if place == 1:
                    act.wait_ge(s_yTe, c + 2)
                    act.dma_start(net.sYc[:, :, bass.ds(c * C, 2 * C)].rearrange("b p t -> p b t"), Yt[:, slot].rearrange("p b c t -> p b (c t)")).then_inc(s_yst[slot], 16)

            def root(c):
                act.wait_ge(s_yv, c + 1)
                act.activation(yv[:], yv[:], ACT.Sqrt).then_inc(s_yr, 1)

            act.wait_ge(s_yz, 1)
            chunks(act, work)
            for k in range(Y_LAG):
                root(NCH + k)
                turned(NCH + k, k, NCH // BODY)
            for n in range(2):
                act.wait_ge(s_T, n + 1)
                act.activation(St[:, 4 * n:4 * n + 4, :], pT[:], ACT.Copy).then_inc(s_Tev, 1)
            act.wait_ge(s_Tev, 3)
            for h in range(2):
                r = slice(64 * h, 64 * h + 64)
                act.dma_start(io["out_wkv_prompt"][0, 0].rearrange("(b h) i j -> h i b j", h=2)[h], St[r, :, r]).then_inc(s_out, 16)
            act.wait_ge(s_yst[0], (NCH // BODY + 1) * 16)
            act.wait_ge(s_yst[1], (NCH // BODY + 1) * 16 + 16)
            act.wait_ge(s_out, 32)

        @block.vector
        def _(dve):
            for buf in (BK[:, 0], U[:], SA[:], S[:]):
                dve.memset(buf, 0.0).then_inc(s_zero, 1)
            for h in range(2):
                r = slice(64 * h, 64 * h + 64)
                dve.tensor_copy(eye[r], ident[r, r]).then_inc(s_eye, 1)
            for n, buf in enumerate((Y, ysq, Yt)):
                dve.memset(buf[:], 0.0).then_inc(s_ydv, 1)
            dve.memset(yv[:], 1.0).then_inc(s_ydv, 1)
            dve.wait_ge(s_ydv, 4)
            dve.sem_inc(s_yz, 1)
            dve.wait_ge(s_zero, 4)
            dve.sem_inc(s_S, 1)
            dve.sem_inc(s_Y, Y0)
            dve.sem_inc(s_Gev, 2)
            dve.sem_inc(s_yst[1], 16)
            for x in (s_yc, s_ysq, s_yn, s_yr, s_yTe, smp.s_dv, s_Yev, s_Ua, s_Ud, s_Sa, s_Sd, s_Tev, s_D):
                dve.sem_inc(x, 1)
            def masked(c, g, half):
                dve.wait_ge(s_G, c * 2 + half + 1)
                b = slice(4 * half, 4 * half + 4)
                dve.tensor_tensor(G[:, g, b, 0:2].rearrange("p b i t -> p b (i t)"), pB[:], maskB, ALU.mult).then_inc(s_Gev, 1)
                dve.tensor_tensor(G[:, g, b, 2:5].rearrange("p (q b) i t -> p q b (i t)", q=2), pK[:, :, 0:384].rearrange("p q (b x) -> p q b x", b=2), maskK, ALU.mult).then_inc(s_Gev, 1)

            def work(c, k, i, last):
                g = k % 2
                dve.wait_ge(s_U, c + 1)
                for o, p in halves(1, U, pU):
                    ins = dve.tensor_copy(o, p)
                ins.then_inc(s_Ud, 1)
                inverse(c)
                smp.step(dve, c, 0)
                if not last:
                    dve.wait_ge(s_Y, c + Y0)
                    masked(c + 1, 1 - g, 0)
                dve.wait_ge(s_SA, c + 1)
                for o, p in halves(1, SA, pSA):
                    ins = dve.tensor_copy(o, p)
                ins.then_inc(s_Sd, 1)
                smp.step(dve, c, 1)
                variance(c)
                dve.wait_ge(s_D, c + 2)
                dve.wait_ge(s_dS, c + 1)
                for h in range(2):
                    for (o, p), (d, _) in zip(halves(h, S, pD), halves(h, Sd, pD)):
                        ins = dve.tensor_tensor(o, p, d, ALU.add)
                ins.then_inc(s_S, 1)
                smp.step(dve, c, 2)
                mean(c, k, c)
                if not last:
                    masked(c + 1, 1 - g, 1)

            def mean(c, k, made):
                dve.wait_ge(s_Yev, made + 1)
                dve.wait_ge(s_yc, c + 1)
                dve.tensor_reduce(ym[:], heads(Y[:, (k - 1) % BODY]), AX, ALU.add).then_inc(s_ydv, 1)
                dve.wait_ge(s_ydv, 4 + c * 2 + 2)
                dve.tensor_scalar(ym[:], ym[:], 1.0 / HD, None, ALU.mult).then_inc(s_ym, 1)

            def variance(c):
                dve.wait_ge(s_ysq, c + 1)
                dve.tensor_reduce(yv[:], ysq[:], AX, ALU.add).then_inc(s_ydv, 1)
                dve.wait_ge(s_ydv, 4 + c * 2 + 1)
                dve.tensor_scalar(yv[:], yv[:], 1.0 / HD, LNX_EPS, ALU.mult, ALU.add).then_inc(s_yv, 1)

            def inverse(c):
                dve.wait_ge(s_yr, c + 1)
                dve.wait_ge(s_yn, c + 1)
                dve.reciprocal(yi[:], yv[:]).then_inc(s_yi, 1)

            for half in range(2):
                masked(0, 0, half)
            dve.wait_ge(smp.s_S, 16)
            dve.wait_ge(smp.s_vec, 96)
            chunks(dve, work)
            for k in range(Y_LAG):
                inverse(NCH + k)
                dve.wait_ge(s_yi, NCH + k + 1)
                variance(NCH + k)
                mean(NCH + k, k, NCH)




class Project:

    def __init__(self, net, ctx, tag, w, gate):
        self.net, self.w, self.gate = net, w, gate
        self.pan = Panels(net, ctx, tag)
        self.smp = ctx.enter_context(net.nc.sbuf_tensor(f"{tag}_smp", [128, DEC], F32))
        self.s_smp = net.semaphore(f"{tag}_smp")

    def sp(self, sp):
        with sp.Fori(0, DB // 2) as j:
            for s in range(2):
                self.load(sp, j, s)

    def load(self, sp, j, s):
        self.pan.load(sp, j * 2 + s, s, panel_of(self.w, j * 256 + s * 128))

    def pool(self, pool):
        with pool.Fori(0, DB // 2) as j:
            for s in range(2):
                self.pan.split(pool, j * 2 + s, s, j)

    def pe(self, pe, ready=None):
        with pe.Fori(0, DB // 2) as j:
            for s in range(2):
                self.pan.multiply(pe, j * 2 + s, s, self.net.HH, self.net.HL, ready=ready)

    def dve_start(self, dve):
        dve.sem_inc(self.pan.low, self.pan.LOW0)
        dve.sem_inc(self.pan.done, self.pan.DONE0)
        dve.sem_inc(self.pan.free, NT)

    def dve(self, dve):
        with dve.Fori(0, DB // 2) as j:
            for s in range(2):
                m = j * 2 + s
                add_gated(dve, self.net, self.pan, m, m, self.gate, self.smp[:], self.pan.free, self.s_smp, m)


def stage_rwkv_out(net):
    nc, io = net.nc, net.io
    with ExitStack() as ctx:
        def sb(name, shape, dt=F32):
            return ctx.enter_context(nc.sbuf_tensor(f"o_{name}", shape, dt))

        def sem(name):
            return net.semaphore(f"o_{name}")

        proj = Project(net, ctx, "op", io["rw_wo"][0], mod_part(net, 0, 2))
        rows, sq = sb("rows", [DEC, D]), sb("sq", [DEC, D])
        mean, var = sb("mean", [DEC, HEADS]), sb("var", [DEC, HEADS])
        smp = sb("smp", [128, DB, DEC])
        slots = 4
        y, bv, g = (sb(n, [128, slots, TOK]) for n in ("y", "bv", "g"))
        tb = ctx.enter_context(nc.psum_tensor("o_tb", [128, 2, 4, 128], F32))
        s_x, s_y, s_root, s_n, s_t, s_tev = sem("x"), sem("y"), sem("root"), sem("n"), sem("t"), sem("tev")
        s_var, s_dv = sem("var"), sem("dv")
        s_bg, s_in, s_aff, s_u, s_hi, s_lo = [sem(f"bg{s}") for s in range(slots)], sem("in"), sem("aff"), sem("u"), sem("hi"), sem("lo")
        ident = c_(net, "ident")
        block = ctx.enter_context(nc.Block())

        @block.sync
        def _(sp):
            def load(b):
                s = b % slots
                if b >= slots:
                    sp.wait_ge(s_lo, b - slots + 1)
                sp.dma_start(y[:, s, 0:SEQ], net.sYc[b][:, Y_PAD * C:Y_PAD * C + SEQ]).then_inc(s_bg[s], 16)
                sp.dma_start(bv[:, s, :], net.sBV[b]).then_inc(s_bg[s], 16)
                sp.dma_start(g[:, s, :], net.sG[b]).then_inc(s_bg[s], 16)

            sp.dma_start(rows[:], net.sY).then_inc(s_y, 16)
            load(0)
            for s in range(2):
                proj.load(sp, 0, s)
            for b in range(1, DB):
                load(b)
            sp.dma_start(net.X[:], net.x_saved).then_inc(s_x, 16)
            with sp.Fori(1, DB // 2) as j:
                for s in range(2):
                    proj.load(sp, j, s)

        @block.gpsimd
        def _(pool):
            proj.pool(pool)

        @block.tensor
        def _(pe):
            pe.wait_ge(s_n, 1)
            for b in range(DB):
                ins = pe.transpose(tb[:, b // 4, b % 4, 0:DEC], rows[:, b * 128:(b + 1) * 128], ident[0:DEC, 0:DEC])
            ins.then_inc(s_t, 1)
            proj.pe(pe, ready=(s_lo, 1))

        @block.scalar
        def _(act):
            act.wait_ge(s_var, 1)
            act.activation(var[:], var[:], ACT.Sqrt).then_inc(s_root, 1)
            act.wait_ge(s_t, 1)
            act.activation(smp[:].rearrange("p (h q) v -> p h q v", h=2), tb[:, :, :, 0:DEC], ACT.Copy).then_inc(s_tev, 1)

            def affine(b):
                x = y[:, b % slots, :]
                gain, shift = (net.param[:, PARAM_AT[n] + b:PARAM_AT[n] + b + 1] for n in ("rw_lnx_g", "rw_lnx_b"))
                act.wait_ge(s_in, b + 1)
                act.activation(x, x, ACT.Identity, bias=shift, scale=gain).then_inc(s_aff, 1)

            affine(0)
            for b in range(DB):
                if b + 1 < DB:
                    affine(b + 1)
                act.wait_ge(s_u, b * 2 + 2)
                act.activation(net.HH[:, b, :], y[:, b % slots, :], ACT.Copy).then_inc(s_hi, 1)

        @block.vector
        def _(dve):
            proj.dve_start(dve)
            ch = Chain(dve, s_dv)
            x = rows[:].rearrange("p (h d) -> p h d", d=HD)
            q = sq[:].rearrange("p (h d) -> p h d", d=HD)
            each = lambda v: v.unsqueeze(2).to_broadcast([DEC, HEADS, HD])
            dve.wait_ge(s_y, 16)
            ch.link(dve.tensor_reduce(mean[:], x, AX, ALU.add))
            ch.link(dve.tensor_scalar(mean[:], mean[:], 1.0 / HD, None, ALU.mult))
            ch.link(dve.tensor_tensor(x, x, each(mean[:]), ALU.subtract))
            ch.link(dve.tensor_tensor(q, x, x, ALU.mult))
            ch.link(dve.tensor_reduce(var[:], q, AX, ALU.add))
            dve.tensor_scalar(var[:], var[:], 1.0 / HD, LNX_EPS, ALU.mult, ALU.add).then_inc(s_var, 1)
            dve.wait_ge(s_root, 1)
            ch.link(dve.reciprocal(var[:], var[:]))
            dve.tensor_tensor(x, x, each(var[:]), ALU.mult).then_inc(s_n, 1)
            dve.wait_ge(s_tev, 1)

            def samples(b):
                dve.wait_ge(s_bg[b % slots], 48 * (b // slots + 1))
                dve.tensor_copy(y[:, b % slots, SEQ:TOK], smp[:, b, :]).then_inc(s_in, 1)

            def low(b):
                dve.wait_ge(s_hi, b + 1)
                dve.tensor_tensor(net.HL[:, b, :], y[:, b % slots, :], net.HH[:, b, :].bitcast(F32), ALU.subtract).then_inc(s_lo, 1)

            samples(0)
            for b in range(DB):
                x = y[:, b % slots, :]
                dve.wait_ge(s_aff, b + 1)
                dve.tensor_tensor(x, x, bv[:, b % slots, :], ALU.add).then_inc(s_u, 1)
                if b:
                    low(b - 1)
                if b + 1 < DB:
                    samples(b + 1)
                dve.wait_ge(s_u, b * 2 + 1)
                dve.tensor_tensor(x, x, g[:, b % slots, :], ALU.mult).then_inc(s_u, 1)
            low(DB - 1)
            dve.wait_ge(s_x, 16)
            proj.dve(dve)




def stage_qkv(net):
    nc, io = net.nc, net.io
    with ExitStack() as ctx:
        def sb(name, shape, dt=F32):
            return ctx.enter_context(nc.sbuf_tensor(f"q_{name}", shape, dt))

        def sem(name):
            return net.semaphore(f"q_{name}")

        weights(net, ctx, "q")
        pan = Panels(net, ctx, "qp")
        cos, sin = sb("cos", [128, TOK]), sb("sin", [128, TOK])
        kv = sb("kv", [128, 2, TOK])
        tmp = sb("tmp", [128, 2, TT])
        ps = ctx.enter_context(nc.psum_tensor("q_ps", [128, NT, 512], F32))
        norm = Norm(net, ctx, "qn", net.gain[:, 2], mod_part(net, 1, 0), sq=kv, rs=cos, ps=ps)
        tb = [ctx.enter_context(nc.psum_tensor(f"q_tb{i}", [128, 4, 128], F32)) for i in range(2)]
        s_ang, s_x, s_t, s_tev, s_sw, s_rot, s_dv, s_kd = sem("ang"), sem("x"), sem("t"), sem("tev"), sem("sw"), sem("rot"), sem("dv"), sem("kd")
        s_vd, s_out = sem("vd"), sem("out")
        ident, swap = c_(net, "ident"), c_(net, "swap")
        w = io["at_wqkv"][0]
        NQ = HEADS * HD
        KVW = KV * HD
        v_at, k_at = NQ + KVW, NQ
        block = ctx.enter_context(nc.Block())

        @block.sync
        def _(sp):
            for p in range(2):
                pan.load(sp, p, p, panel_of(w, v_at + p * 128))
            sp.wait_ge(norm.s_lo, DB)
            sp.dma_start(cos[:], io["const_wide"][:, TOK:2 * TOK]).then_inc(s_ang, 16)
            sp.dma_start(sin[:], io["const_wide"][:, 2 * TOK:3 * TOK]).then_inc(s_ang, 16)
            for p in range(2):
                pan.load(sp, 2 + p, p, panel_of(w, k_at + p * 128))
            with sp.Fori(0, DB // 2) as j:
                for s in range(2):
                    pan.load(sp, j * 2 + s + 4, s, panel_of(w, j * 256 + s * 128))
            for name in ("k", "v"):
                sp.dma_start(io[f"out_{name}_sample"][0, :, 0:WIN - 1].rearrange("s w k d -> s (w k d)"), io[f"cache_{name}"][0, :, 1:WIN].rearrange("s w k d -> s (w k d)")).then_inc(s_out, 16)
            sp.wait_ge(s_out, 32)

        @block.gpsimd
        def _(pool):
            with pool.Fori(0, DB // 2 + 2) as j:
                for s in range(2):
                    pan.split(pool, j * 2 + s, s, j)

        @block.tensor
        def _(pe):
            def turn(v):
                pe.wait_ge(s_x, v * NT + NT)
                for n in range(3):
                    pe.wait_ge(s_tev, 3 * v + n + 1)
                    for q in range(4 if n < 2 else 1):
                        cols, t = (128, (4 * n + q) * 128) if n < 2 else (DEC, SEQ)
                        ins = pe.transpose(tb[(3 * v + n) % 2][0:cols, q, :], kv[:, v, t:t + cols], ident)
                    ins.then_inc(s_t, 1)

            def partners(p, x):
                pe.wait_ge(s_x, p * NT + NT)
                for n in range(NT):
                    pe.wait_ge(s_dv, ((p - 3) * NT + n) * 3 + 2 + 3 * NT)
                    ins = pe.matmul(ps[:, n, 0:TT], swap, x[:, n * TT:(n + 1) * TT], start=True, stop=True)
                    ins.then_inc(s_sw, 1)

            norm.pe(pe)
            pan.multiply(pe, 0, 0, net.HH, net.HL, ready=(norm.s_lo, 1))
            pan.multiply(pe, 1, 1, net.HH, net.HL)
            turn(0)
            pan.multiply(pe, 2, 0, net.HH, net.HL)
            turn(1)
            pan.multiply(pe, 3, 1, net.HH, net.HL)
            partners(2, kv[:, 0, :])

            def body(b, s, i):
                pan.multiply(pe, b + 4, s, net.HH, net.HL)
                if isinstance(b, int) and b == 0:
                    partners(3, kv[:, 1, :])
                else:
                    partners(b + 3, blk(net.Q, b - 1))
            around(pe, body)
            partners(DB + 3, net.Q[:, DB - 1, :])

        @block.scalar
        def _(act):
            def add_bias(p, x, at):
                for n in range(NT):
                    pan.summed(act, p, n)
                    act.activation(x[:, n * TT:(n + 1) * TT], pan.acc[:, n, 0:TT], ACT.Identity, bias=net.param[:, bass.ds(at, 1)]).then_inc(s_x, 1)
                act.wait_ge(s_x, p * NT + NT)
                act.sem_inc(pan.free, NT)

            norm.act(act)
            at = PARAM_AT["at_bqkv"]
            for v in range(2):
                add_bias(v, kv[:, v, :], at + v_at // 128 + v)
            for v in range(2):
                for n in range(3):
                    act.wait_ge(s_t, 3 * v + n + 1)
                    bank, cols = tb[(3 * v + n) % 2], slice(v * 128, (v + 1) * 128)
                    if n < 2:
                        act.activation(net.Vt[:, 4 * n:4 * n + 4, cols], bank[:], ACT.Copy).then_inc(s_tev, 1)
                    else:
                        act.activation(net.Vt[0:DEC, 2 * 4, cols], bank[0:DEC, 0, :], ACT.Copy).then_inc(s_tev, 1)
                act.wait_ge(s_vd, v * 4 + 4)
                add_bias(2 + v, kv[:, v, :], at + k_at // 128 + v)
            with act.Fori(0, DB) as b:
                add_bias(b + 4, blk(net.Q, b), b + at)

        @block.vector
        def _(dve):
            dve.sem_inc(pan.low, pan.LOW0)
            dve.sem_inc(pan.done, pan.DONE0)
            dve.sem_inc(pan.free, NT)
            dve.sem_inc(s_tev, 2)
            dve.sem_inc(s_dv, 3 * NT)
            norm.dve(dve)
            for v in range(2):
                dve.wait_ge(s_x, v * NT + NT)
                for h in range(2):
                    for a in range(2):
                        dve.tensor_copy(net.Vd[64 * a:64 * a + 64, 2 * v + h, :], kv[64 * h:64 * h + 64, v, SEQ:TOK]).then_inc(s_vd, 1)
            dve.wait_ge(s_ang, 32)

            def rotate(p, x):
                dve.wait_ge(s_x, p * NT + NT)
                for n in range(NT):
                    t = slice(n * TT, (n + 1) * TT)
                    base = ((p - 2) * NT + n) * 3 + 3 * NT
                    dve.wait_ge(s_sw, (p - 2) * NT + n + 1)
                    dve.wait_ge(s_dv, base)
                    dve.tensor_tensor(tmp[:, n % 2, :], ps[:, n, 0:TT], sin[:, t], ALU.mult).then_inc(s_dv, 1)
                    dve.tensor_tensor(x[:, t], x[:, t], cos[:, t], ALU.mult).then_inc(s_dv, 1)
                    dve.wait_ge(s_dv, base + 2)
                    dve.tensor_tensor(x[:, t], x[:, t], tmp[:, n % 2, :], ALU.add).then_inc(s_dv, 1)

            for k in range(2):
                rotate(2 + k, kv[:, k, :])
                dve.wait_ge(s_dv, (k + 1) * 3 * NT + 3 * NT)
                for h in range(2):
                    for a in range(2):
                        dve.tensor_copy(net.Kd[64 * a:64 * a + 64, 2 * k + h, :], kv[64 * h:64 * h + 64, k, :]).then_inc(s_kd, 1)
            with dve.Fori(0, DB) as b:
                rotate(b + 4, blk(net.Q, b))
            dve.wait_ge(s_dv, 11 * 3 * NT)
            dve.wait_ge(s_kd, 8)


def stage_attend_samples(net):
    nc, io = net.nc, net.io
    with ExitStack() as ctx:
        def sb(name, shape, dt=F32):
            return ctx.enter_context(nc.sbuf_tensor(f"as_{name}", shape, dt))

        def sem(name):
            return net.semaphore(f"as_{name}")

        ck, cv = (sb(n, [WIN, DEC, KV, 2, HD]) for n in ("ck", "cv"))
        KT = sb("KT", [128, 2, KV, WIN])
        qd, pd = sb("qd", [128, DEC, DB, 2]), sb("pd", [128, DEC, DB, 2])
        ST, PT = sb("ST", [WIN, 128]), sb("PT", [WIN, 128])
        R = sb("R", [128, WIN + 1])
        mx, nm, es, den = (sb(n, [128, 1]) for n in ("mx", "nm", "es", "den"))
        sink = sb("sink", [128, 1])
        diag, o, o2 = sb("diag", [128, 128]), sb("o", [128, DEC, DB, 2]), sb("o2", [128, DB, DEC])
        krow, ksrow = sb("krow", [WIN, KV, HD]), sb("ksrow", [DEC, KV, HD])
        tb = [ctx.enter_context(nc.psum_tensor(f"as_tb{i}", [128, 4, 128], F32)) for i in range(2)]
        pST, pR, pB, pO, pK, pKs = (ctx.enter_context(nc.psum_tensor(f"as_p{i}", [128, 512], F32)) for i in range(6))
        s_ck = [sem(f"ck{i}") for i in range(DEC // 2)]
        s_cv, s_sink, s_zero, s_out = sem("cv"), sem("sink"), sem("zero"), sem("out")
        s_t, s_tev, s_q, s_ST, s_STev, s_R, s_dv = sem("t"), sem("tev"), sem("q"), sem("ST"), sem("STev"), sem("R"), sem("dv")
        s_e, s_P, s_PT, s_PTev, s_O, s_k, s_kev = sem("e"), sem("P"), sem("PT"), sem("PTev"), sem("O"), sem("k"), sem("kev")
        s_hi = sem("hi")
        ident, ones = c_(net, "ident"), c_(net, "ones")
        LAST = SEQ // 128 - 1
        block = ctx.enter_context(nc.Block())

        @block.sync
        def _(sp):
            src = io["cache_k"][0].rearrange("s w k d -> w s k d")
            for s in range(DEC):
                for h in range(2):
                    sp.dma_start(ck[:, s, :, h, :], src[:, s]).then_inc(s_ck[s // 2], 16)
            sp.dma_start(io["out_v_sample"][0, :, WIN - 1].rearrange("s k d -> s (k d)"), net.Vt[0:DEC, LAST + 1, :]).then_inc(s_out, 16)
            sp.dma_start(io["out_v_prompt"][0, 0].rearrange("w k d -> w (k d)"), net.Vt[:, LAST, :]).then_inc(s_out, 16)
            sp.wait_ge(s_kev, 2)
            sp.dma_start(io["out_k_prompt"][0, 0], krow[:]).then_inc(s_out, 16)
            sp.dma_start(io["out_k_sample"][0, :, WIN - 1], ksrow[:]).then_inc(s_out, 16)
            sp.wait_ge(s_out, 64)

        @block.gpsimd
        def _(pool):
            for s in range(DEC):
                pool.dma_start(sink[s * HEADS:(s + 1) * HEADS, :], io["at_sink"].rearrange("a h -> h a")).then_inc(s_sink, 16)
            src = io["cache_v"][0].rearrange("s w k d -> w s k d")
            for h in range(2):
                for s in range(DEC):
                    pool.dma_start(cv[:, s, :, h, :], src[:, s]).then_inc(s_cv, 16)

        @block.tensor
        def _(pe):
            for k in range(KV):
                ins = pe.transpose(pK[:, k * HD:(k + 1) * HD], net.Kd[0:64, k, LAST * 128:SEQ], ident[0:64, 0:64])
            ins.then_inc(s_k, 1)
            for k in range(KV):
                ins = pe.transpose(pKs[0:DEC, k * HD:(k + 1) * HD], net.Kd[0:64, k, SEQ:TOK], ident[0:64, 0:64])
            ins.then_inc(s_k, 1)
            pe.wait_ge(s_q, 4)

            def turn(s):
                pe.wait_ge(s_ck[s // 2], 64)
                if s >= 2:
                    pe.wait_ge(s_tev, s - 1)
                for k in range(KV):
                    ins = pe.transpose(tb[s % 2][:, k, :], ck[:, s, k].rearrange("w a d -> w (a d)"), ident)
                ins.then_inc(s_t, 1)

            turn(0)
            for s in range(DEC):
                if s + 1 < DEC:
                    turn(s + 1)
                pe.wait_ge(s_tev, s + 1)
                for k in range(KV):
                    at = s * HEADS + 4 * k
                    ins = pe.matmul(pST[:, at:at + 4], KT[:, s % 2, k, :], qd[:, s, 2 * k:2 * k + 2, :].rearrange("p b a -> p (b a)"), start=True, stop=True, skip_group_check=True)
                ins.then_inc(s_ST, 1)
            pe.wait_ge(s_STev, 1)
            pe.matmul(pR[:, WIN:WIN + 1], pd[:].rearrange("p s b a -> p (s b a)"), ones[:, 0:1], start=True, stop=True)
            pe.transpose(pR[:, 0:WIN], ST[:], ident).then_inc(s_R, 1)
            pe.wait_ge(s_P, 2)
            pe.matmul(pB[:, 0:128], ones, diag[:], start=True, stop=True)
            pe.transpose(pST[:, 128:256], R[:, 0:WIN], ident).then_inc(s_PT, 1)
            pe.wait_ge(s_PTev, 1)
            pe.wait_ge(s_cv, 2 * DEC * 16)
            for s in range(DEC):
                for k in range(KV):
                    at = s * HEADS + 4 * k
                    ins = pe.matmul(pO[:, at:at + 4], cv[:, s, k].rearrange("w a d -> w (a d)"), PT[:, at:at + 4], start=True, stop=True, skip_group_check=True)
            ins.then_inc(s_O, 1)

        @block.scalar
        def _(act):
            act.wait_ge(s_k, 1)
            act.activation(krow[:].rearrange("w k d -> w (k d)"), pK[:, 0:KV * HD], ACT.Copy).then_inc(s_kev, 1)
            act.wait_ge(s_k, 2)
            act.activation(ksrow[:].rearrange("w k d -> w (k d)"), pKs[0:DEC, 0:KV * HD], ACT.Copy).then_inc(s_kev, 1)
            for s in range(DEC):
                act.wait_ge(s_t, s + 1)
                if s >= 2:
                    act.wait_ge(s_ST, s - 1)
                act.activation(KT[:, s % 2], tb[s % 2][:], ACT.Copy).then_inc(s_tev, 1)
            act.wait_ge(s_ST, DEC)
            act.activation(ST[:], pST[:, 0:128], ACT.Copy).then_inc(s_STev, 1)
            act.wait_ge(s_dv, 5)
            act.activation(R[:], R[:], ACT.Exp, bias=nm[:], accum_out=den[:]).then_inc(s_e, 1)
            act.activation(es[:], sink[:], ACT.Exp, bias=nm[:]).then_inc(s_e, 1)
            act.wait_ge(s_PT, 1)
            act.activation(PT[:], pST[:, 128:256], ACT.Copy).then_inc(s_PTev, 1)
            act.wait_ge(s_dv, 11)
            act.activation(net.HH[:, :, SEQ:TOK], o2[:], ACT.Copy).then_inc(s_hi, 1)

        @block.vector
        def _(dve):
            ch = Chain(dve, s_dv)
            dve.memset(qd[:], 0.0).then_inc(s_zero, 1)
            dve.memset(pd[:], 0.0).then_inc(s_zero, 1)
            dve.wait_ge(s_zero, 2)
            for a in range(2):
                r = slice(64 * a, 64 * a + 64)
                q = net.Q[r, :, SEQ:TOK].rearrange("p b s -> p s b")
                dve.tensor_copy(qd[r, :, :, a], q).then_inc(s_q, 1)
                dve.tensor_tensor(pd[r].rearrange("p s (k j) a -> p s k j a", j=2)[:, :, :, :, a], q.rearrange("p s (k j) -> p s k j", j=2),
                                  net.Kd[r, :, SEQ:TOK].rearrange("p k s -> p s k").unsqueeze(3).to_broadcast([64, DEC, KV, 2]), ALU.mult).then_inc(s_q, 1)
            dve.wait_ge(s_R, 1)
            ch.link(dve.tensor_scalar(R[:], pR[:, 0:WIN + 1], SCALE, None, ALU.mult))
            ch.link(dve.tensor_reduce(mx[:], R[:], AX, ALU.max))
            dve.wait_ge(s_sink, DEC * 16)
            ch.link(dve.tensor_tensor(mx[:], mx[:], sink[:], ALU.max))
            ch.link(dve.tensor_scalar(nm[:], mx[:], -1.0, None, ALU.mult))
            dve.sem_inc(s_dv, 1)
            ch.n += 1
            dve.wait_ge(s_e, 2)
            ch.link(dve.tensor_tensor(den[:], den[:], es[:], ALU.add))
            ch.link(dve.reciprocal(den[:], den[:]))
            dve.tensor_scalar(R[:], R[:], den[:], None, ALU.mult).then_inc(s_P, 1)
            dve.wait_ge(s_P, 1)
            dve.tensor_scalar(diag[:], ident, R[:, WIN:WIN + 1], None, ALU.mult).then_inc(s_P, 1)
            dve.wait_ge(s_O, 1)
            new = net.Vd[:].rearrange("p k s -> p s k").unsqueeze(3).to_broadcast([128, DEC, KV, 4])
            ch.link(dve.tensor_tensor(o[:].rearrange("p s (k j) a -> p s k (j a)", j=2), pB[:, 0:128].rearrange("p (s k g) -> p s k g", k=KV, g=4), new, ALU.mult))
            flat = o[:].rearrange("p s b a -> p (s b a)")
            ch.link(dve.tensor_tensor(flat, flat, pO[:, 0:128], ALU.add))
            for a in range(2):
                r = slice(64 * a, 64 * a + 64)
                ch.link(dve.tensor_copy(o2[r], o[r, :, :, a].rearrange("p s b -> p b s")))
            assert ch.n == 11
            dve.wait_ge(s_hi, 1)
            dve.tensor_tensor(net.HL[:, :, SEQ:TOK], o2[:], net.HH[:, :, SEQ:TOK].bitcast(F32), ALU.subtract).then_inc(s_q, 1)
            dve.wait_ge(s_q, 5)


def stage_attend(net):
    nc, io = net.nc, net.io
    TILES = SEQ // 128
    with ExitStack() as ctx:
        def sb(name, shape, dt=F32):
            return ctx.enter_context(nc.sbuf_tensor(f"at_{name}", shape, dt))

        def sem(name):
            return net.semaphore(f"at_{name}")

        mask, sink = sb("mask", [128, 256]), sb("sink", [128, HEADS])
        S = sb("S", [128, 2, 4, 256])
        PT = sb("PT", [128, 4, 2, 128])
        Qs, Vs = sb("Qs", [128, 2, 4, 128]), sb("Vs", [128, 2, 2, HD])
        mx, nm, es, den = (sb(n, [128, 2, 4]) for n in ("mx", "nm", "es", "den"))
        pS = [ctx.enter_context(nc.psum_tensor(f"at_pS{i}", [128, 4, 256], F32)) for i in range(2)]
        pT = ctx.enter_context(nc.psum_tensor("at_pT", [128, 4, 2, 128], F32))
        pO = [ctx.enter_context(nc.psum_tensor(f"at_pO{i}", [128, 2, 128], F32, )) for i in range(2)]
        s_qs, s_vs, s_zero = sem("qs"), sem("vs"), sem("zero")
        s_in, s_s, s_sev, s_nm, s_e, s_P = sem("in"), sem("s"), sem("sev"), sem("nm"), sem("e"), sem("P")
        s_t, s_tev, s_o, s_hi, s_lo, s_dv, s_dv2 = sem("t"), sem("tev"), sem("o"), sem("hi"), sem("lo"), sem("dv"), sem("dv2")
        ident = c_(net, "ident")
        block = ctx.enter_context(nc.Block())

        def steps(eng, work):
            def tile(t, k):
                def at(d):
                    t2, k2 = t + (k + d) // KV, (k + d) % KV
                    return None if isinstance(t, int) and not 0 <= t2 < TILES else (t2, k2)
                work(t, k, at)
            for t in (0, 1):
                for k in range(KV):
                    tile(t, k)
            with eng.Fori(2, TILES - 1) as t:
                for k in range(KV):
                    tile(t, k)
            for k in range(KV):
                tile(TILES - 1, k)

        def keys(t):
            return (1, 0) if isinstance(t, int) and t == 0 else (2, t - 1)

        @block.sync
        def _(sp):
            sp.dma_start(mask[:], io["const_mask"]).then_inc(s_in, 16)
            sp.dma_start(sink[:], io["at_sink"].to_broadcast([128, HEADS])).then_inc(s_in, 16)

        @block.gpsimd
        def _(pool):
            def queries(t, k):
                if not (isinstance(t, int) and t == 0 and k < 2):
                    pool.wait_ge(s_s, t * KV + k - 1)
                for a in range(2):
                    r = slice(64 * a, 64 * a + 64)
                    pool.tensor_copy(Qs[r, k % 2, a::2], net.Q[r, 2 * k:2 * k + 2, bass.ds(t * 128, 128)]).then_inc(s_qs, 1)
                    pool.wait_ge(s_qs, (t * KV + k) * 2 + a + 1)

            pool.memset(Qs[:], 0.0).then_inc(s_zero, 1)
            pool.wait_ge(s_zero, 1)
            queries(0, 0)
            queries(0, 1)

            def work(t, k, at):
                if at(2):
                    queries(*at(2))
                n, first = keys(t)
                if not (isinstance(t, int) and t == 0 and k < 2):
                    pool.wait_ge(s_o, t * KV + k)
                pool.tensor_copy(Vs[:, k % 2, 0:n], net.Vt[:, bass.ds(first, n), k * HD:(k + 1) * HD]).then_inc(s_vs, 1)
            steps(pool, work)

        @block.tensor
        def _(pe):
            def scores(t, k):
                n, first = keys(t)
                s = k % 2
                pe.wait_ge(s_sev, t * KV + k + 1)
                pe.wait_ge(s_qs, (t * KV + k) * 2 + 2)
                for g in range(4):
                    ins = pe.matmul(pS[s][:, g, 0:n * 128], Qs[:, s, g, :], net.Kd[:, k, bass.ds(first * 128, n * 128)], start=True, stop=True, skip_group_check=True)
                ins.then_inc(s_s, 1)

            def turn(t, k):
                n, first = keys(t)
                pe.wait_ge(s_P, t * KV + k + 1)
                pe.wait_ge(s_tev, t * KV + k + 1)
                for g in range(4):
                    for j in range(n):
                        ins = pe.transpose(pT[:, g, j, :], S[:, k % 2, g, j * 128:(j + 1) * 128], ident)
                ins.then_inc(s_t, 1)

            def values(t, k):
                n, first = keys(t)
                pe.wait_ge(s_tev, t * KV + k + 2)
                pe.wait_ge(s_vs, t * KV + k + 1)
                pe.wait_ge(s_lo, t * KV + k + 1)
                for g in range(4):
                    a = g % 2
                    for j in range(n):
                        ins = pe.matmul(pO[k % 2][64 * a:64 * a + 64, g // 2, :], Vs[:, k % 2, j, :], PT[:, g, j, :], start=(j == 0), stop=(j == n - 1), skip_group_check=True, tile_position=(0, 64 * a))
                ins.then_inc(s_o, 1)

            scores(0, 0)
            scores(0, 1)

            def work(t, k, at):
                if at(2):
                    scores(*at(2))
                if at(-1):
                    values(*at(-1))
                turn(t, k)
            steps(pe, work)
            values(TILES - 1, KV - 1)

        @block.scalar
        def _(act):
            def exps(t, k):
                n, first = keys(t)
                s = k % 2
                act.wait_ge(s_nm, (t * KV + k) * 2 + 2)
                for g in range(4):
                    x = S[:, s, g, 0:n * 128]
                    ins = act.activation(x, x, ACT.Exp, bias=nm[:, s, g:g + 1], accum_out=den[:, s, g:g + 1])
                ins.then_inc(s_e, 1)
                act.activation(es[:, s], es[:, s], ACT.Exp).then_inc(s_e, 1)

            def turned(t, k):
                n, first = keys(t)
                act.wait_ge(s_t, t * KV + k + 1)
                act.wait_ge(s_o, t * KV + k + 1)
                act.activation(PT[:, :, 0:n, :], pT[:, :, 0:n, :], ACT.Copy).then_inc(s_tev, 1)

            def high(t, k):
                act.wait_ge(s_o, t * KV + k + 2)
                act.activation(net.HH[:, 2 * k:2 * k + 2, bass.ds(t * 128, 128)], pO[k % 2][:], ACT.Copy).then_inc(s_hi, 1)

            exps(0, 0)

            def work(t, k, at):
                if at(1):
                    exps(*at(1))
                turned(t, k)
                if at(-1):
                    high(*at(-1))
            steps(act, work)
            high(TILES - 1, KV - 1)

        @block.vector
        def _(dve):
            dve.sem_inc(s_sev, 2)
            dve.sem_inc(s_tev, 1)
            dve.sem_inc(s_lo, 2)
            dve.sem_inc(s_o, 1)
            dve.wait_ge(s_in, 32)

            def masked(t, k):
                n, first = keys(t)
                s = k % 2
                u = t * KV + k
                m = mask[:, 256 - n * 128:256].unsqueeze(1).to_broadcast([128, 4, n * 128])
                dve.wait_ge(s_s, u + 1)
                if not (isinstance(t, int) and t == 0 and k < 2):
                    dve.wait_ge(s_t, u - 1)
                dve.scalar_tensor_tensor(out=S[:, s, :, 0:n * 128], in0=pS[s][:, :, 0:n * 128], scalar=SCALE, in1=m, op0=ALU.mult, op1=ALU.add).then_inc(s_sev, 1)
                dve.wait_ge(s_sev, u + 3)
                dve.tensor_reduce(mx[:, s], S[:, s, :, 0:n * 128], AX, ALU.max).then_inc(s_dv, 1)
                dve.wait_ge(s_dv, u * 2 + 1)
                dve.tensor_tensor(mx[:, s], mx[:, s], sink[:, 4 * k:4 * k + 4], ALU.max).then_inc(s_dv, 1)
                dve.wait_ge(s_dv, u * 2 + 2)
                dve.tensor_scalar(nm[:, s], mx[:, s], -1.0, None, ALU.mult).then_inc(s_nm, 1)
                dve.tensor_tensor(es[:, s], sink[:, 4 * k:4 * k + 4], mx[:, s], ALU.subtract).then_inc(s_nm, 1)

            def normal(t, k):
                n, first = keys(t)
                s = k % 2
                u = t * KV + k
                dve.wait_ge(s_e, u * 2 + 2)
                dve.tensor_tensor(den[:, s], den[:, s], es[:, s], ALU.add).then_inc(s_dv2, 1)
                dve.wait_ge(s_dv2, u * 2 + 1)
                dve.reciprocal(den[:, s], den[:, s]).then_inc(s_dv2, 1)
                dve.wait_ge(s_dv2, u * 2 + 2)
                x = S[:, s, :, 0:n * 128]
                dve.tensor_tensor(x, x, den[:, s].unsqueeze(2).to_broadcast([128, 4, n * 128]), ALU.mult).then_inc(s_P, 1)

            def low(t, k):
                dve.wait_ge(s_hi, t * KV + k + 1)
                o = lambda x: x[:, 2 * k:2 * k + 2, bass.ds(t * 128, 128)]
                dve.tensor_tensor(o(net.HL), pO[k % 2][:], o(net.HH).bitcast(F32), ALU.subtract).then_inc(s_lo, 1)

            masked(0, 0)

            def work(t, k, at):
                if at(1):
                    masked(*at(1))
                normal(t, k)
                if at(-2):
                    low(*at(-2))
            steps(dve, work)
            low(TILES - 1, KV - 2)
            low(TILES - 1, KV - 1)
            dve.wait_ge(s_lo, TILES * KV + 2)


def stage_attend_out(net):
    nc, io = net.nc, net.io
    with ExitStack() as ctx:
        weights(net, ctx, "ao")
        proj = Project(net, ctx, "aop", io["at_wo"][0], mod_part(net, 1, 2))
        block = ctx.enter_context(nc.Block())
        block.sync(proj.sp)
        block.gpsimd(proj.pool)
        block.tensor(proj.pe)

        @block.vector
        def _(dve):
            proj.dve_start(dve)
            proj.dve(dve)


def stage_final(net):
    nc, io = net.nc, net.io
    TILES = [(t * 128, 128) for t in range(SEQ // 128)] + [(SEQ, DEC)]
    with ExitStack() as ctx:
        def sb(name, shape):
            return ctx.enter_context(nc.sbuf_tensor(f"f_{name}", shape, F32))

        def sem(name):
            return net.semaphore(f"f_{name}")

        g, rows, sq = sb("g", [128, D]), sb("rows", [128, 2, D]), sb("sq", [128, 512])
        ss, r = sb("ss", [128, 2, 2]), sb("r", [128, 2])
        tb = [[ctx.enter_context(nc.psum_tensor(f"f_tb{s}{h}", [128, 4, 128], F32)) for h in range(2)] for s in range(2)]
        s_g, s_t, s_sq, s_m, s_root, s_inv, s_y = sem("g"), sem("t"), sem("sq"), sem("m"), sem("root"), sem("inv"), sem("y")
        s_out = [sem("out0"), sem("out1")]
        ident = c_(net, "ident")
        flat = lambda bank: bank[:].rearrange("p q c -> p (q c)")
        block = ctx.enter_context(nc.Block())

        @block.sync
        def _(sp):
            sp.dma_start(g[:], io["final_g"].rearrange("(a d) -> a d", a=1).to_broadcast([128, D])).then_inc(s_g, 16)
            for t, (at, n) in enumerate(TILES):
                s = t % 2
                sp.wait_ge(s_y, 2 * t + 2)
                to = io["out_y_prompt"][0, at:at + n] if n == 128 else io["out_y_sample"].rearrange("b o d -> (b o) d")
                sp.dma_start(to, rows[0:n, s, :]).then_inc(s_out[s], 16)
            for s in range(2):
                sp.wait_ge(s_out[s], 16 * ((len(TILES) + 1 - s) // 2))

        @block.tensor
        def _(pe):
            for t, (at, n) in enumerate(TILES):
                if t >= 2:
                    pe.wait_ge(s_y, 2 * t - 2)
                for h in range(2):
                    for q in range(4):
                        ins = pe.transpose(tb[t % 2][h][0:n, q, :], net.X[:, 4 * h + q, at:at + n], ident)
                    ins.then_inc(s_t, 1)

        @block.scalar
        def _(act):
            for t, (at, n) in enumerate(TILES):
                s = t % 2
                if t >= 2:
                    act.wait_ge(s_m, 2 * t - 2)
                for h in range(2):
                    act.wait_ge(s_t, 2 * t + h + 1)
                    if t or h:
                        act.wait_ge(s_sq, 2 * t + h)
                    act.activation(sq[0:n], flat(tb[s][h])[0:n], ACT.Square, accum_out=ss[0:n, s, h:h + 1]).then_inc(s_sq, 1)
                act.wait_ge(s_m, 2 * t + 2)
                act.activation(r[0:n, s:s + 1], r[0:n, s:s + 1], ACT.Sqrt).then_inc(s_root, 1)

        @block.vector
        def _(dve):
            def mean(t):
                s, n = t % 2, TILES[t][1]
                m = r[0:n, s:s + 1]
                dve.wait_ge(s_sq, 2 * t + 2)
                dve.tensor_scalar(m, ss[0:n, s, 0:1], 1.0 / D, EPS, ALU.mult, ALU.add).then_inc(s_m, 1)
                dve.wait_ge(s_m, 2 * t + 1)
                dve.scalar_tensor_tensor(out=m, in0=ss[0:n, s, 1:2], scalar=1.0 / D, in1=m, op0=ALU.mult, op1=ALU.add).then_inc(s_m, 1)

            mean(0)
            dve.wait_ge(s_g, 16)
            for t, (at, n) in enumerate(TILES):
                s = t % 2
                m = r[0:n, s:s + 1]
                if t + 1 < len(TILES):
                    mean(t + 1)
                dve.wait_ge(s_root, t + 1)
                dve.reciprocal(m, m).then_inc(s_inv, 1)
                dve.wait_ge(s_inv, t + 1)
                if t >= 2:
                    dve.wait_ge(s_out[s], 16 * (t // 2))
                for h in range(2):
                    c = slice(512 * h, 512 * h + 512)
                    dve.scalar_tensor_tensor(out=rows[0:n, s, c], in0=flat(tb[s][h])[0:n], scalar=m, in1=g[0:n, c], op0=ALU.mult, op1=ALU.mult).then_inc(s_y, 1)


_OUTS = [("y_prompt", (1, SEQ, D)), ("y_sample", (DEC, 1, D)), ("wkv_prompt", (1, 1, HEADS, HD, HD)), ("wkv_sample", (1, DEC, HEADS, HD, HD)),
         ("shift_prompt", (1, 1, D)), ("shift_sample", (1, DEC, D)), ("k_prompt", (1, 1, WIN, KV, HD)), ("k_sample", (1, DEC, WIN, KV, HD)),
         ("v_prompt", (1, 1, WIN, KV, HD)), ("v_sample", (1, DEC, WIN, KV, HD))]


def layout(nc, inputs):
    arrays, io = {}, {}
    for name, a in {**inputs, **shape_constants()}.items():
        a = np.ascontiguousarray(a)
        arrays[f"in_{name}"] = a
        io[name] = nc.dram_tensor(f"in_{name}", a.shape, F32, kind="ExternalInput").ap()
    for name, shape in _OUTS:
        io["out_" + name] = nc.dram_tensor(f"out_{name}", shape, F32, kind="ExternalOutput").ap()
    return arrays, io


def kernel(**inputs):
    import concourse.bacc as bacc
    from concourse.bass_utils import run_bass_kernel_spmd

    nc = bacc.Bacc("TRN2", target_bir_lowering=False, num_devices=1)
    arrays, io = layout(nc, inputs)
    build(nc, io)
    r = run_bass_kernel_spmd(nc, [arrays], core_ids=[0])
    return tuple(r.results[0][f"out_{name}"] for name, _ in _OUTS)
```
